# Optimizing a Trainium2 kernel written in Bass

```python
import numpy as np
import jax
import jax.numpy as jnp
from jax import lax
import math
import jax, jax.numpy as jnp

D_MODEL = 1024
BATCH = 1
SEQ = 512
DEPTH = 1

POOL_WINDOWS = (2, 4, 8, 16)
POOL_GROUPS = len(POOL_WINDOWS)
POOL_GROUP_W = 128
POOL_W = POOL_GROUPS * POOL_GROUP_W
N_HEADS = 8
HEAD_DIM = 64
N_KV_GROUPS = 2
HEADS_PER_GROUP = N_HEADS // N_KV_GROUPS
ATTN_W = N_HEADS * HEAD_DIM
KV_W = N_KV_GROUPS * HEAD_DIM
N_KV_SLOTS = 6
N_NSA_BRANCHES = 3
CMP_BLOCK = 32
CMP_STRIDE = 16
CMP_HIDDEN = 128
SEL_BLOCK = 64
N_SELECT = 16
WINDOW = 512
QUERY_CHUNK = 16
ROPE_THETA = 500000.0
ROT_DIM = HEAD_DIM // 4
N_MERGE = 2
D_FF = 2816
CONV_WIDTH = 3
IN_W = POOL_W + ATTN_W + N_KV_SLOTS * KV_W + N_HEADS * N_NSA_BRANCHES + N_MERGE * D_MODEL
RMS_EPS = 1e-6
NEG_INF = -1e30
SEL_FORCE = 1e9


def rms_norm(x, g):
    xf = x.astype(jnp.float32)
    y = xf * lax.rsqrt(jnp.mean(xf * xf, axis=-1, keepdims=True) + RMS_EPS)
    return (y * g.astype(jnp.float32)).astype(x.dtype)

def partial_rope(x, pos):
    half = ROT_DIM // 2
    inv = ROPE_THETA ** (-(jnp.arange(half, dtype=jnp.float32) * 2.0 / ROT_DIM))
    ang = pos.astype(jnp.float32)[:, :, None, None] * inv
    cos, sin = jnp.cos(ang), jnp.sin(ang)
    xf = x.astype(jnp.float32)
    x1, x2 = xf[..., :half], xf[..., half:ROT_DIM]
    rot = jnp.concatenate([x1 * cos - x2 * sin, x2 * cos + x1 * sin], axis=-1).astype(x.dtype)
    return jnp.concatenate([rot, x[..., ROT_DIM:]], axis=-1)

def masked_softmax(s, mask, axis):
    s = jnp.where(mask, s.astype(jnp.float32), NEG_INF)
    p = jax.nn.softmax(s, axis=axis)
    return jnp.where(mask, p, 0.0)

def pooling_mixer(u, pool_w, pool_scale):
    S = u.shape[1]
    uf = u.astype(jnp.float32)
    cs = jnp.cumsum(uf, axis=1)
    count = jnp.arange(S, dtype=jnp.float32) + 1.0
    outs = []
    for gi, w in enumerate(POOL_WINDOWS):
        sl = slice(gi * POOL_GROUP_W, (gi + 1) * POOL_GROUP_W)
        c = cs[..., sl]
        lag = jnp.pad(c[:, :S - w], ((0, 0), (w, 0), (0, 0)))
        mean = (c - lag) / jnp.minimum(count, float(w))[None, :, None]
        pooled = (mean - uf[..., sl]).astype(u.dtype)
        outs.append(pooled @ pool_w[gi])
    return jnp.concatenate(outs, axis=-1) * pool_scale

def compress_blocks(kv, pe, w1, w2, idx):
    blk = kv[:, idx] + pe[None, None, :, None, :]
    hid = jax.nn.silu(jnp.einsum('bnlgd,ldh->bngh', blk, w1))
    return jnp.einsum('bngh,hd->bngd', hid, w2)

def nsa_mixer(q, k_cmp, v_cmp, k_sel, v_sel, k_win, v_win, gates, positions,
              q_norm_g, k_norm_g, cmp_pe, cmp_w1, cmp_w2):
    B, S = q.shape[0], q.shape[1]
    G, R, dh = N_KV_GROUPS, HEADS_PER_GROUP, HEAD_DIM
    scale = HEAD_DIM ** -0.5
    q = partial_rope(rms_norm(q, q_norm_g), positions)

    n_cmp = (S - CMP_BLOCK) // CMP_STRIDE + 1
    cmp_idx = np.arange(n_cmp)[:, None] * CMP_STRIDE + np.arange(CMP_BLOCK)[None, :]
    cmp_end = jnp.asarray(cmp_idx[:, -1], dtype=jnp.int32)
    kc = compress_blocks(k_cmp, cmp_pe[0], cmp_w1[0], cmp_w2[0], cmp_idx)
    vc = compress_blocks(v_cmp, cmp_pe[1], cmp_w1[1], cmp_w2[1], cmp_idx)
    kc = partial_rope(rms_norm(kc, k_norm_g[0]), positions[:, cmp_idx[:, -1]])

    n_sel = S // SEL_BLOCK
    k_top = min(N_SELECT, n_sel)
    ks = partial_rope(rms_norm(k_sel, k_norm_g[1]), positions)
    ks_blocks = ks.reshape(B, n_sel, SEL_BLOCK, G, dh).transpose(0, 3, 1, 2, 4)
    vs_blocks = v_sel.reshape(B, n_sel, SEL_BLOCK, G, dh).transpose(0, 3, 1, 2, 4)
    sel_start = np.arange(n_sel)[:, None] * SEL_BLOCK
    cmp_start = np.arange(n_cmp)[None, :] * CMP_STRIDE
    ov = np.clip(np.minimum(sel_start + SEL_BLOCK, cmp_start + CMP_BLOCK)
                 - np.maximum(sel_start, cmp_start), 0, None) / CMP_BLOCK
    overlap = jnp.asarray(ov, dtype=jnp.float32)
    gather_blocks = jax.vmap(jax.vmap(lambda blocks, i: blocks[i]))

    kw = partial_rope(rms_norm(k_win, k_norm_g[2]), positions)
    kw_pad = jnp.pad(kw, ((0, 0), (WINDOW, 0), (0, 0), (0, 0)))
    vw_pad = jnp.pad(v_win, ((0, 0), (WINDOW, 0), (0, 0), (0, 0)))

    n_chunks = S // QUERY_CHUNK
    q_ch = q.reshape(B, n_chunks, QUERY_CHUNK, G, R, dh).swapaxes(0, 1)
    g_ch = gates.reshape(B, n_chunks, QUERY_CHUNK, G, R, N_NSA_BRANCHES).swapaxes(0, 1)
    j_blk = jnp.arange(n_sel)
    tok_off = jnp.arange(SEL_BLOCK)
    win_off = jnp.arange(WINDOW + QUERY_CHUNK)

    def chunk(args):
        c, qc, gc = args
        t = c * QUERY_CHUNK + jnp.arange(QUERY_CHUNK)
        s = jnp.einsum('bqgrd,bngd->bgrqn', qc, kc) * scale
        p_cmp = masked_softmax(s, cmp_end[None, :] <= t[:, None], -1)
        o_cmp = jnp.einsum('bgrqn,bngd->bqgrd', p_cmp.astype(vc.dtype), vc)
        imp = jnp.einsum('bgrqn,jn->bgqj', p_cmp, overlap)
        cur = t // SEL_BLOCK
        forced = (j_blk[None, :] == 0) | (j_blk[None, :] == cur[:, None]) | (j_blk[None, :] == cur[:, None] - 1)
        future = j_blk[None, :] * SEL_BLOCK > t[:, None]
        imp = jnp.where(forced, SEL_FORCE, jnp.where(future, NEG_INF, imp))
        _, top = lax.top_k(imp, k_top)
        ksel = gather_blocks(ks_blocks, top)
        vsel = gather_blocks(vs_blocks, top)
        tok = top[..., None] * SEL_BLOCK + tok_off
        m_sel = (tok <= t[None, None, :, None, None])[:, :, None]
        s = jnp.einsum('bqgrd,bgqkld->bgrqkl', qc, ksel) * scale
        p = masked_softmax(s, m_sel, (-2, -1))
        o_sel = jnp.einsum('bgrqkl,bgqkld->bqgrd', p.astype(vsel.dtype), vsel)
        kwc = lax.dynamic_slice_in_dim(kw_pad, c * QUERY_CHUNK, WINDOW + QUERY_CHUNK, axis=1)
        vwc = lax.dynamic_slice_in_dim(vw_pad, c * QUERY_CHUNK, WINDOW + QUERY_CHUNK, axis=1)
        kpos = c * QUERY_CHUNK - WINDOW + win_off
        m_win = (kpos[None, :] >= 0) & (kpos[None, :] <= t[:, None]) & (t[:, None] - kpos[None, :] < WINDOW)
        s = jnp.einsum('bqgrd,bkgd->bgrqk', qc, kwc) * scale
        p = masked_softmax(s, m_win, -1)
        o_win = jnp.einsum('bgrqk,bkgd->bqgrd', p.astype(vwc.dtype), vwc)
        return gc[..., 0:1] * o_cmp + gc[..., 1:2] * o_sel + gc[..., 2:3] * o_win

    out = lax.map(chunk, (jnp.arange(n_chunks), q_ch, g_ch))
    return out.swapaxes(0, 1).reshape(B, S, ATTN_W)

def causal_dwconv(x, w, b):
    C = x.shape[-1]
    y = lax.conv_general_dilated(x, w[:, None, :].astype(x.dtype), window_strides=(1,),
                                 padding=[(CONV_WIDTH - 1, 0)],
                                 dimension_numbers=('NWC', 'WIO', 'NWC'),
                                 feature_group_count=C)
    return y + b

def first_inputs(seed: int = 0) -> dict:
    key = jax.random.key(seed)
    ks = jax.random.split(key, 20)
    f32 = jnp.float32

    def nrm(k, shape, s):
        return jax.random.normal(k, shape, f32) * s

    x = jax.random.normal(ks[0], (BATCH, SEQ, D_MODEL), f32)
    offsets = jax.random.randint(ks[1], (BATCH, 1), 0, 4096, dtype=jnp.int32)
    positions = (jnp.arange(SEQ, dtype=jnp.int32)[None, :] + offsets).astype(jnp.int32)
    return {
        "x": x,
        "positions": positions,
        "mix_norm_g": 1.0 + nrm(ks[2], (DEPTH, D_MODEL), 0.05),
        "w_in": nrm(ks[3], (DEPTH, D_MODEL, IN_W), D_MODEL ** -0.5),
        "q_norm_g": 1.0 + nrm(ks[4], (DEPTH, HEAD_DIM), 0.05),
        "k_norm_g": 1.0 + nrm(ks[5], (DEPTH, 3, HEAD_DIM), 0.05),
        "cmp_pe": nrm(ks[6], (DEPTH, 2, CMP_BLOCK, HEAD_DIM), 0.1),
        "cmp_w1": nrm(ks[7], (DEPTH, 2, CMP_BLOCK, HEAD_DIM, CMP_HIDDEN), (CMP_BLOCK * HEAD_DIM) ** -0.5),
        "cmp_w2": nrm(ks[8], (DEPTH, 2, CMP_HIDDEN, HEAD_DIM), CMP_HIDDEN ** -0.5),
        "pool_w": nrm(ks[9], (DEPTH, POOL_GROUPS, POOL_GROUP_W, POOL_GROUP_W), POOL_GROUP_W ** -0.5),
        "pool_scale": 1.0 + nrm(ks[10], (DEPTH, POOL_W), 0.1),
        "w_pool_out": nrm(ks[11], (DEPTH, POOL_W, D_MODEL), POOL_W ** -0.5),
        "w_nsa_out": nrm(ks[12], (DEPTH, ATTN_W, D_MODEL), ATTN_W ** -0.5),
        "w_out": nrm(ks[13], (DEPTH, D_MODEL, D_MODEL), D_MODEL ** -0.5),
        "ffn_norm_g": 1.0 + nrm(ks[14], (DEPTH, D_MODEL), 0.05),
        "w_up": nrm(ks[15], (DEPTH, D_MODEL, 2 * D_FF), D_MODEL ** -0.5),
        "conv_w": nrm(ks[16], (DEPTH, CONV_WIDTH, D_FF), CONV_WIDTH ** -0.5),
        "conv_b": nrm(ks[17], (DEPTH, D_FF), 0.01),
        "w_down": nrm(ks[18], (DEPTH, D_FF, D_MODEL), D_FF ** -0.5),
    }

def first_block(x, positions, mix_norm_g, w_in, q_norm_g, k_norm_g, cmp_pe, cmp_w1, cmp_w2,
              pool_w, pool_scale, w_pool_out, w_nsa_out, w_out, ffn_norm_g, w_up, conv_w,
              conv_b, w_down):
    B, S = x.shape[0], x.shape[1]
    split_at = [POOL_W, POOL_W + ATTN_W, POOL_W + ATTN_W + N_KV_SLOTS * KV_W,
                POOL_W + ATTN_W + N_KV_SLOTS * KV_W + N_HEADS * N_NSA_BRANCHES]
    for l in range(DEPTH):
        h = rms_norm(x, mix_norm_g[l])
        proj = h @ w_in[l]
        u, q, kv, nsa_g, merge_g = jnp.split(proj, split_at, axis=-1)
        q = q.reshape(B, S, N_HEADS, HEAD_DIM)
        kv = kv.reshape(B, S, N_KV_SLOTS, N_KV_GROUPS, HEAD_DIM)
        nsa_gates = jax.nn.sigmoid(nsa_g.reshape(B, S, N_HEADS, N_NSA_BRANCHES))
        gate_pool, gate_nsa = jnp.split(jax.nn.sigmoid(merge_g), N_MERGE, axis=-1)
        y_pool = pooling_mixer(u, pool_w[l], pool_scale[l]) @ w_pool_out[l]
        y_nsa = nsa_mixer(q, kv[:, :, 0], kv[:, :, 1], kv[:, :, 2], kv[:, :, 3], kv[:, :, 4], kv[:, :, 5],
                          nsa_gates, positions, q_norm_g[l], k_norm_g[l], cmp_pe[l], cmp_w1[l],
                          cmp_w2[l]) @ w_nsa_out[l]
        x = x + (gate_pool * y_pool + gate_nsa * y_nsa) @ w_out[l]
        h = rms_norm(x, ffn_norm_g[l])
        gate_pre, val = jnp.split(h @ w_up[l], 2, axis=-1)
        gate_c = causal_dwconv(gate_pre, conv_w[l], conv_b[l])
        x = x + (jax.nn.silu(gate_c) * val) @ w_down[l]
    return x


DEPTH_2 = 2

CHUNK = 64
Q_BLOCK = 128
EPS = 1e-6

GLA_HEADS = 4
GLA_DK = 64
GLA_DV = 128
GLA_RANK = 16
GLA_TAU = 16.0
DSA_HEADS = 4
DSA_HD = 128
IDX_HEADS = 8
IDX_HD = 64
TOPK_MAX = 256
DIFF_HEADS = 4
DIFF_HD = 64

BR_W = 512
N_BRANCH = 3

SIZES = [
    GLA_HEADS * GLA_DK, GLA_HEADS * GLA_DK, GLA_HEADS * GLA_DV, GLA_RANK, BR_W,
    DSA_HEADS * DSA_HD, DSA_HEADS * DSA_HD, DSA_HEADS * DSA_HD,
    IDX_HEADS * IDX_HD, IDX_HD, IDX_HEADS, BR_W,
    DIFF_HEADS * 2 * DIFF_HD, DIFF_HEADS * 2 * DIFF_HD, DIFF_HEADS * 2 * DIFF_HD, BR_W,
    N_BRANCH * D_MODEL,
]
N_IN = int(sum(SIZES))
SPLIT_AT = [int(s) for s in np.cumsum(SIZES)[:-1]]


F32 = jnp.float32

def _rms(x, g=None):
    xf = x.astype(F32)
    y = xf * lax.rsqrt(jnp.mean(xf * xf, axis=-1, keepdims=True) + EPS)
    if g is not None:
        y = y * g.astype(F32)
    return y.astype(x.dtype)

def _chunk_visible(start, n_q, n_k):
    pos_q = start + jnp.arange(n_q)
    vis_end = (pos_q // CHUNK + 1) * CHUNK
    return jnp.arange(n_k)[None, :] < vis_end[:, None]

def _to_blocks(a, nb):
    return a.reshape((a.shape[0], nb, Q_BLOCK) + a.shape[2:]).swapaxes(0, 1)

def _gla(q, k, v, a_lr, wa2, ba, norm_g):
    B, T, _ = q.shape
    nc = T // CHUNK
    shp = (B, nc, CHUNK, GLA_HEADS)
    q = q.astype(F32).reshape(shp + (GLA_DK,)) * GLA_DK ** -0.5
    k = k.astype(F32).reshape(shp + (GLA_DK,))
    v = v.astype(F32).reshape(shp + (GLA_DV,))
    log_a = jax.nn.log_sigmoid((a_lr @ wa2 + ba).astype(F32)) / GLA_TAU
    log_a = log_a.reshape(shp + (GLA_DK,))
    cum = jnp.cumsum(log_a, axis=2)
    total = cum[:, :, -1]
    k_dec = k * jnp.exp(total[:, :, None] - cum)
    u = jnp.einsum('bnchk,bnchv->nbhkv', k_dec, v)
    decay = jnp.exp(total).transpose(1, 0, 2, 3)

    def step(S, inp):
        a, uc = inp
        S = a[..., None] * S + uc
        return S, S

    S0 = jnp.zeros((B, GLA_HEADS, GLA_DK, GLA_DV), F32)
    _, states = lax.scan(step, S0, (decay, u))
    o = jnp.einsum('bnchk,nbhkv->bnchv', q, states)
    o = _rms(o, norm_g)
    return o.reshape(B, T, GLA_HEADS * GLA_DV)

def _dsa(q, k, v, iq, ik, iw, qn_g, kn_g):
    B, T, _ = q.shape
    nb = T // Q_BLOCK
    topk = min(TOPK_MAX, T // 4)
    q = _rms(q.reshape(B, T, DSA_HEADS, DSA_HD), qn_g)
    k = _rms(k.reshape(B, T, DSA_HEADS, DSA_HD), kn_g)
    v = v.reshape(B, T, DSA_HEADS, DSA_HD)
    iq = iq.reshape(B, T, IDX_HEADS, IDX_HD)
    iw = iw.astype(F32) * IDX_HEADS ** -0.5
    starts = jnp.arange(nb) * Q_BLOCK

    def one(inp):
        qb, iqb, iwb, start = inp
        allowed = _chunk_visible(start, Q_BLOCK, T)
        dots = jnp.einsum('bqhd,bsd->bqhs', iqb, ik, preferred_element_type=F32) * IDX_HD ** -0.5
        score = jnp.einsum('bqhs,bqh->bqs', jax.nn.relu(dots), iwb)
        score = jnp.where(allowed[None], score, -jnp.inf)
        top_val, top_idx = lax.top_k(score, topk)
        valid = jnp.isfinite(top_val)
        k_sel = jax.vmap(lambda kk, ii: kk[ii])(k, top_idx)
        v_sel = jax.vmap(lambda vv, ii: vv[ii])(v, top_idx)
        logits = jnp.einsum('bqhd,bqshd->bhqs', qb, k_sel, preferred_element_type=F32) * DSA_HD ** -0.5
        logits = jnp.where(valid[:, None], logits, -jnp.inf)
        p = jax.nn.softmax(logits, axis=-1).astype(v.dtype)
        return jnp.einsum('bhqs,bqshd->bqhd', p, v_sel)

    out = lax.map(one, (_to_blocks(q, nb), _to_blocks(iq, nb), _to_blocks(iw, nb), starts))
    return out.swapaxes(0, 1).reshape(B, T, DSA_HEADS * DSA_HD)

def _diff(q, k, v, qn_g, kn_g, lq1, lk1, lq2, lk2, lambda_init):
    B, T, _ = q.shape
    nb = T // Q_BLOCK
    q = _rms(q.reshape(B, T, DIFF_HEADS, 2, DIFF_HD), qn_g)
    k = _rms(k.reshape(B, T, DIFF_HEADS, 2, DIFF_HD), kn_g)
    v = v.reshape(B, T, DIFF_HEADS, 2 * DIFF_HD)
    lam = (jnp.exp(jnp.sum(lq1.astype(F32) * lk1.astype(F32)))
           - jnp.exp(jnp.sum(lq2.astype(F32) * lk2.astype(F32))) + lambda_init)
    starts = jnp.arange(nb) * Q_BLOCK

    def one(inp):
        qb, start = inp
        allowed = _chunk_visible(start, Q_BLOCK, T)
        logits = jnp.einsum('bqhcd,bshcd->bhcqs', qb, k, preferred_element_type=F32) * DIFF_HD ** -0.5
        logits = jnp.where(allowed, logits, -jnp.inf)
        p = jax.nn.softmax(logits, axis=-1)
        attn = (p[:, :, 0] - lam * p[:, :, 1]).astype(v.dtype)
        return jnp.einsum('bhqs,bshd->bqhd', attn, v)

    out = lax.map(one, (_to_blocks(q, nb), starts)).swapaxes(0, 1)
    out = _rms(out) * (1.0 - lambda_init)
    return out.reshape(B, T, DIFF_HEADS * 2 * DIFF_HD)

def second_inputs(seed: int = 0) -> dict:
    key = jax.random.key(seed)
    ks = jax.random.split(key, 16)
    nrm = jax.random.normal
    L = DEPTH_2
    return {
        "x": nrm(ks[0], (BATCH, SEQ, D_MODEL), F32),
        "norm_g": 1.0 + 0.02 * nrm(ks[1], (L, D_MODEL), F32),
        "w_in": nrm(ks[2], (L, D_MODEL, N_IN), F32) * D_MODEL ** -0.5,
        "gla_wa2": nrm(ks[3], (L, GLA_RANK, GLA_HEADS * GLA_DK), F32) * GLA_RANK ** -0.5,
        "gla_ba": 1.0 + 0.1 * nrm(ks[4], (L, GLA_HEADS * GLA_DK), F32),
        "gla_norm_g": 1.0 + 0.02 * nrm(ks[5], (L, GLA_DV), F32),
        "dsa_qn_g": 1.0 + 0.02 * nrm(ks[6], (L, DSA_HD), F32),
        "dsa_kn_g": 1.0 + 0.02 * nrm(ks[7], (L, DSA_HD), F32),
        "diff_qn_g": 1.0 + 0.02 * nrm(ks[8], (L, DIFF_HD), F32),
        "diff_kn_g": 1.0 + 0.02 * nrm(ks[9], (L, DIFF_HD), F32),
        "diff_lq1": 0.1 * nrm(ks[10], (L, DIFF_HD), F32),
        "diff_lk1": 0.1 * nrm(ks[11], (L, DIFF_HD), F32),
        "diff_lq2": 0.1 * nrm(ks[12], (L, DIFF_HD), F32),
        "diff_lk2": 0.1 * nrm(ks[13], (L, DIFF_HD), F32),
        "w_br": nrm(ks[14], (L, N_BRANCH, BR_W, D_MODEL), F32) * BR_W ** -0.5,
        "w_out": nrm(ks[15], (L, D_MODEL, D_MODEL), F32) * D_MODEL ** -0.5,
    }

def second_block(x, norm_g, w_in, gla_wa2, gla_ba, gla_norm_g, dsa_qn_g, dsa_kn_g, diff_qn_g, diff_kn_g,
              diff_lq1, diff_lk1, diff_lq2, diff_lk2, w_br, w_out):
    B, T, _ = x.shape
    for l in range(DEPTH_2):
        h = _rms(x, norm_g[l])
        proj = h @ w_in[l]
        (gq, gk, gv, ga, gz, bq, bk, bv, iq, ik, iw, bz,
         cq, ck, cv, cz, gate) = jnp.split(proj, SPLIT_AT, axis=-1)
        lambda_init = 0.8 - 0.6 * math.exp(-0.3 * l)
        y_a = _gla(gq, gk, gv, ga, gla_wa2[l], gla_ba[l], gla_norm_g[l]).astype(x.dtype) * jax.nn.silu(gz)
        y_b = _dsa(bq, bk, bv, iq, ik, iw, dsa_qn_g[l], dsa_kn_g[l]) * jax.nn.silu(bz)
        y_c = _diff(cq, ck, cv, diff_qn_g[l], diff_kn_g[l], diff_lq1[l], diff_lk1[l],
                    diff_lq2[l], diff_lk2[l], lambda_init) * jax.nn.silu(cz)
        g = jax.nn.sigmoid(gate.reshape(B, T, N_BRANCH, D_MODEL))
        merged = (g[:, :, 0] * (y_a @ w_br[l, 0])
                  + g[:, :, 1] * (y_b @ w_br[l, 1])
                  + g[:, :, 2] * (y_c @ w_br[l, 2]))
        x = x + merged @ w_out[l]
    return x


def setup_inputs(seed=0):
    out = dict(first_inputs(seed))
    for name, value in second_inputs(seed + 1).items():
        if name != "x":
            out[name + "_2"] = value
    return out


def reference(
    x, positions, mix_norm_g, w_in, q_norm_g, k_norm_g, cmp_pe, cmp_w1, cmp_w2, pool_w,
    pool_scale, w_pool_out, w_nsa_out, w_out, ffn_norm_g, w_up, conv_w, conv_b, w_down,
    norm_g_2, w_in_2, gla_wa2_2, gla_ba_2, gla_norm_g_2, dsa_qn_g_2, dsa_kn_g_2, diff_qn_g_2,
    diff_kn_g_2, diff_lq1_2, diff_lk1_2, diff_lq2_2, diff_lk2_2, w_br_2, w_out_2,
):
    x = first_block(
        x, positions, mix_norm_g, w_in, q_norm_g, k_norm_g, cmp_pe, cmp_w1, cmp_w2, pool_w,
        pool_scale, w_pool_out, w_nsa_out, w_out, ffn_norm_g, w_up, conv_w, conv_b, w_down,
    )
    return second_block(
        x, norm_g_2, w_in_2, gla_wa2_2, gla_ba_2, gla_norm_g_2, dsa_qn_g_2, dsa_kn_g_2,
        diff_qn_g_2, diff_kn_g_2, diff_lq1_2, diff_lk1_2, diff_lq2_2, diff_lk2_2, w_br_2,
        w_out_2,
    )


_drawn_inputs = setup_inputs


def setup_inputs(seed=0):
    import zlib

    import numpy as np

    out = dict(_drawn_inputs(seed))
    spreads = {}
    factors = {'q_norm_g': 8.0,
     'k_norm_g': 8.0,
     'conv_b': 8.0,
     'norm_g_2': 2.858,
     'gla_ba_2': 2.958,
     'gla_norm_g_2': 7.579,
     'dsa_qn_g_2': 8.0,
     'dsa_kn_g_2': 8.0,
     'diff_qn_g_2': 8.0,
     'diff_kn_g_2': 8.0,
     'diff_lq1_2': 3.294,
     'diff_lk1_2': 8.0,
     'diff_lk2_2': 8.0}
    for name, (base, spread) in spreads.items():
        noise = np.random.default_rng([zlib.crc32(name.encode()), seed]).standard_normal(out[name].shape)
        drawn = base * np.exp(spread * noise) if base else spread * noise
        out[name] = jnp.asarray(drawn.astype(out[name].dtype))
    for name, factor in factors.items():
        out[name] = (out[name] * factor).astype(out[name].dtype)
    return out
```

```python
from contextlib import ExitStack

import numpy as np

import concourse.bass as bass
from concourse import mybir

F32 = mybir.dt.float32
F32R = mybir.dt.float32r
BF16 = mybir.dt.bfloat16
I32 = mybir.dt.int32
ALU = mybir.AluOpType
ACT = mybir.ActivationFunctionType
AX = mybir.AxisListType

P = 128
S = 512
D = 1024
KT = D // P
QT = S // P
EPS = 1e-6
NEG = -1e30
ROT = 16
THETA = 500000.0
N_CMP = 31
CMP_STRIDE = 16
WINDOWS = (2, 4, 8, 16)
D_FF = 2816
FF_TILES = D_FF // P
ROUNDS = (8, 8, 6)
TOPK = 128
CH = 64
LAYERS = 2
CHUNK = 2048
OFF = (0, 128, 384, 768)
TRI = 1280
KOFF = (0, 512, 896, 1152)

V_MIX, V_FFN, V_N2 = 0, 8, 16
V_CONVB, V_CONVW = 32, 54
V_PSCALE = 120
V_QG, V_KG = 124, 125
V_PE = 128
V_GLA, V_DQ, V_DK, V_CQ, V_CK = 192, 194, 196, 198, 200
V_LAM = 202
NVEC = 210
C_ID, C_BLK, C_ONE, C_PERM, C_SUF = 0, 128, 256, 384, 512
C_IND = 640
C_CNT = 642
C_INVF, C_SGN, C_VALID, C_EPS, C_ONES1 = 706, 707, 708, 709, 710
C_LINIT, C_1ML = 712, 714
C_E64, C_E128 = 716, 746
C_S128 = 761
NCST = 769
M_ID, M_TRI, M_CH, M_CMP = 0, 128, 256, 384
NMSK = 512

TWO_PI = 2 * np.pi
PI_HI = float(np.float32(201 / 32))
PI_MID = float(np.float32(np.floor((TWO_PI - 201 / 32) * 2**20) / 2**20))
PI_LO = float(np.float32(TWO_PI - 201 / 32 - np.floor((TWO_PI - 201 / 32) * 2**20) / 2**20))
ROUND = float(1.5 * 2**23)
TAKEN = -3e38


BLOCK1 = [("u", 2, 2), ("q", 2, 2), ("cmp", 1, 2), ("ksw", 1, 2), ("vsw", 1, 4), ("nsag", 1, 4),
          ("mg", 8, 2), ("merge1", 4, 4), ("wout", 4, 2),
          ("up0", 8, 2), ("down0", 4, 2), ("up1", 8, 2), ("down1", 4, 2), ("up2", 6, 2), ("down2", 4, 2)]
BLOCK2 = [("bq", 2, 2), ("bk", 2, 2), ("iq", 2, 2), ("ik", 1, 5), ("bv", 2, 4),
          ("bz", 2, 2), ("bgate", 4, 2), ("bbr", 2, 4),
          ("cq", 2, 2), ("ck", 2, 2), ("cv", 2, 4),
          ("cz", 2, 2), ("cgate", 4, 2), ("cbr", 2, 4),
          ("gq", 1, 2), ("gk", 1, 4), ("gv", 2, 4), ("ga", 1, 1), ("gz", 2, 2), ("agate", 4, 2), ("abr", 2, 4),
          ("wout2", 4, 2)]


def positions(sections):
    at, c, t = {}, 0, 0
    for name, n, per in sections:
        at[name] = (c, n, t, per)
        c += n
        t += n * per
    return at, c, t


POS1, CHUNKS1, TILES1 = positions(BLOCK1)
POS2, CHUNKS2, TILES2 = positions(BLOCK2)
CHUNKS = CHUNKS1 + LAYERS * CHUNKS2
assert CHUNKS1 % 2 == 0 and CHUNKS2 % 2 == 0 and TILES1 % 2 == 0 and TILES2 % 2 == 0


def section(name, l=None):
    if l is None:
        return POS1[name]
    c, n, t, per = POS2[name]
    return CHUNKS1 + CHUNKS2 * l + c, n, TILES1 + TILES2 * l + t, per


def two_block_kernel(nc, x_in, pos_in, w_in, vec_in, cst_in, msk_in, cmpw_in, small_in, spread_in, out):
    with ExitStack() as ctx:
        def sb(name, shape, dt):
            return ctx.enter_context(nc.sbuf_tensor(name, shape, dt))

        def sem(name):
            return ctx.enter_context(nc.semaphore(name))

        xT = sb("xT", [P, KT, S], F32)
        hhi, hlo = sb("hhi", [P, KT, S], F32R), sb("hlo", [P, KT, S], F32R)
        wraw = sb("wraw", [P, 2, CHUNK], F32)
        whi, wlo = sb("whi", [P, 2, CHUNK], F32R), sb("wlo", [P, 2, CHUNK], F32R)
        vec, cst, msk = sb("vec", [P, NVEC], F32), sb("cst", [P, NCST], F32), sb("msk", [P, NMSK], BF16)
        stat = sb("stat", [P, 64], F32)
        work = sb("work", [P, 15360], F32)
        split = sb("split", [P, 11328], F32R)

        pp = [ctx.enter_context(nc.psum_tensor(f"pp{i}", [P, S], F32)) for i in range(2)]
        ps = [ctx.enter_context(nc.psum_tensor(f"ps{i}", [P, S], F32)) for i in range(2)]
        pt = [ctx.enter_context(nc.psum_tensor(f"pt{i}", [P, S], F32)) for i in range(2)]
        po = [ctx.enter_context(nc.psum_tensor(f"po{i}", [P, S], F32)) for i in range(2)]

        def wv(at, *dims):
            n = int(np.prod(dims))
            v = work[:, at:at + n]
            if len(dims) == 2:
                v = v.rearrange("p (a b) -> p a b", a=dims[0])
            elif len(dims) == 3:
                v = v.rearrange("p (a b c) -> p a b c", a=dims[0], b=dims[1])
            return v

        def rv(at, *dims):
            n = int(np.prod(dims))
            v = split[:, at:at + n]
            if len(dims) == 2:
                v = v.rearrange("p (a b) -> p a b", a=dims[0])
            elif len(dims) == 3:
                v = v.rearrange("p (a b c) -> p a b c", a=dims[0], b=dims[1])
            return v

        def col(c, n=1):
            return vec[:, c:c + n]

        def con(c, n=1):
            return cst[:, c:c + n]

        ident, blk, ones, perm, suf = (con(c, P) for c in (C_ID, C_BLK, C_ONE, C_PERM, C_SUF))
        idb = msk[:, M_ID:M_ID + P]

        raw_in = [sem(f"raw_in{i}") for i in range(2)]
        w_hi, w_lo = sem("w_hi"), sem("w_lo")
        mm_done = sem("mm_done")
        evac = sem("evac")
        const_in = sem("const_in")
        stage = {e: sem(f"stage_{e}") for e in ("pe", "act", "dve", "pool")}
        sq_ready, ss_done, root_ready = sem("sq_ready"), sem("ss_done"), sem("root_ready")
        nrm_ready, nrm_hi = sem("nrm_ready"), sem("nrm_hi")
        hn_sq, hn_ss, hn_root, hn_out = sem("hn_sq"), sem("hn_ss"), sem("hn_root"), sem("hn_out")
        hn_inv, hn_bc, spread_in_sb = sem("hn_inv"), sem("hn_bc"), sem("spread_in_sb")
        hn_perm, hn_rope = sem("hn_perm"), sem("hn_rope")
        post = sem("post")
        rope_red, rope_sin = sem("rope_red"), sem("rope_sin")
        cmp_in, blk_ready, hid_done, hid_out = sem("cmp_in"), sem("blk_ready"), sem("hid_done"), sem("hid_out")
        kvc_done, kvc_out = sem("kvc_done"), sem("kvc_out")
        sc_ready, mx_ready, ex_done = sem("sc_ready"), sem("mx_ready"), sem("ex_done")
        diag_ready = sem("diag_ready")
        tr_done, pt_hi, pt_lo, pv_done = sem("tr_done"), sem("pt_hi"), sem("pt_lo"), sem("pv_done")
        o_out, ring_in, v_in = sem("o_out"), sem("ring_in"), sem("v_in")
        cs_ready, cs_sub, cs_exp, cs_p = sem("cs_ready"), sem("cs_sub"), sem("cs_exp"), sem("cs_p")
        ct_done, ct_out = sem("ct_done"), sem("ct_out")
        pool_in, pool_mm, poolw_in = sem("pool_in"), sem("pool_mm"), sem("poolw_in")
        part_hi = sem("part_hi")
        ff_conv, ff_sig, ff_prod, ff_hi = sem("ff_conv"), sem("ff_sig"), sem("ff_prod"), sem("ff_hi")
        ix_done, ix_relu = sem("ix_done"), sem("ix_relu")
        y_ready = sem("y_ready")
        lam_in, lam_sum, lam_exp = sem("lam_in"), sem("lam_sum"), sem("lam_exp")
        o_done, pool_out = sem("o_done"), sem("pool_out")
        wa2_in, z_done, g_exp, g_la = sem("wa2_in"), sem("z_done"), sem("g_exp"), sem("g_la")
        suf_done, decayed, kdec_ready = sem("suf_done"), sem("decayed"), sem("kdec_ready")
        u_done, state_ready, gla_o = sem("u_done"), sem("state_ready"), sem("gla_o")
        out_done = sem("out_done")

        stage_no = {e: 0 for e in stage}
        block = ctx.enter_context(nc.Block())

        def stage_end(eng, me):
            eng.drain().then_inc(stage[me], 1)
            stage_no[me] += 1
            for other in stage:
                if other != me:
                    eng.wait_ge(stage[other], stage_no[me])

        def pairs(eng, n, body, peel=False):
            if peel:
                for j in range(n):
                    body(j)
            elif n >= 2:
                with eng.Fori(0, n) as j:
                    body(j)
            else:
                body(0)

        def act_conv(act, c, slot):
            act.wait_ge(raw_in[slot], (c - slot) * 8 + 16)
            nc.scalar.activation(whi[:, slot, :], wraw[:, slot, :], ACT.Copy).then_inc(w_hi, 1)

        def dve_conv(dve, c, slot):
            dve.wait_ge(w_hi, c + 1)
            nc.vector.tensor_tensor(wlo[:, slot, :], wraw[:, slot, :], whi[:, slot, :].bitcast(F32),
                                    ALU.subtract).then_inc(w_lo, 1)

        def three(out_ap, a, b, start, stop):
            (ah, al), (bh, bl) = a, b
            nc.tensor.matmul(out_ap, ah, bh, start=start, stop=False)
            nc.tensor.matmul(out_ap, ah, bl, start=False, stop=False)
            return nc.tensor.matmul(out_ap, al, bh, start=False, stop=stop)

        def weights(slot, kt, cols):
            return [w[:, slot, 0:kt * cols].rearrange("p (k n) -> p k n", k=kt) for w in (whi, wlo)]

        def pe_tile(pe, t, par, product):
            if not (isinstance(t, int) and t < 2):
                pe.wait_ge(evac, t - 1)
            product(pp[par]).then_inc(mm_done, 1)

        def pe_fm(pe, name, l, h, kt, cols, tiles=None, m0=0):
            c0, n, t0, per = section(name, l)
            par0, slot0 = par_of(name, l)

            def body(j):
                for k in range(min(2, n)):
                    slot = (slot0 + k) % 2
                    c = c0 + 2 * j + k
                    pe.wait_ge(w_lo, c + 1)
                    wh, wl = weights(slot, kt, cols)
                    for m in range(per):
                        t = t0 + (2 * j + k) * per + m

                        def product(bank):
                            for x in range(kt):
                                cc = slice(m * P, m * P + P)
                                last = three(bank[:, :], (wh[:, x, cc], wl[:, x, cc]),
                                             (h[0][:, x, :], h[1][:, x, :]), x == 0, x == kt - 1)
                            return last
                        pe_tile(pe, t, (par0 + k * per + m) % 2, product)
            pairs(pe, max(1, n // 2), body)

        def pe_tm(pe, name, l, cols, at=0, stride=256, tile0=0, chunk_waits=True):
            c0, n, t0, per = section(name, l)
            par0, slot0 = par_of(name, l)
            for k in range(n):
                slot = (slot0 + k) % 2
                if chunk_waits:
                    pe.wait_ge(w_lo, c0 + k + 1)
                wh, wl = weights(slot, KT, stride)
                for i in range(QT):
                    def product(bank):
                        for x in range(KT):
                            tt = slice(i * P, i * P + P)
                            last = three(bank[:, 0:cols], (hhi[:, x, tt], hlo[:, x, tt]),
                                         (wh[:, x, at:at + cols], wl[:, x, at:at + cols]), x == 0, x == KT - 1)
                        return last
                    pe_tile(pe, t0 + k * per + tile0 + i, (par0 + k * per + tile0 + i) % 2, product)

        def par_of(name, l):
            c, _, t, _ = (POS1 if l is None else POS2)[name]
            return t % 2, c % 2

        def act_tiles(act, name, l, evacuate):
            c0, n, t0, per = section(name, l)
            par0, slot0 = par_of(name, l)

            def body(j):
                for k in range(min(2, n)):
                    for m in range(per):
                        t = t0 + (2 * j + k) * per + m
                        act.wait_ge(mm_done, t + 1)
                        evacuate(pp[(par0 + k * per + m) % 2], (2 * j + k) * per + m, m).then_inc(evac, 1)
                    act_next(act, name, l, c0 + 2 * j + k, (slot0 + k) % 2)
            pairs(act, max(1, n // 2), body, peel=is_last(name, l))

        def is_last(name, l):
            return name == "wout2" and l == LAYERS - 1

        def act_next(act, name, l, c, slot):
            if not is_last(name, l) or c + 2 < CHUNKS:
                act_conv(act, c + 2, slot)

        def dve_next(dve, name, l, after=None):
            c0, n, t0, per = section(name, l)
            _, slot0 = par_of(name, l)

            def body(j):
                for k in range(min(2, n)):
                    if not is_last(name, l) or c0 + 2 * j + k + 2 < CHUNKS:
                        dve_conv(dve, c0 + 2 * j + k + 2, (slot0 + k) % 2)
                    if after is not None:
                        for m in range(per):
                            after((2 * j + k) * per + m, t0 + (2 * j + k) * per + m)
            pairs(dve, max(1, n // 2), body, peel=is_last(name, l))

        T_SQ, T_ROOT, T_RR, T_T = 0, 1024, 1536, 2048

        def act_norm(act, n):
            for k in range(KT):
                if k >= 2:
                    act.wait_ge(ss_done, KT * n + k - 1)
                nc.scalar.activation(wv(T_SQ + 512 * (k % 2), 512), xT[:, k, :], ACT.Square).then_inc(sq_ready, 1)
            act.wait_ge(ss_done, KT * n + KT)
            nc.scalar.activation(wv(T_ROOT, 512), ps[0][:, :], ACT.Sqrt, scale=1.0 / D,
                                 bias=con(C_EPS)).then_inc(root_ready, 1)
            for k in range(KT):
                act.wait_ge(nrm_ready, KT * n + k + 1)
                nc.scalar.activation(hhi[:, k, :], wv(T_T + 512 * k, 512), ACT.Copy).then_inc(nrm_hi, 1)

        def pe_norm(pe, n):
            for k in range(KT):
                pe.wait_ge(sq_ready, KT * n + k + 1)
                nc.tensor.matmul(ps[0][:, :], ones, wv(T_SQ + 512 * (k % 2), 512), start=(k == 0),
                                 stop=(k == KT - 1)).then_inc(ss_done, 1)

        def inverse_root(dve, inv, root, squares, dim):
            nc.vector.reciprocal(inv, root)
            dve.drain()
            nc.vector.scalar_tensor_tensor(out=root, in0=inv, scalar=-0.5 / dim, in1=inv, op0=ALU.mult, op1=ALU.mult)
            dve.drain()
            nc.vector.scalar_tensor_tensor(out=root, in0=squares, scalar=EPS * dim, in1=root, op0=ALU.add, op1=ALU.mult)
            dve.drain()
            nc.vector.scalar_tensor_tensor(out=inv, in0=root, scalar=1.5, in1=inv, op0=ALU.add, op1=ALU.mult)
            dve.drain()

        def dve_norm(dve, n, gain):
            dve.wait_ge(root_ready, n + 1)
            inverse_root(dve, wv(T_RR, 512), wv(T_ROOT, 512), ps[0][:, :], D)
            for k in range(KT):
                nc.vector.scalar_tensor_tensor(out=wv(T_T + 512 * k, 512), in0=xT[:, k, :], scalar=gain(k),
                                               in1=wv(T_RR, 512), op0=ALU.mult, op1=ALU.mult).then_inc(nrm_ready, 1)

        def pool_norm(pool, n):
            for k in range(KT):
                pool.wait_ge(nrm_hi, KT * n + k + 1)
                nc.gpsimd.tensor_tensor(hlo[:, k, :], wv(T_T + 512 * k, 512), hhi[:, k, :].bitcast(F32),
                                        ALU.subtract)

        def act_hn(act, base, call, items, sq, root):
            if items[0][3] == 64:
                act.dma_start(wv(root + 1536, 8 * P)[0:16, :], spread_in[min(call, 1)]).then_inc(spread_in_sb, 16)
            for s, (src, width, _, dim, _, _) in enumerate(items):
                if s >= 2:
                    act.wait_ge(hn_ss, base + s - 1)
                nc.scalar.activation(wv(sq + 512 * (s % 2), 512)[:, 0:width], src, ACT.Square).then_inc(hn_sq, 1)
            act.wait_ge(hn_ss, base + len(items))
            rows = 8 * P // dim
            nc.scalar.activation(wv(root, 512)[0:rows, :], po[1][0:rows, :], ACT.Sqrt, scale=1.0 / dim,
                                 bias=con(C_EPS)[0:rows, :]).then_inc(hn_root, 1)

        def pe_hn(pe, base, call, rbase, items, sq, inv):
            for s, (_, width, _, dim, _, _) in enumerate(items):
                pe.wait_ge(hn_sq, base + s + 1)
                pick = con(C_E64 + 14 - 2 * s, 16) if dim == 64 else con(C_E128 + 7 - s, 8)
                nc.tensor.matmul(po[1][0:pick.shape[1], 0:width], pick, wv(sq + 512 * (s % 2), 512)[:, 0:width],
                                 start=(s == 0), stop=(s == len(items) - 1)).then_inc(hn_ss, 1)
            pe.wait_ge(hn_inv, call + 1)
            r = 0
            for s in range(len(items) + 1):
                if s < len(items):
                    _, width, _, dim, _, spread = items[s]
                    if s >= 2:
                        pe.wait_ge(hn_out, base + s - 1)
                    if dim == 64:
                        if s == 0:
                            pe.wait_ge(spread_in_sb, 16 * (1 + (call + 2) // 4))
                        rows, lhs = 16, wv(inv + 1024 + s * P, P)[0:16, :]
                    else:
                        rows, lhs = 8, con(spread + s)[0:8, :].broadcast_to([8, P])
                    nc.tensor.matmul(ps[s % 2][:, 0:width], lhs, wv(inv, 512)[0:rows, 0:width], start=True,
                                     stop=True).then_inc(hn_bc, 1)
                if s >= 1:
                    src, width, _, _, tables, _ = items[s - 1]
                    if tables is not None:
                        pe.wait_ge(hn_out, base + s)
                        if r >= 2:
                            pe.wait_ge(hn_rope, rbase + r - 1)
                        nc.tensor.matmul(pt[r % 2][:, 0:width], perm, src, start=True, stop=True).then_inc(hn_perm, 1)
                        r += 1

        def dve_hn(dve, base, call, rbase, items, root, inv, tmp):
            dim = items[0][3]
            rows = 8 * P // dim
            dve.wait_ge(hn_root, call + 1)
            inverse_root(dve, wv(inv, 512)[0:rows, :], wv(root, 512)[0:rows, :], po[1][0:rows, :], dim)
            dve.drain().then_inc(hn_inv, 1)

            def rotate(s, r):
                src, width, _, _, (cos, sin), _ = items[s]
                t2 = wv(tmp, 512)[:, 0:width]
                dve.wait_ge(hn_perm, rbase + r + 1)
                nc.vector.tensor_tensor(t2, pt[r % 2][:, 0:width], sin, ALU.mult).then_inc(hn_rope, 1)
                nc.vector.tensor_tensor(src, src, cos, ALU.mult)
                dve.drain()
                nc.vector.tensor_tensor(src, src, t2, ALU.add)
                dve.drain()
            for s, (src, width, gain, _, tables, _) in enumerate(items):
                dve.wait_ge(hn_bc, base + s + 1)
                nc.vector.scalar_tensor_tensor(out=src, in0=src, scalar=gain, in1=ps[s % 2][:, 0:width], op0=ALU.mult,
                                               op1=ALU.mult).then_inc(hn_out, 1)
                if tables is not None and s >= 1:
                    rotate(s - 1, s - 1)
            if items[-1][4] is not None:
                rotate(len(items) - 1, len(items) - 1)

        u_f, q_f, kcv_f, ksw_f = wv(0, 4, S), wv(2048, 4, S), wv(4096, 2, S), wv(5120, 2, S)
        v_f, g_f = wv(6144, 4, 256), wv(7168, 4, 24)
        kc_f, vc_f = wv(7264, 32), wv(7296, P)
        cos_t, sin_t = wv(7424, S), wv(7936, S)
        T = 8448
        w1_f = wv(T, 32, P)
        blk_f = wv(T + 4096, 32, N_CMP)
        hid_f = wv(T + 4096 + 992, 2, 32)
        cw2 = wv(T + 5152, 2, P)
        cp_f, ct_f = wv(T, 4, 32), wv(T + 128, S)
        poolw = wv(T + 2048, 4, P)
        mg_f, br_f = wv(4096, 16, S), wv(12288, 2, S)
        prod_f = wv(4096, KT, S)
        gp_f, vl_f, dn_f = wv(0, KT, S), wv(4096, KT, S), wv(8192, KT, S)
        cv_f, sg_f = wv(12288, 2, S), wv(13312, 2, S)
        pt_r = [[rv(2560 * b + TRI * y, TRI) for y in range(2)] for b in range(2)]
        qr = [[rv(5120 + 1024 * b + 512 * y, 512) for y in range(2)] for b in range(2)]
        kr = [[rv(7168 + 1024 * b + 512 * y, 512) for y in range(2)] for b in range(2)]
        vr = [[rv(9216 + 1024 * b + 512 * y, 4, P) for y in range(2)] for b in range(2)]
        kcr = [rv(11264 + 32 * y, 32) for y in range(2)]
        yr = [rv(0, 4, S), rv(2048, 4, S)]
        yr2 = [rv(4096, 4, S), rv(6144, 4, S)]
        mr = [rv(0, KT, S), rv(4096, KT, S)]
        merged = wv(0, KT, S)
        a_f, b_f = wv(4096, 4, S), wv(6144, 4, S)
        c_f = wv(8192, 4, S)
        iq_f, ik_f, iw_f = wv(10240, 4, S), wv(12288, S), wv(14464, 4, 8)
        sc_f = [wv(12800 + 512 * b, S) for b in range(2)]
        selm = wv(13824, 640).bitcast(BF16)
        relu_f = [wv(512 * b, S) for b in range(2)]
        iqr = [rv(2048 * y, 4, S) for y in range(2)]
        ikr = [rv(4096 + 512 * y, 512) for y in range(2)]
        z_f, gate_f, br2_f = wv(6144, 4, S), wv(8192, KT, S), wv(12288, 2, S)
        gq_f, gk_f, gv_f = wv(6144, 2, S), wv(7168, 4, 256), wv(8192, 4, S)
        alr_f, za_f, la_f, kd_f = wv(10240, S), wv(10752, 4, 256), wv(11776, 4, 256), wv(12800, 4, 256)
        st_f = [wv(13824 + 512 * b, 2, 256) for b in range(2)]
        dec_f, wa2_f = wv(14848, 2, 8), wv(14880, 256)
        nmx = [stat[:, 4 * b:4 * b + 4] for b in range(2)]
        rsum = [stat[:, 8 + 4 * b:12 + 4 * b] for b in range(2)]
        rcp = [stat[:, 16 + 4 * b:20 + 4 * b] for b in range(2)]
        cstat, lam = stat[:, 24:32], stat[:, 32:40]

        def p_of(base, b):
            return wv(base + TRI * b, TRI)

        P1, P_DSA, P_DIFF = 12800, 10240, 10240
        diag1, diag_dsa = wv(10240, QT, P), wv(12800, QT, P)
        diag_diff = [b_f[:, c, :].rearrange("p (i n) -> p i n", i=QT) for c in range(2)]

        h = (hhi, hlo)

        def pe_scores(pe, u, i, q, k, rows, mask):
            w = P * (i + 1)
            if 4 * u + i >= 2:
                pe.wait_ge(ex_done, 4 * u + i - 1)
            bank = ps[i % 2]
            three(bank[:, 0:w], [x[rows, i * P:i * P + P] for x in q], [x[rows, 0:w] for x in k], True, False)
            at, mk = mask(i)
            nc.tensor.matmul(bank[:, at:w], idb, mk, start=False, stop=True).then_inc(sc_ready, 1)

        def dve_max(dve, u, i):
            dve.wait_ge(sc_ready, 4 * u + i + 1)
            nc.vector.tensor_reduce(nmx[u % 2][:, i:i + 1], ps[i % 2][:, 0:P * (i + 1)], AX.X, ALU.max,
                                    negate=True).then_inc(mx_ready, 1)

        def act_exp(act, u, i, dst):
            w = P * (i + 1)
            act.wait_ge(mx_ready, 4 * u + i + 1)
            nc.scalar.activation(dst[:, OFF[i]:OFF[i] + w], ps[i % 2][:, 0:w], ACT.Exp, bias=nmx[u % 2][:, i:i + 1],
                                 accum_out=rsum[u % 2][:, i:i + 1]).then_inc(ex_done, 1)

        def pe_transpose(pe, v, kb, exps, diags):
            if kb == 0:
                pe.wait_ge(diag_ready, v + 1)
            if 4 * v + kb >= 2:
                pe.wait_ge(pt_lo, 4 * v + kb - 1)
            for i in range(kb, QT):
                for n, (src, diag) in enumerate(zip(exps, diags)):
                    last = nc.tensor.matmul(pt[kb % 2][:, (i - kb) * P:(i - kb + 1) * P],
                                            src[:, OFF[i] + kb * P:OFF[i] + kb * P + P], diag[:, i, :],
                                            start=(n == 0), stop=(n == len(exps) - 1))
            last.then_inc(tr_done, 1)

        def make_diag(diag, factor):
            return nc.vector.tensor_tensor(diag, ident.unsqueeze(1).broadcast_to([P, QT, P]),
                                           factor.unsqueeze(2).broadcast_to([P, QT, P]), ALU.mult)

        def act_pt(act, v, kb):
            w = S - P * kb
            act.wait_ge(tr_done, 4 * v + kb + 1)
            nc.scalar.activation(pt_r[v % 2][0][:, KOFF[kb]:KOFF[kb] + w], pt[kb % 2][:, 0:w],
                                 ACT.Copy).then_inc(pt_hi, 1)

        def dve_pt(dve, v, kb):
            w = S - P * kb
            dve.wait_ge(pt_hi, 4 * v + kb + 1)
            nc.vector.tensor_tensor(pt_r[v % 2][1][:, KOFF[kb]:KOFF[kb] + w], pt[kb % 2][:, 0:w],
                                    pt_r[v % 2][0][:, KOFF[kb]:KOFF[kb] + w].bitcast(F32),
                                    ALU.subtract).then_inc(pt_lo, 1)

        def pe_pv(pe, v, kb, vals, bank, start, stop):
            pe.wait_ge(pt_lo, 4 * v + kb + 1)
            w = S - P * kb
            last = three(bank[:, kb * P:S], [x[:, kb, :] for x in vals],
                         [x[:, KOFF[kb]:KOFF[kb] + w] for x in pt_r[v % 2]], start, stop)
            if kb == QT - 1:
                last.then_inc(pv_done, 1)

        def split_pool(pool, parts, src):
            nc.gpsimd.tensor_copy(parts[0], src)
            pool.drain()
            return nc.gpsimd.tensor_tensor(parts[1], src, parts[0].bitcast(F32), ALU.subtract)

        def copy_to(dst, func=ACT.Copy, **kw):
            return lambda bank, n, m: nc.scalar.activation(tile(dst, n), bank[:, :], func, **kw)

        def tile(v, n):
            return v[:, n, :] if isinstance(n, int) else v[:, bass.ds(n, 1), :].rearrange("p a s -> p (a s)")

        def gated_add(dve, t0, first, gate, branch, n, par, merged_tile):
            dve.wait_ge(evac, t0 + n + 1)
            if first:
                nc.vector.tensor_tensor(merged_tile, gate, branch[:, par, :], ALU.mult).then_inc(post, 1)
            else:
                nc.vector.tensor_tensor(branch[:, par, :], gate, branch[:, par, :], ALU.mult)
                dve.drain()
                nc.vector.tensor_tensor(merged_tile, merged_tile, branch[:, par, :], ALU.add).then_inc(post, 1)

        def act_branch(act, name, l, post0, branch):
            c0, n, t0, per = section(name, l)
            par0, slot0 = par_of(name, l)
            for k in range(n):
                for m in range(4):
                    tt = 4 * k + m
                    act.wait_ge(mm_done, t0 + tt + 1)
                    if tt >= 2:
                        act.wait_ge(post, post0 + tt - 1)
                    nc.scalar.activation(branch[:, m % 2, :], pp[(par0 + m) % 2][:, :], ACT.Copy).then_inc(evac, 1)
                act_next(act, name, l, c0 + k, (slot0 + k) % 2)

        def pe_branch(pe, name, l, operand):
            c0, n, t0, per = section(name, l)
            par0, slot0 = par_of(name, l)
            for k in range(n):
                pe.wait_ge(w_lo, c0 + k + 1)
                wh, wl = weights((slot0 + k) % 2, 4, 512)
                y = operand(k)
                for m in range(4):
                    def product(bank):
                        for x in range(4):
                            cc = slice(m * P, m * P + P)
                            last = three(bank[:, :], (wh[:, x, cc], wl[:, x, cc]), (y[0][:, x, :], y[1][:, x, :]),
                                         x == 0, x == 3)
                        return last
                    pe_tile(pe, t0 + 4 * k + m, (par0 + m) % 2, product)

        def dve_add_x(dve, src, n, t):
            dve.wait_ge(evac, t + 1)
            nc.vector.tensor_tensor(tile(xT, n), tile(xT, n), tile(src, n), ALU.add)

        def y_rows(g):
            return slice(64 * g, 64 * g + 64)

        k_items = [(ksw_f[:, 0, :], S, col(V_KG + 1), 64, (cos_t, sin_t), None),
                   (ksw_f[:, 1, :], S, col(V_KG + 2), 64, (cos_t, sin_t), None)]
        k_items += [(q_f[:, t, :], S, col(V_QG), 64, (cos_t, sin_t), C_ID) for t in range(4)]
        cmp_at = slice(2 * CMP_STRIDE - 1, None, CMP_STRIDE)
        k_items += [(kc_f[:, 0:N_CMP], N_CMP, col(V_KG), 64, (cos_t[:, cmp_at], sin_t[:, cmp_at]), None)]
        HN1, ROPES = len(k_items), len(k_items)
        HN_LAYER = 8 + 8 + 4 + 4
        U1 = 16
        FF = [0, 8, 16]

        def causal(i):
            return P * i, msk[:, M_TRI:M_TRI + P]

        def chunked(i):
            return P * i, msk[:, M_CH:M_CH + P]

        def selected(i):
            return (0, selm[:, OFF[i]:OFF[i] + P * (i + 1)]) if i else (0, msk[:, M_CH:M_CH + P])

        def layer_items(l):
            dsa = [(a_f[:, t, :], S, col(V_DQ + l), P, None, C_ID) for t in range(4)]
            dsa += [(b_f[:, t, :], S, col(V_DK + l), P, None, C_S128) for t in range(4)]
            diff = [(a_f[:, t, :], S, col(V_CQ + l), 64, None, C_ID) for t in range(4)]
            diff += [(b_f[:, t, :], S, col(V_CK + l), 64, None, None) for t in range(4)]
            diff_o = [(a_f[:, t, :], S, con(C_1ML + l), P, None, C_ID) for t in range(4)]
            gla_o_ = [(a_f[:, t, :], S, col(V_GLA + l), P, None, C_ID) for t in range(4)]
            return dsa, diff, diff_o, gla_o_

        def pe_layer(pe, l):
            dsa, diff, diff_out, gla_out = layer_items(l)
            hb = HN1 + HN_LAYER * l
            pe_norm(pe, 2 + l)
            stage_end(pe, "pe")
            for name in ("bq", "bk", "iq"):
                pe_fm(pe, name, l, h, KT, 256)
            c0, n, t0, per = section("ik", l)
            par0, slot0 = par_of("ik", l)
            pe.wait_ge(w_lo, c0 + 1)
            wh, wl = weights(slot0, KT, 256)

            def ik_product(bank):
                for x in range(KT):
                    last = three(bank[:, :], (wh[:, x, 0:P], wl[:, x, 0:P]), (hhi[:, x, :], hlo[:, x, :]), x == 0, x == KT - 1)
                return last
            pe_tile(pe, t0, par0, ik_product)
            pe_tm(pe, "ik", l, 8, at=P, tile0=1, chunk_waits=False)
            pe_tm(pe, "bv", l, 256)
            stage_end(pe, "pe")
            pe_hn(pe, hb, 1 + 4 * l, 0, dsa, 0, 0 + 1536)
            stage_end(pe, "pe")
            for i in range(1, QT):
                for hd in range(8):
                    e = 24 * l + 8 * (i - 1) + hd
                    if e >= 2:
                        pe.wait_ge(ix_relu, e - 1)
                    rows = y_rows(hd % 2)
                    three(ps[e % 2][:, 0:P * (i + 1)], [x[rows, hd // 2, i * P:i * P + P] for x in iqr],
                          [x[rows, 0:P * (i + 1)] for x in ikr], True, True).then_inc(ix_done, 1)
            stage_end(pe, "pe")
            for s in range(4 + 2):
                if s < 4:
                    pe.wait_ge(ring_in, 4 + 8 * l + s + 1)
                for i in range(QT + 1):
                    if s < 4 and i < QT:
                        pe_scores(pe, U1 + 12 * l + s, i, qr[s % 2], kr[s % 2], slice(0, P), selected)
                    if 1 <= s <= 4 and i >= 1:
                        pe_transpose(pe, U1 + 8 * l + s - 1, i - 1, [p_of(P_DSA, (s - 1) % 2)], [diag_dsa])
                    if s >= 2 and i < QT:
                        if i == 0 and s >= 4:
                            pe.wait_ge(o_out, 8 + 8 * l + s - 3)
                        if i == 0:
                            pe.wait_ge(v_in, 8 * l + s - 1)
                        pe_pv(pe, U1 + 8 * l + s - 2, i, vr[s % 2], po[s % 2], i == 0, i == 3)
            stage_end(pe, "pe")
            pe_fm(pe, "bz", l, h, KT, 256)
            pe_fm(pe, "bgate", l, h, KT, 256)
            stage_end(pe, "pe")
            pe_branch(pe, "bbr", l, lambda k: yr)
            stage_end(pe, "pe")
            pe_fm(pe, "cq", l, h, KT, 256)
            pe_fm(pe, "ck", l, h, KT, 256)
            pe_tm(pe, "cv", l, 256)
            stage_end(pe, "pe")
            pe.wait_ge(lam_in, l + 1)
            nc.tensor.matmul(po[0][:, 0:2], ones, lam[:, 0:2], start=True, stop=True).then_inc(lam_sum, 1)
            pe_hn(pe, hb + 8, 2 + 4 * l, 0, diff, P_DIFF, P_DIFF + 1536)
            stage_end(pe, "pe")
            for s in range(4 + 2):
                if s < 4:
                    pe.wait_ge(ring_in, 4 + 8 * l + 4 + s + 1)
                for comp in range(2):
                    for i in range(QT):
                        if s < 4:
                            pe_scores(pe, U1 + 12 * l + 4 + 2 * s + comp, i, qr[s % 2], kr[s % 2], y_rows(comp), chunked)
                        if s >= 2 and comp == 0:
                            if i == 0 and s >= 4:
                                pe.wait_ge(o_out, 8 + 8 * l + 4 + s - 3)
                            if i == 0:
                                pe.wait_ge(v_in, 8 * l + 4 + s - 1)
                            pe_pv(pe, U1 + 8 * l + 4 + s - 2, i, vr[s % 2], po[s % 2], i == 0, i == 3)
                        if 1 <= s <= 4 and comp == 1:
                            pe_transpose(pe, U1 + 8 * l + 4 + s - 1, i,
                                         [wv(P_DIFF + TRI * (2 * ((s - 1) % 2) + c), TRI) for c in range(2)], diag_diff)
            stage_end(pe, "pe")
            pe_hn(pe, hb + 16, 3 + 4 * l, 0, diff_out, P_DIFF, P_DIFF + 1536)
            stage_end(pe, "pe")
            pe_fm(pe, "cz", l, h, KT, 256)
            pe_fm(pe, "cgate", l, h, KT, 256)
            stage_end(pe, "pe")
            pe_branch(pe, "cbr", l, lambda k: yr)
            stage_end(pe, "pe")
            pe_fm(pe, "gq", l, h, KT, 256)
            pe_tm(pe, "gk", l, 256)
            pe_tm(pe, "gv", l, 256)
            pe_fm(pe, "ga", l, h, KT, 256, )
            stage_end(pe, "pe")
            pe.wait_ge(wa2_in, 16 * (l + 1))
            for i in range(QT):
                last = nc.tensor.matmul(ps[i // 2][:, 256 * (i % 2):256 * (i % 2) + 256], alr_f[0:17, i * P:i * P + P],
                                        wa2_f[0:17, :], start=True, stop=True)
            last.then_inc(z_done, 1)
            pe.wait_ge(g_la, l + 1)
            for i in range(QT):
                nc.tensor.matmul(pt[i // 2][:, 256 * (i % 2):256 * (i % 2) + 256], suf, la_f[:, i, :], start=True, stop=True)
            for hp in range(2):
                for i in range(QT):
                    last = nc.tensor.matmul(pp[0][:, 8 * hp + 2 * i:8 * hp + 2 * i + 2], la_f[:, i, hp * P:hp * P + P],
                                            con(C_IND, 2), start=True, stop=True)
            last.then_inc(suf_done, 1)
            pe.wait_ge(kdec_ready, l + 1)
            for c in range(8 + 1):
                if c < 8:
                    i, rows = c // 2, y_rows(c % 2)
                    if c >= 1:
                        pe.wait_ge(state_ready, 8 * l + c)
                    for hp in range(2):
                        last = nc.tensor.matmul(pp[1][:, 256 * hp:256 * hp + 256], kd_f[rows, i, hp * P:hp * P + P],
                                                gv_f[rows, i, 256 * hp:256 * hp + 256], start=True, stop=True)
                    last.then_inc(u_done, 1)
                if c >= 1:
                    pe.wait_ge(state_ready, 8 * l + c)
                    for hd in range(4):
                        rows = y_rows(hd % 2)
                        bank = (po[0], po[1], ps[0], ps[1])[hd]
                        last = nc.tensor.matmul(bank[:, CH * (c - 1):CH * c],
                                                st_f[(c - 1) % 2][rows, hd // 2, P * (hd % 2):P * (hd % 2) + P],
                                                gq_f[rows, hd // 2, CH * (c - 1):CH * c], start=True, stop=True)
                    last.then_inc(gla_o, 1)
            stage_end(pe, "pe")
            pe_hn(pe, hb + 20, 4 + 4 * l, 0, gla_out, 6144, 6144 + 1536)
            stage_end(pe, "pe")
            pe_fm(pe, "gz", l, h, KT, 256)
            pe_fm(pe, "agate", l, h, KT, 256)
            stage_end(pe, "pe")
            pe_branch(pe, "abr", l, lambda k: yr)
            stage_end(pe, "pe")
            stage_end(pe, "pe")
            pe_fm(pe, "wout2", l, mr, KT, 256)
            stage_end(pe, "pe")

        def act_layer(act, l):
            dsa, diff, diff_out, gla_out = layer_items(l)
            hb = HN1 + HN_LAYER * l
            act_norm(act, 2 + l)
            stage_end(act, "act")
            act_tiles(act, "bq", l, copy_to(a_f))
            act_tiles(act, "bk", l, copy_to(b_f))
            act_tiles(act, "iq", l, copy_to(iq_f))
            act_tiles(act, "ik", l, lambda bank, n, m: nc.scalar.activation(
                ik_f if m == 0 else iw_f[:, m - 1, :], bank[:, :] if m == 0 else bank[:, 0:8], ACT.Copy))
            act_tiles(act, "bv", l, lambda bank, n, m: nc.scalar.activation(
                c_f[:, m, 256 * (n // 4):256 * (n // 4) + 256], bank[:, 0:256], ACT.Copy))
            stage_end(act, "act")
            act_hn(act, hb, 1 + 4 * l, dsa, 0, 0 + 1024)
            for x in range(5):
                dst, src = (iqr[0][:, x, :], iq_f[:, x, :]) if x < 4 else (ikr[0], ik_f)
                nc.scalar.activation(dst, src, ACT.Copy).then_inc(part_hi, 1)
            stage_end(act, "act")
            for i in range(1, QT):
                for hd in range(8):
                    e = 24 * l + 8 * (i - 1) + hd
                    act.wait_ge(ix_done, e + 1)
                    if e - 24 * l >= 2:
                        act.wait_ge(post, POST_IX(l) + e - 24 * l - 1)
                    nc.scalar.activation(relu_f[e % 2][:, 0:P * (i + 1)], ps[e % 2][:, 0:P * (i + 1)], ACT.Relu,
                                         scale=0.125).then_inc(ix_relu, 1)
            stage_end(act, "act")
            for s in range(4 + 2):
                for i in range(QT + 1):
                    if s < 4 and i < QT:
                        u = U1 + 12 * l + s
                        if i == 0 and s >= 2:
                            act.wait_ge(tr_done, 4 * (U1 + 8 * l + s - 2) + 4)
                        act_exp(act, u, i, p_of(P_DSA, s % 2))
                    if 1 <= s <= 4 and i >= 1:
                        v = U1 + 8 * l + s - 1
                        if i == 1 and s >= 3:
                            act.wait_ge(pv_done, v - 1)
                        act_pt(act, v, i - 1)
                if 2 <= s < 6:
                    act.wait_ge(pv_done, U1 + 8 * l + s - 2 + 1)
                    nc.scalar.activation(a_f[:, s - 2, :], po[s % 2][:, :], ACT.Copy).then_inc(o_out, 1)
            stage_end(act, "act")
            act_tiles(act, "bz", l, copy_to(z_f, ACT.Silu))
            act_tiles(act, "bgate", l, copy_to(gate_f, ACT.Sigmoid))
            act_y(act, 3 * l)
            stage_end(act, "act")
            act_branch(act, "bbr", l, POST_BR(l, 0), br2_f)
            stage_end(act, "act")
            act_tiles(act, "cq", l, copy_to(a_f))
            act_tiles(act, "ck", l, copy_to(b_f))
            act_tiles(act, "cv", l, lambda bank, n, m: nc.scalar.activation(
                c_f[:, m, 256 * (n // 4):256 * (n // 4) + 256], bank[:, 0:256], ACT.Copy))
            stage_end(act, "act")
            act.wait_ge(lam_sum, l + 1)
            nc.scalar.activation(lam[:, 2:4], po[0][:, 0:2], ACT.Exp).then_inc(lam_exp, 1)
            act_hn(act, hb + 8, 2 + 4 * l, diff, P_DIFF, P_DIFF + 1024)
            stage_end(act, "act")
            for s in range(4 + 2):
                for comp in range(2):
                    for i in range(QT):
                        if s < 4:
                            u = U1 + 12 * l + 4 + 2 * s + comp
                            if comp == 0 and i == 0 and s >= 2:
                                act.wait_ge(tr_done, 4 * (U1 + 8 * l + 4 + s - 2) + 4)
                            act_exp(act, u, i, wv(P_DIFF + TRI * (2 * (s % 2) + comp), TRI))
                        if 1 <= s <= 4 and comp == 1:
                            v = U1 + 8 * l + 4 + s - 1
                            if i == 0 and s >= 3:
                                act.wait_ge(pv_done, v - 1)
                            act_pt(act, v, i)
                if 2 <= s < 6:
                    act.wait_ge(pv_done, U1 + 8 * l + 4 + s - 2 + 1)
                    nc.scalar.activation(a_f[:, s - 2, :], po[s % 2][:, :], ACT.Copy).then_inc(o_out, 1)
            stage_end(act, "act")
            act_hn(act, hb + 16, 3 + 4 * l, diff_out, P_DIFF, P_DIFF + 1024)
            stage_end(act, "act")
            act_tiles(act, "cz", l, copy_to(z_f, ACT.Silu))
            act_tiles(act, "cgate", l, copy_to(gate_f, ACT.Sigmoid))
            act_y(act, 3 * l + 1)
            stage_end(act, "act")
            act_branch(act, "cbr", l, POST_BR(l, 1), br2_f)
            stage_end(act, "act")
            act.dma_start(wa2_f, small_in[:, 6 * P + 256 * l:6 * P + 256 * l + 256]).then_inc(wa2_in, 16)
            act_tiles(act, "gq", l, copy_to(gq_f, scale=0.125))
            act_tiles(act, "gk", l, lambda bank, n, m: nc.scalar.activation(gk_f[:, m, :], bank[:, 0:256], ACT.Copy))
            act_tiles(act, "gv", l, lambda bank, n, m: nc.scalar.activation(
                gv_f[:, m, 256 * (n // 4):256 * (n // 4) + 256], bank[:, 0:256], ACT.Copy))
            act_tiles(act, "ga", l, lambda bank, n, m: nc.scalar.activation(alr_f[0:16, :], bank[0:16, :], ACT.Copy))
            stage_end(act, "act")
            act.wait_ge(z_done, l + 1)
            for x in range(2):
                nc.scalar.activation(za_f[:, 2 * x:2 * x + 2, :].rearrange("p a b -> p (a b)"), ps[x][:, :], ACT.Abs)
            act.drain()
            za = za_f.rearrange("p a b -> p (a b)")
            nc.scalar.activation(za, za, ACT.Exp, scale=-1.0)
            act.drain()
            nc.scalar.activation(za, za, ACT.Ln, bias=con(C_ONES1)).then_inc(g_exp, 1)
            act.wait_ge(suf_done, l + 1)
            for x in range(2):
                nc.scalar.activation(za_f[:, 2 * x:2 * x + 2, :].rearrange("p a b -> p (a b)"), pt[x][:, :], ACT.Exp)
            nc.scalar.activation(dec_f, pp[0][:, 0:16].rearrange("p (a b) -> p a b", a=2), ACT.Exp)
            act.drain().then_inc(decayed, 1)
            act.wait_ge(gla_o, 8 * l + 8)
            for hd in range(4):
                nc.scalar.activation(a_f[:, hd, :], (po[0], po[1], ps[0], ps[1])[hd][:, :], ACT.Copy)
            stage_end(act, "act")
            act_hn(act, hb + 20, 4 + 4 * l, gla_out, 6144, 6144 + 1024)
            stage_end(act, "act")
            act_tiles(act, "gz", l, copy_to(z_f, ACT.Silu))
            act_tiles(act, "agate", l, copy_to(gate_f, ACT.Sigmoid))
            act_y(act, 3 * l + 2)
            stage_end(act, "act")
            act_branch(act, "abr", l, POST_BR(l, 2), br2_f)
            stage_end(act, "act")
            for x in range(KT):
                nc.scalar.activation(mr[0][:, x, :], merged[:, x, :], ACT.Copy).then_inc(part_hi, 1)
            stage_end(act, "act")
            act_tiles(act, "wout2", l, copy_to(prod_f))
            stage_end(act, "act")

        def act_y(act, n):
            for x in range(4):
                act.wait_ge(y_ready, 4 * n + x + 1)
                nc.scalar.activation(yr[0][:, x, :], a_f[:, x, :], ACT.Copy).then_inc(part_hi, 1)

        def pool_y(pool, n, hi0):
            for x in range(4):
                pool.wait_ge(part_hi, hi0 + x + 1)
                nc.gpsimd.tensor_tensor(yr[1][:, x, :], a_f[:, x, :], yr[0][:, x, :].bitcast(F32), ALU.subtract)

        POST_LAYER = 24 + 24
        def POST_IX(l):
            return 16 + POST_LAYER * l

        def POST_BR(l, b):
            return 16 + POST_LAYER * l + 24 + 8 * b

        PART1 = 4 + KT
        PART_LAYER = 5 + 12 + KT

        def dve_branch(dve, name, l, b):
            c0, n, t0, per = section(name, l)
            _, slot0 = par_of(name, l)
            for k in range(n):
                for m in range(4):
                    j = 4 * k + m
                    gated_add(dve, t0, b == 0, gate_f[:, j, :], br2_f, j, m % 2, merged[:, j, :])
                dve_conv(dve, c0 + k + 2, (slot0 + k) % 2)

        def dve_y(dve, z_name, gate_name, l):
            c0, n, t0, per = section(z_name, l)

            def after(nn, t):
                dve.wait_ge(evac, t + 1)
                nc.vector.tensor_tensor(tile(a_f, nn), tile(a_f, nn), tile(z_f, nn), ALU.mult).then_inc(y_ready, 1)
            dve_next(dve, z_name, l, after)
            dve_next(dve, gate_name, l)

        def dve_layer(dve, l):
            dsa, diff, diff_out, gla_out = layer_items(l)
            hb = HN1 + HN_LAYER * l
            dve_norm(dve, 2 + l, lambda k: col(V_N2 + 8 * l + k))
            stage_end(dve, "dve")
            for name in ("bq", "bk", "iq", "ik", "bv"):
                dve_next(dve, name, l)
            stage_end(dve, "dve")
            nc.vector.tensor_scalar(iw_f, iw_f, float(8 ** -0.5), None, ALU.mult)
            dve_hn(dve, hb, 1 + 4 * l, 0, dsa, 0 + 1024, 0 + 1536, 0 + 2048)
            stage_end(dve, "dve")
            for i in range(1, QT):
                w = P * (i + 1)
                sc, m8 = sc_f[i % 2][:, 0:w], stat[:, 48:56]
                for hd in range(8):
                    e = 24 * l + 8 * (i - 1) + hd
                    dve.wait_ge(ix_relu, e + 1)
                    r = relu_f[e % 2][:, 0:w]
                    if hd == 0:
                        nc.vector.tensor_scalar(sc, r, iw_f[:, i, hd:hd + 1], None, ALU.mult).then_inc(post, 1)
                    else:
                        dve.drain()
                        nc.vector.scalar_tensor_tensor(out=sc, in0=r, scalar=iw_f[:, i, hd:hd + 1], in1=sc,
                                                       op0=ALU.mult, op1=ALU.add).then_inc(post, 1)
                dve.drain()
                nc.vector.memset(sc[0:64, w - CH:w], NEG)
                for _ in range(TOPK // 8):
                    dve.drain()
                    nc.vector.max(m8, sc)
                    dve.drain()
                    nc.vector.match_replace(sc, m8, sc, TAKEN)
                dve.drain()
                nc.vector.tensor_scalar(selm[:, OFF[i]:OFF[i] + w], sc, TAKEN, NEG, ALU.is_gt, ALU.mult)
            stage_end(dve, "dve")
            for s in range(4 + 1):
                for i in range(QT + 1):
                    if s < 4 and i < QT:
                        u = U1 + 12 * l + s
                        if i == 0 and s >= 2:
                            dve.wait_ge(ex_done, 4 * (u - 1))
                        dve_max(dve, u, i)
                    if 1 <= s <= 4 and i >= 1:
                        dve_pt(dve, U1 + 8 * l + s - 1, i - 1)
                if s < 4:
                    u = U1 + 12 * l + s
                    v = U1 + 8 * l + s
                    dve.wait_ge(ex_done, 4 * u + 4)
                    nc.vector.reciprocal(rcp[0], rsum[u % 2])
                    dve.drain()
                    if s >= 1:
                        dve.wait_ge(tr_done, 4 * v)
                    make_diag(diag_dsa, rcp[0]).then_inc(diag_ready, 1)
            stage_end(dve, "dve")
            dve_y(dve, "bz", "bgate", l)
            stage_end(dve, "dve")
            dve_branch(dve, "bbr", l, 0)
            stage_end(dve, "dve")
            for name in ("cq", "ck", "cv"):
                dve_next(dve, name, l)
            stage_end(dve, "dve")
            v0 = V_LAM + 4 * l
            for x in range(2):
                nc.vector.tensor_tensor(lam[:, x:x + 1], col(v0 + 2 * x), col(v0 + 2 * x + 1), ALU.mult)
            dve.drain().then_inc(lam_in, 1)
            dve.wait_ge(lam_exp, l + 1)
            nc.vector.tensor_tensor(lam[:, 4:5], lam[:, 3:4], lam[:, 2:3], ALU.subtract)
            dve.drain()
            nc.vector.tensor_tensor(lam[:, 4:5], lam[:, 4:5], con(C_LINIT + l), ALU.subtract)
            dve_hn(dve, hb + 8, 2 + 4 * l, 0, diff, P_DIFF + 1024, P_DIFF + 1536, P_DIFF + 2048)
            stage_end(dve, "dve")
            for s in range(4 + 1):
                for comp in range(2):
                    for i in range(QT):
                        if s < 4:
                            u = U1 + 12 * l + 4 + 2 * s + comp
                            if i == 0 and 2 * s + comp >= 2:
                                dve.wait_ge(ex_done, 4 * (u - 1))
                            dve_max(dve, u, i)
                        if 1 <= s <= 4 and comp == 1:
                            dve_pt(dve, U1 + 8 * l + 4 + s - 1, i)
                    if s < 4:
                        dve.wait_ge(ex_done, 4 * u + 4)
                        nc.vector.reciprocal(rcp[comp], rsum[u % 2])
                        dve.drain()
                if s < 4:
                    nc.vector.tensor_scalar(rcp[1], rcp[1], lam[:, 4:5], None, ALU.mult)
                    dve.drain()
                    if s == 0:
                        dve.wait_ge(ring_in, 4 + 8 * l + 4 + 2)
                    else:
                        dve.wait_ge(tr_done, 4 * (U1 + 8 * l + 4 + s))
                    make_diag(diag_diff[0], rcp[0])
                    make_diag(diag_diff[1], rcp[1])
                    dve.drain().then_inc(diag_ready, 1)
            stage_end(dve, "dve")
            dve_hn(dve, hb + 16, 3 + 4 * l, 0, diff_out, P_DIFF + 1024, P_DIFF + 1536, P_DIFF + 2048)
            stage_end(dve, "dve")
            dve_y(dve, "cz", "cgate", l)
            stage_end(dve, "dve")
            dve_branch(dve, "cbr", l, 1)
            nc.vector.memset(alr_f[0:32, :], 1.0)
            stage_end(dve, "dve")
            for name in ("gq", "gk", "gv", "ga"):
                dve_next(dve, name, l)
            stage_end(dve, "dve")
            dve.wait_ge(g_exp, l + 1)
            for x in range(2):
                a = la_f[:, 2 * x:2 * x + 2, :].rearrange("p a b -> p (a b)")
                nc.vector.tensor_scalar(a, ps[x][:, :], 0.0, None, ALU.min)
            dve.drain()
            nc.vector.tensor_tensor(la_f, la_f, za_f, ALU.subtract)
            dve.drain()
            nc.vector.tensor_scalar(la_f, la_f, 1.0 / 16, None, ALU.mult).then_inc(g_la, 1)
            dve.wait_ge(decayed, l + 1)
            nc.vector.tensor_tensor(kd_f, gk_f, za_f, ALU.mult).then_inc(kdec_ready, 1)
            for c in range(8):
                dve.wait_ge(u_done, 8 * l + c + 1)
                if c >= 2:
                    dve.wait_ge(gla_o, 8 * l + c - 1)
                for hp in range(2):
                    new = st_f[c % 2][:, hp, :]
                    if c == 0:
                        nc.vector.tensor_copy(new, pp[1][:, 256 * hp:256 * hp + 256])
                    else:
                        nc.vector.scalar_tensor_tensor(out=new, in0=st_f[(c - 1) % 2][:, hp, :], scalar=dec_f[:, hp, c:c + 1],
                                                       in1=pp[1][:, 256 * hp:256 * hp + 256], op0=ALU.mult, op1=ALU.add)
                dve.drain().then_inc(state_ready, 1)
            stage_end(dve, "dve")
            dve_hn(dve, hb + 20, 4 + 4 * l, 0, gla_out, 6144 + 1024, 6144 + 1536, 6144 + 2048)
            stage_end(dve, "dve")
            dve_y(dve, "gz", "agate", l)
            stage_end(dve, "dve")
            dve_branch(dve, "abr", l, 2)
            stage_end(dve, "dve")
            stage_end(dve, "dve")
            dve_next(dve, "wout2", l, lambda n, t: dve_add_x(dve, prod_f, n, t))
            stage_end(dve, "dve")

        def pool_layer(pool, l):
            p0 = PART1 + PART_LAYER * l
            pool_norm(pool, 2 + l)
            stage_end(pool, "pool")
            stage_end(pool, "pool")
            for x in range(5):
                hi, lo, src = (iqr[0][:, x, :], iqr[1][:, x, :], iq_f[:, x, :]) if x < 4 else (ikr[0], ikr[1], ik_f)
                pool.wait_ge(part_hi, p0 + x + 1)
                nc.gpsimd.tensor_tensor(lo, src, hi.bitcast(F32), ALU.subtract)
            stage_end(pool, "pool")
            stage_end(pool, "pool")

            def ring(s):
                split_pool(pool, qr[s % 2], a_f[:, s, :])
                split_pool(pool, kr[s % 2], b_f[:, s, :])
                pool.drain().then_inc(ring_in, 1)

            def v_ring(s, v):
                if s >= 2:
                    pool.wait_ge(pv_done, v - 1)
                split_pool(pool, vr[s % 2], c_f[:, :, s * P:s * P + P]).then_inc(v_in, 1)
            ring(0)
            ring(1)
            v_ring(0, 0)
            v_ring(1, 0)
            for s in range(4):
                if s < 2:
                    pool.wait_ge(ex_done, 4 * (U1 + 12 * l + s + 1))
                    ring(s + 2)
                else:
                    v_ring(s, U1 + 8 * l + 0 + s)
            stage_end(pool, "pool")
            pool_y(pool, 3 * l, p0 + 5)
            stage_end(pool, "pool")
            stage_end(pool, "pool")
            stage_end(pool, "pool")
            stage_end(pool, "pool")
            ring(0)
            ring(1)
            v_ring(0, 0)
            v_ring(1, 0)
            for s in range(4):
                if s < 2:
                    pool.wait_ge(ex_done, 4 * (U1 + 12 * l + 4 + 2 * s + 2))
                    ring(s + 2)
                else:
                    v_ring(s, U1 + 8 * l + 4 + s)
            stage_end(pool, "pool")
            stage_end(pool, "pool")
            pool_y(pool, 3 * l + 1, p0 + 9)
            stage_end(pool, "pool")
            for _ in range(4):
                stage_end(pool, "pool")
            pool_y(pool, 3 * l + 2, p0 + 13)
            stage_end(pool, "pool")
            stage_end(pool, "pool")
            for x in range(KT):
                pool.wait_ge(part_hi, p0 + 17 + x + 1)
                nc.gpsimd.tensor_tensor(mr[1][:, x, :], merged[:, x, :], mr[0][:, x, :].bitcast(F32), ALU.subtract)
            stage_end(pool, "pool")
            stage_end(pool, "pool")

        def act_ff(act, r, k):
            n = sum(ROUNDS[:r]) + k
            act.wait_ge(ff_conv, n + 1)
            nc.scalar.activation(sg_f[:, k % 2, :], cv_f[:, k % 2, :], ACT.Sigmoid).then_inc(ff_sig, 1)
            act.wait_ge(ff_prod, n + 1)
            nc.scalar.activation(mr[0][:, k, :], gp_f[:, k, :], ACT.Copy).then_inc(ff_hi, 1)

        @block.tensor
        def _(pe):
            pe.wait_ge(const_in, 80)
            stage_end(pe, "pe")
            pe_norm(pe, 0)
            stage_end(pe, "pe")
            pe_fm(pe, "u", None, h, KT, 256)
            pe_fm(pe, "q", None, h, KT, 256)
            pe_fm(pe, "cmp", None, h, KT, 256)
            pe_fm(pe, "ksw", None, h, KT, 256)
            pe_tm(pe, "vsw", None, 256)
            pe_tm(pe, "nsag", None, 24)
            stage_end(pe, "pe")
            for kv in range(2):
                pe.wait_ge(blk_ready, kv + 1)
                pe.wait_ge(cmp_in, 32 + 16 * kv)
                for g in range(2):
                    rows = y_rows(g)
                    for l in range(32):
                        last = nc.tensor.matmul(ps[g][:, 0:N_CMP], w1_f[rows, l, :], blk_f[rows, l, :],
                                                start=(l == 0), stop=(l == 31))
                    last.then_inc(hid_done, 1)
                pe.wait_ge(hid_out, 2 * kv + 2)
                if kv:
                    pe.wait_ge(kvc_out, 2)
                for g in range(2):
                    if kv == 0:
                        last = nc.tensor.matmul(pt[g][:, 0:N_CMP], cw2[:, 0, :], hid_f[:, g, 0:N_CMP],
                                                start=True, stop=True)
                    else:
                        last = nc.tensor.matmul(pt[g][0:N_CMP, 0:64], hid_f[:, g, 0:N_CMP], cw2[:, 1, 0:64],
                                                start=True, stop=True)
                    last.then_inc(kvc_done, 1)
            stage_end(pe, "pe")
            pe_hn(pe, 0, 0, 0, k_items, T, T + 1536)
            stage_end(pe, "pe")
            stage_end(pe, "pe")
            for s in range(U1 + 2):
                if s < U1:
                    hd, b = s // 2, s % 2
                    t, g = hd // 2, hd % 2
                    if b == 0:
                        if g == 0:
                            pe.wait_ge(ring_in, t + 1)
                        if hd >= 1:
                            pe.wait_ge(cs_sub, hd)
                        rows = y_rows(g)
                        for i in range(QT):
                            three(pp[0][:, 32 * i:32 * i + 32], [x[rows, i * P:i * P + P] for x in qr[t % 2]],
                                  [x[rows, :] for x in kcr], True, False)
                            last = nc.tensor.matmul(pp[0][:, 32 * i:32 * i + 32], idb,
                                                    msk[:, M_CMP + 32 * i:M_CMP + 32 * i + 32],
                                                    start=False, stop=True)
                        last.then_inc(cs_ready, 1)
                for i in range(QT + 1):
                    if s < U1 and i < QT:
                        pe_scores(pe, s, i, qr[t % 2], kr[b], y_rows(g), causal)
                    if 1 <= s <= U1 and i >= 1:
                        pe_transpose(pe, s - 1, i - 1, [p_of(P1, (s - 1) % 2)], [diag1])
                    if s >= 2 and i < QT:
                        v = s - 2
                        hv = v // 2
                        if v % 2 == 0 and i == 0 and hv >= 2:
                            pe.wait_ge(o_out, hv - 1)
                        pe_pv(pe, v, i, vr[v % 2], po[hv % 2], v % 2 == 0 and i == 0, False)
                        if v % 2 == 1 and i == 3:
                            pe.wait_ge(ct_out, hv + 1)
                            last = nc.tensor.matmul(po[hv % 2][:, :], vc_f[0:32, :], ct_f[0:32, :],
                                                    start=False, stop=True)
                            last.then_inc(o_done, 1)
                if s < U1 and s % 2 == 1:
                    hd = s // 2
                    pe.wait_ge(cs_p, hd + 1)
                    if hd >= 1:
                        pe.wait_ge(ct_out, hd)
                    for i in range(QT):
                        last = nc.tensor.transpose(pp[1][0:32, i * P:i * P + P], cp_f[:, i, :], ident)
                    last.then_inc(ct_done, 1)
            stage_end(pe, "pe")
            for g in range(4):
                pe.wait_ge(pool_in, g + 1)
                if g == 0:
                    pe.wait_ge(poolw_in, 16)
                if g >= 2:
                    pe.wait_ge(pool_out, g - 1)
                nc.tensor.matmul(ps[g % 2][:, :], poolw[:, g, :], u_f[:, g, :], start=True,
                                 stop=True).then_inc(pool_mm, 1)
            stage_end(pe, "pe")
            pe_fm(pe, "mg", None, h, KT, 256)
            stage_end(pe, "pe")
            pe_branch(pe, "merge1", None, lambda k: yr if k % 2 == 0 else yr2)
            stage_end(pe, "pe")
            stage_end(pe, "pe")
            pe_fm(pe, "wout", None, mr, KT, 256)
            stage_end(pe, "pe")
            pe_norm(pe, 1)
            stage_end(pe, "pe")
            for r in range(3):
                pe_fm(pe, f"up{r}", None, h, KT, 256)
                stage_end(pe, "pe")
                pe_fm(pe, f"down{r}", None, mr, ROUNDS[r], 256)
                stage_end(pe, "pe")
            for l in range(LAYERS):
                pe_layer(pe, l)

        @block.scalar
        def _(act):
            act.wait_ge(const_in, 80)
            act_conv(act, 0, 0)
            act_conv(act, 1, 1)
            act.wait_ge(rope_red, 1)
            nc.scalar.activation(sin_t, wv(T + 1024, S), ACT.Sin).then_inc(rope_sin, 1)
            nc.scalar.activation(cos_t, wv(T + 1536, S), ACT.Sin)
            stage_end(act, "act")
            act_norm(act, 0)
            stage_end(act, "act")
            act.dma_start(w1_f, cmpw_in[0]).then_inc(cmp_in, 16)
            act.dma_start(cw2, small_in[:, 4 * P:6 * P].rearrange("p (v n) -> p v n", v=2)).then_inc(cmp_in, 16)
            act_tiles(act, "u", None, copy_to(u_f))
            act_tiles(act, "q", None, copy_to(q_f))
            act_tiles(act, "cmp", None, copy_to(kcv_f))
            act_tiles(act, "ksw", None, copy_to(ksw_f))
            act_tiles(act, "vsw", None, lambda bank, n, m: nc.scalar.activation(v_f[:, m, :], bank[:, 0:256], ACT.Copy))
            act_tiles(act, "nsag", None,
                      lambda bank, n, m: nc.scalar.activation(g_f[:, m, :], bank[:, 0:24], ACT.Sigmoid))
            stage_end(act, "act")
            for kv in range(2):
                for g in range(2):
                    act.wait_ge(hid_done, 2 * kv + g + 1)
                    if kv == 0 and g == 1:
                        act.dma_start(w1_f, cmpw_in[1]).then_inc(cmp_in, 16)
                    if kv == 1 and g == 0:
                        act.wait_ge(kvc_done, 2)
                    nc.scalar.activation(hid_f[:, g, 0:N_CMP], ps[g][:, 0:N_CMP], ACT.Silu).then_inc(hid_out, 1)
                for g in range(2):
                    act.wait_ge(kvc_done, 2 * kv + g + 1)
                    if kv == 0:
                        nc.scalar.activation(kc_f[y_rows(g), 0:N_CMP], pt[g][y_rows(g), 0:N_CMP],
                                             ACT.Copy).then_inc(kvc_out, 1)
                    else:
                        nc.scalar.activation(vc_f[0:N_CMP, y_rows(g)], pt[g][0:N_CMP, 0:64],
                                             ACT.Copy).then_inc(kvc_out, 1)
            stage_end(act, "act")
            act_hn(act, 0, 0, k_items, T, T + 1024)
            stage_end(act, "act")
            stage_end(act, "act")
            for s in range(U1 + 2):
                for i in range(QT + 1):
                    if s < U1 and i < QT:
                        if i == 0 and s >= 2:
                            act.wait_ge(tr_done, 4 * (s - 2) + 4)
                        act_exp(act, s, i, p_of(P1, s % 2))
                    if 1 <= s <= U1 and i >= 1:
                        v = s - 1
                        if i == 1 and v >= 2:
                            act.wait_ge(pv_done, v - 1)
                        act_pt(act, v, i - 1)
                if s < U1 and s % 2 == 0:
                    hd = s // 2
                    act.wait_ge(cs_sub, hd + 1)
                    nc.scalar.activation(cp_f, cp_f, ACT.Exp).then_inc(cs_exp, 1)
                if s < U1 and s % 2 == 1:
                    hd = s // 2
                    act.wait_ge(ct_done, hd + 1)
                    if hd >= 1:
                        act.wait_ge(o_done, hd)
                    nc.scalar.activation(ct_f[0:32, :], pp[1][0:32, :], ACT.Copy).then_inc(ct_out, 1)
                if s >= 3 and s % 2 == 1:
                    hv = (s - 3) // 2
                    t, g = hv // 2, hv % 2
                    act.wait_ge(o_done, hv + 1)
                    nc.scalar.activation(q_f[y_rows(g), t, :], po[hv % 2][y_rows(g), :], ACT.Copy).then_inc(o_out, 1)
            stage_end(act, "act")
            act.dma_start(poolw, small_in[:, 0:4 * P].rearrange("p (g n) -> p g n", g=4)).then_inc(poolw_in, 16)
            for g in range(4):
                act.wait_ge(pool_mm, g + 1)
                nc.scalar.activation(u_f[:, g, :], ps[g % 2][:, :], ACT.Copy, scale=col(V_PSCALE + g)
                                     ).then_inc(pool_out, 1)
            stage_end(act, "act")
            act_tiles(act, "mg", None, copy_to(mg_f, ACT.Sigmoid))
            for x in range(4):
                nc.scalar.activation(yr[0][:, x, :], u_f[:, x, :], ACT.Copy)
                nc.scalar.activation(yr2[0][:, x, :], q_f[:, x, :], ACT.Copy).then_inc(part_hi, 1)
            stage_end(act, "act")
            act_branch(act, "merge1", None, 0, br_f)
            stage_end(act, "act")
            for x in range(KT):
                nc.scalar.activation(mr[0][:, x, :], mg_f[:, x, :], ACT.Copy).then_inc(part_hi, 1)
            stage_end(act, "act")
            act_tiles(act, "wout", None, copy_to(prod_f))
            stage_end(act, "act")
            act_norm(act, 1)
            stage_end(act, "act")
            for r in range(3):
                c0, n, t0, per = section(f"up{r}")
                for k in range(ROUNDS[r]):
                    act.wait_ge(mm_done, t0 + 2 * k + 1)
                    nc.scalar.activation(gp_f[:, k, :], pp[0][:, :], ACT.Copy).then_inc(evac, 1)
                    act.wait_ge(mm_done, t0 + 2 * k + 2)
                    nc.scalar.activation(vl_f[:, k, :], pp[1][:, :], ACT.Copy).then_inc(evac, 1)
                    act_conv(act, c0 + k + 2, (c0 + k) % 2)
                    if k >= 1:
                        act_ff(act, r, k - 1)
                act_ff(act, r, ROUNDS[r] - 1)
                stage_end(act, "act")
                act_tiles(act, f"down{r}", None, copy_to(dn_f))
                stage_end(act, "act")
            for l in range(LAYERS):
                act_layer(act, l)

        @block.vector
        def _(dve):
            dve.wait_ge(const_in, 80)
            dve_conv(dve, 0, 0)
            dve_conv(dve, 1, 1)
            ang, kk, red, redc = wv(T, S), wv(T + 512, S), wv(T + 1024, S), wv(T + 1536, S)
            nc.vector.tensor_copy(kk, cos_t.bitcast(I32))
            nc.vector.tensor_copy(msk[:, :], wv(T + 2048, NMSK))
            dve.drain()
            nc.vector.tensor_scalar(ang, kk, con(C_INVF), None, ALU.mult)
            dve.drain()
            nc.vector.tensor_scalar(kk, ang, 1.0 / TWO_PI, None, ALU.mult)
            dve.drain()
            nc.vector.tensor_scalar(kk, kk, ROUND, None, ALU.add)
            dve.drain()
            nc.vector.tensor_scalar(kk, kk, -ROUND, None, ALU.add)
            dve.drain()
            for part in (PI_HI, PI_MID, PI_LO):
                nc.vector.scalar_tensor_tensor(out=ang, in0=kk, scalar=-part, in1=ang, op0=ALU.mult, op1=ALU.add)
                dve.drain()
            nc.vector.tensor_scalar(red, ang, 3.1415925, -3.1415925, ALU.min, ALU.max)
            nc.vector.tensor_scalar(redc, ang, float(np.pi / 2), None, ALU.add)
            dve.drain()
            nc.vector.tensor_scalar(kk, redc, float(np.pi), -TWO_PI, ALU.is_gt, ALU.mult)
            dve.drain()
            nc.vector.tensor_tensor(redc, redc, kk, ALU.add)
            dve.drain()
            nc.vector.tensor_scalar(redc, redc, 3.1415925, -3.1415925, ALU.min, ALU.max).then_inc(rope_red, 1)
            dve.wait_ge(rope_sin, 1)
            nc.vector.tensor_scalar(sin_t, sin_t, con(C_SGN), None, ALU.mult)
            nc.vector.memset(kc_f, 0.0)
            nc.vector.memset(vc_f, 0.0)
            stage_end(dve, "dve")
            dve_norm(dve, 0, lambda k: col(V_MIX + k))
            stage_end(dve, "dve")
            for name in ("u", "q", "cmp", "ksw", "vsw", "nsag"):
                dve_next(dve, name, None)
            stage_end(dve, "dve")
            for kv in range(2):
                if kv == 1:
                    dve.wait_ge(hid_done, 2)
                src = kcv_f[:, kv, :]
                taps = bass.AP(src.tensor, src.offset, [src.ap[0], [1, 32], [CMP_STRIDE, N_CMP]])
                pe_b = vec[:, V_PE + 32 * kv:V_PE + 32 * kv + 32].unsqueeze(2).broadcast_to([P, 32, N_CMP])
                nc.vector.tensor_tensor(blk_f, taps, pe_b, ALU.add).then_inc(blk_ready, 1)
            stage_end(dve, "dve")
            dve_hn(dve, 0, 0, 0, k_items, T + 1024, T + 1536, T + 2048)
            stage_end(dve, "dve")
            stage_end(dve, "dve")
            for s in range(U1 + 2):
                if s < U1 and s % 2 == 0:
                    hd = s // 2
                    dve.wait_ge(cs_ready, hd + 1)
                    if hd >= 1:
                        dve.wait_ge(ct_done, hd)
                    c3 = pp[0][:, 0:P].rearrange("p (i n) -> p i n", i=4)
                    nc.vector.tensor_reduce(cstat[:, 0:4], c3, AX.X, ALU.max)
                    dve.drain()
                    nc.vector.tensor_tensor(cp_f, c3, cstat[:, 0:4].unsqueeze(2).broadcast_to([P, 4, 32]),
                                            ALU.subtract).then_inc(cs_sub, 1)
                for i in range(QT + 1):
                    if s < U1 and i < QT:
                        if i == 0 and s >= 2:
                            dve.wait_ge(ex_done, 4 * (s - 1))
                        dve_max(dve, s, i)
                    if 1 <= s <= U1 and i >= 1:
                        dve_pt(dve, s - 1, i - 1)
                if s < U1 and s % 2 == 0:
                    hd = s // 2
                    head = hd // 2 + 4 * (hd % 2)
                    dve.wait_ge(cs_exp, hd + 1)
                    nc.vector.tensor_reduce(cstat[:, 4:8], cp_f, AX.X, ALU.add)
                    dve.drain()
                    nc.vector.reciprocal(cstat[:, 4:8], cstat[:, 4:8])
                    dve.drain()
                    nc.vector.tensor_tensor(cstat[:, 4:8], cstat[:, 4:8], g_f[:, :, 3 * head], ALU.mult)
                    dve.drain()
                    nc.vector.tensor_tensor(cstat[:, 4:5], cstat[:, 4:5], con(C_VALID), ALU.mult)
                    dve.drain()
                    nc.vector.tensor_tensor(cp_f, cp_f, cstat[:, 4:8].unsqueeze(2).broadcast_to([P, 4, 32]),
                                            ALU.mult).then_inc(cs_p, 1)
                if s < U1:
                    hd, b = s // 2, s % 2
                    head = hd // 2 + 4 * (hd % 2)
                    dve.wait_ge(ex_done, 4 * s + 4)
                    nc.vector.reciprocal(rcp[0], rsum[s % 2])
                    dve.drain()
                    nc.vector.tensor_tensor(rcp[0], rcp[0], g_f[:, :, 3 * head + 1 + b], ALU.mult)
                    dve.drain()
                    if s >= 1:
                        dve.wait_ge(tr_done, 4 * s)
                    make_diag(diag1, rcp[0]).then_inc(diag_ready, 1)
            stage_end(dve, "dve")
            pa, pb = wv(T, S), wv(T + 512, S)
            for g, w in enumerate(WINDOWS):
                src = u_f[:, g, :]
                cur, span, bufs = src, 1, [pa, pb]
                while span < w:
                    dst = bufs[0] if cur is not bufs[0] else bufs[1]
                    nc.vector.tensor_copy(dst[:, 0:span], cur[:, 0:span])
                    nc.vector.tensor_tensor(dst[:, span:S], cur[:, span:S], cur[:, 0:S - span], ALU.add)
                    dve.drain()
                    cur, span = dst, 2 * span
                nc.vector.tensor_tensor(cur[:, 0:16], cur[:, 0:16], con(C_CNT + 16 * g, 16), ALU.mult)
                dve.drain()
                nc.vector.scalar_tensor_tensor(out=src[:, 16:S], in0=cur[:, 16:S], scalar=1.0 / w, in1=src[:, 16:S],
                                               op0=ALU.mult, op1=ALU.subtract)
                nc.vector.tensor_tensor(src[:, 0:16], cur[:, 0:16], src[:, 0:16], ALU.subtract)
                dve.drain().then_inc(pool_in, 1)
            stage_end(dve, "dve")
            dve_next(dve, "mg", None)
            stage_end(dve, "dve")
            c0, n, t0, per = section("merge1")
            for k in range(4):
                for m in range(4):
                    j = 4 * (k // 2) + m
                    if k % 2 == 0:
                        gated_add(dve, t0, True, mg_f[:, j, :], br_f, 4 * k + m, m % 2, mg_f[:, j, :])
                    else:
                        gated_add(dve, t0, False, mg_f[:, 8 + j, :], br_f, 4 * k + m, m % 2, mg_f[:, j, :])
                dve_conv(dve, c0 + k + 2, (c0 + k) % 2)
            stage_end(dve, "dve")
            stage_end(dve, "dve")
            dve_next(dve, "wout", None, lambda n, t: dve_add_x(dve, prod_f, n, t))
            stage_end(dve, "dve")
            dve_norm(dve, 1, lambda k: col(V_FFN + k))
            stage_end(dve, "dve")
            for r in range(3):
                c0, n, t0, per = section(f"up{r}")
                for k in range(ROUNDS[r]):
                    dve_conv(dve, c0 + k + 2, (c0 + k) % 2)
                    ft = sum(ROUNDS[:r]) + k
                    y, gp = cv_f[:, k % 2, :], gp_f[:, k, :]
                    dve.wait_ge(evac, t0 + 2 * k + 1)
                    nc.vector.tensor_scalar(y, gp, col(V_CONVW + 2 * FF_TILES + ft), None, ALU.mult)
                    dve.drain()
                    nc.vector.scalar_tensor_tensor(out=y[:, 1:S], in0=gp[:, 0:S - 1], scalar=col(V_CONVW + FF_TILES + ft),
                                                   in1=y[:, 1:S], op0=ALU.mult, op1=ALU.add)
                    dve.drain()
                    nc.vector.scalar_tensor_tensor(out=y[:, 2:S], in0=gp[:, 0:S - 2], scalar=col(V_CONVW + ft),
                                                   in1=y[:, 2:S], op0=ALU.mult, op1=ALU.add)
                    dve.drain()
                    nc.vector.tensor_scalar(y, y, col(V_CONVB + ft), None, ALU.add).then_inc(ff_conv, 1)
                    dve.wait_ge(evac, t0 + 2 * k + 2)
                    dve.drain()
                    nc.vector.tensor_tensor(gp, y, vl_f[:, k, :], ALU.mult)
                    dve.drain()
                    dve.wait_ge(ff_sig, ft + 1)
                    nc.vector.tensor_tensor(gp, gp, sg_f[:, k % 2, :], ALU.mult).then_inc(ff_prod, 1)
                stage_end(dve, "dve")
                dve_next(dve, f"down{r}", None, lambda n, t: dve_add_x(dve, dn_f, n, t))
                stage_end(dve, "dve")
            for l in range(LAYERS):
                dve_layer(dve, l)

        @block.gpsimd
        def _(pool):
            pool.wait_ge(const_in, 80)
            stage_end(pool, "pool")
            pool_norm(pool, 0)
            stage_end(pool, "pool")
            stage_end(pool, "pool")
            stage_end(pool, "pool")
            stage_end(pool, "pool")
            for b in range(2):
                split_pool(pool, kr[b], ksw_f[:, b, :])
                split_pool(pool, vr[b], v_f[:, :, b * P:b * P + P])
            split_pool(pool, kcr, kc_f)
            stage_end(pool, "pool")

            def q_parts(t):
                if t >= 2:
                    pool.wait_ge(ex_done, 16 * (t - 1))
                split_pool(pool, qr[t % 2], q_f[:, t, :]).then_inc(ring_in, 1)
            q_parts(0)
            for t in range(1, 4):
                q_parts(t)
            stage_end(pool, "pool")
            stage_end(pool, "pool")
            for x in range(4):
                pool.wait_ge(part_hi, x + 1)
                nc.gpsimd.tensor_tensor(yr[1][:, x, :], u_f[:, x, :], yr[0][:, x, :].bitcast(F32), ALU.subtract)
                nc.gpsimd.tensor_tensor(yr2[1][:, x, :], q_f[:, x, :], yr2[0][:, x, :].bitcast(F32), ALU.subtract)
            stage_end(pool, "pool")
            stage_end(pool, "pool")
            for x in range(KT):
                pool.wait_ge(part_hi, 4 + x + 1)
                nc.gpsimd.tensor_tensor(mr[1][:, x, :], mg_f[:, x, :], mr[0][:, x, :].bitcast(F32), ALU.subtract)
            stage_end(pool, "pool")
            stage_end(pool, "pool")
            pool_norm(pool, 1)
            stage_end(pool, "pool")
            for r in range(3):
                for k in range(ROUNDS[r]):
                    n = sum(ROUNDS[:r]) + k
                    pool.wait_ge(ff_hi, n + 1)
                    nc.gpsimd.tensor_tensor(mr[1][:, k, :], gp_f[:, k, :], mr[0][:, k, :].bitcast(F32), ALU.subtract)
                stage_end(pool, "pool")
                stage_end(pool, "pool")
            for l in range(LAYERS):
                pool_layer(pool, l)

        assert len(set(stage_no.values())) == 1, stage_no

        @block.sync
        def _(sp):
            sp.dma_start(xT[:, :, :], x_in).then_inc(const_in, 16)
            sp.dma_start(cst[:, :], cst_in).then_inc(const_in, 16)
            sp.dma_start(vec[:, :], vec_in).then_inc(const_in, 16)
            sp.dma_start(wv(T + 2048, NMSK), msk_in).then_inc(const_in, 16)
            sp.dma_start(cos_t.bitcast(I32), pos_in).then_inc(const_in, 16)
            for k in range(2):
                sp.dma_start(wraw[:, k, :], w_in[k]).then_inc(raw_in[k], 16)
            with sp.Fori(1, CHUNKS // 2) as j:
                for k in range(2):
                    sp.wait_ge(w_lo, 2 * j + k - 1)
                    sp.dma_start(wraw[:, k, :], w_in[bass.ds(2 * j + k, 1)].rearrange("a p n -> p (a n)")
                                 ).then_inc(raw_in[k], 16)
            sp.wait_ge(stage["dve"], stage_no["dve"])
            sp.dma_start(out, xT[:, :, :]).then_inc(out_done, 16)
            sp.wait_ge(out_done, 16)


_OUTS = [((P, KT, S), "float32")]


def _tiles(m):
    return m.reshape(-1, P, m.shape[1]).transpose(1, 0, 2)


def _stream(a):
    chunks = []

    def put(m):
        t = _tiles(m)
        c = np.zeros((P, CHUNK), np.float32)
        c[:, :t.shape[1] * t.shape[2]] = t.reshape(P, -1)
        chunks.append(c)

    def columns(m, width=256):
        for c in range(0, m.shape[1], width):
            put(m[:, c:c + width])

    w = a["w_in"][0]
    columns(w[:, 0:512])
    q = w[:, 512:1024].reshape(D, 2, 4, 64).transpose(0, 2, 1, 3).reshape(D, 512)
    columns(q)
    kv = w[:, 1024:1792].reshape(D, 6, P)
    put(kv[:, 0:2].reshape(D, 256))
    put(kv[:, [2, 4]].reshape(D, 256))
    put(kv[:, [3, 5]].reshape(D, 256))
    put(np.pad(w[:, 1792:1816], ((0, 0), (0, 232))))
    columns(w[:, 1816:3864])
    nsa_out = a["w_nsa_out"][0].reshape(2, 4, 64, D).transpose(1, 0, 2, 3).reshape(512, D)
    for half in range(2):
        for m in (a["w_pool_out"][0], nsa_out):
            put(m[:, 512 * half:512 * half + 512])
    columns(a["w_out"][0])
    up, down = a["w_up"][0], a["w_down"][0]
    first = 0
    for n in ROUNDS:
        for f in range(first, first + n):
            put(np.concatenate([up[:, f * P:f * P + P], up[:, D_FF + f * P:D_FF + f * P + P]], axis=1))
        columns(down[first * P:(first + n) * P])
        first += n
    for l in range(LAYERS):
        w, br = a["w_in_2"][l], a["w_br_2"][l]
        gate = w[:, 6232:]
        columns(w[:, 1552:2064])
        columns(w[:, 2064:2576])
        columns(w[:, 3088:3600])
        put(np.pad(np.concatenate([w[:, 3600:3664], w[:, 3600:3664], w[:, 3664:3672]], axis=1), ((0, 0), (0, 120))))
        columns(w[:, 2576:3088])
        columns(w[:, 3672:4184])
        columns(gate[:, 1024:2048])
        columns(br[1], 512)
        columns(w[:, 4184:4696])
        columns(w[:, 4696:5208])
        columns(w[:, 5208:5720])
        columns(w[:, 5720:6232])
        columns(gate[:, 2048:3072])
        columns(br[2], 512)
        columns(w[:, 0:256])
        columns(w[:, 256:512])
        columns(w[:, 512:1024])
        put(np.pad(w[:, 1024:1040], ((0, 0), (0, 240))))
        columns(w[:, 1040:1552])
        columns(gate[:, 0:1024])
        columns(br[0], 512)
        columns(a["w_out_2"][l])
    assert len(chunks) == CHUNKS
    return np.stack(chunks)


def _vectors(a):
    v = np.zeros((P, NVEC), np.float32)

    def cols(at, x):
        x = x.reshape(-1, P)
        v[:, at:at + len(x)] = x.T

    def twice(at, x):
        v[:, at] = np.concatenate([x, x])

    cols(V_MIX, a["mix_norm_g"]), cols(V_FFN, a["ffn_norm_g"]), cols(V_N2, a["norm_g_2"])
    cols(V_CONVB, a["conv_b"]), cols(V_CONVW, a["conv_w"]), cols(V_PSCALE, a["pool_scale"])
    twice(V_QG, a["q_norm_g"][0])
    for i in range(3):
        twice(V_KG + i, a["k_norm_g"][0, i])
    for kv in range(2):
        for t in range(32):
            twice(V_PE + 32 * kv + t, a["cmp_pe"][0, kv, t])
    cols(V_GLA, a["gla_norm_g_2"]), cols(V_DQ, a["dsa_qn_g_2"]), cols(V_DK, a["dsa_kn_g_2"])
    for l in range(LAYERS):
        twice(V_CQ + l, a["diff_qn_g_2"][l])
        twice(V_CK + l, a["diff_kn_g_2"][l])
        for i, name in enumerate(("diff_lq1_2", "diff_lk1_2", "diff_lq2_2", "diff_lk2_2")):
            v[0:64, V_LAM + 4 * l + i] = a[name][l]
    return v


def _constants():
    c = np.zeros((P, NCST), np.float32)
    p = np.arange(P)
    c[:, C_ID:C_ID + P] = np.eye(P)
    c[:, C_BLK:C_BLK + P] = p[:, None] // 64 == p[None, :] // 64
    c[:, C_ONE:C_ONE + P] = 1
    d = p % 64
    partner = np.where(d < ROT // 2, p + ROT // 2, np.where(d < ROT, p - ROT // 2, -1))
    c[:, C_PERM:C_PERM + P] = p[:, None] == partner[None, :]
    c[:, C_SUF:C_SUF + P] = (p[:, None] > p[None, :]) & (p[:, None] // CH == p[None, :] // CH)
    c[:, C_IND:C_IND + 2] = p[:, None] // CH == np.arange(2)
    for g, w in enumerate(WINDOWS):
        c[:, C_CNT + 16 * g:C_CNT + 16 * g + 16] = np.float32(1) / np.minimum(np.arange(16) + 1, w).astype(np.float32)
    inv = THETA ** (-np.arange(ROT // 2) * 2.0 / ROT)
    c[:, C_INVF] = np.where(d < ROT, inv[d % (ROT // 2)], 0)
    c[:, C_SGN] = np.where(d < ROT // 2, -1, np.where(d < ROT, 1, 0))
    c[:, C_VALID] = p >= 2 * CMP_STRIDE - 1
    c[:, C_EPS] = EPS
    c[:, C_ONES1] = 1
    c[0:64, C_E64 + 14] = c[64:128, C_E64 + 15] = c[:, C_E128 + 7] = 1
    c[0:8, C_S128:C_S128 + 8] = np.eye(8) * P ** -0.5
    for l in range(LAYERS):
        init = 0.8 - 0.6 * np.exp(-0.3 * l)
        c[:, C_LINIT + l], c[:, C_1ML + l] = init, 1.0 - init
    m = np.zeros((P, NMSK), np.float32)
    m[:, M_ID:M_ID + P] = np.eye(P)
    m[:, M_TRI:M_TRI + P] = np.where(p[None, :] <= p[:, None], 0, NEG)
    m[:, M_CH:M_CH + P] = np.where(p[None, :] // CH <= p[:, None] // CH, 0, NEG)
    for i in range(QT):
        end = np.arange(32) * CMP_STRIDE + 2 * CMP_STRIDE - 1
        seen = (end[None, :] <= p[:, None] + P * i) & (np.arange(32) < N_CMP)[None, :]
        m[:, M_CMP + 32 * i:M_CMP + 32 * i + 32] = np.where(seen, 0, NEG)
    heads = np.repeat(np.eye(16), 64, axis=1).astype(np.float32)
    is_key = np.zeros((2, 8, P), np.float32)
    is_key[0, [0, 1, 6]] = is_key[1, 4:8] = 1
    spread = heads * np.where(is_key == 1, 0.125, 1).reshape(2, 1, 8 * P)
    return c, m, spread.astype(np.float32)


def kernel(**inputs):
    import concourse.bacc as bacc
    from concourse.bass_utils import run_bass_kernel_spmd

    a = {k: np.asarray(v) for k, v in inputs.items()}
    cst, msk, spread = _constants()
    w1 = a["cmp_w1"][0].transpose(0, 2, 1, 3)
    w2 = a["cmp_w2"][0].transpose(1, 0, 2)
    wa2 = np.zeros((P, LAYERS, 256), np.float32)
    wa2[0:16] = a["gla_wa2_2"].transpose(1, 0, 2)
    wa2[16] = a["gla_ba_2"]
    arrays = {
        "x_t": np.ascontiguousarray(a["x"][0].T.reshape(KT, P, S).transpose(1, 0, 2)),
        "positions": np.ascontiguousarray(np.broadcast_to(a["positions"][0].astype(np.int32), (P, S))),
        "weights": _stream(a),
        "vectors": _vectors(a),
        "constants": cst,
        "masks": msk,
        "cmp_w1": np.ascontiguousarray(np.concatenate([w1, w1], axis=1)),
        "small": np.ascontiguousarray(np.concatenate([
            a["pool_w"][0].transpose(1, 0, 2).reshape(P, 4 * P), np.concatenate([w2, w2], axis=2).reshape(P, 2 * P),
            wa2.reshape(P, LAYERS * 256)], axis=1)),
        "spread": spread,
    }
    nc = bacc.Bacc("TRN2", target_bir_lowering=False, num_devices=1)
    args = [nc.dram_tensor(name, v.shape, mybir.dt.from_np(v.dtype), kind="ExternalInput").ap()
            for name, v in arrays.items()]
    args.append(nc.dram_tensor("out_t", (P, KT, S), F32, kind="ExternalOutput").ap())
    two_block_kernel(nc, *args)
    r = run_bass_kernel_spmd(nc, [arrays], core_ids=[0])
    y = r.results[0]["out_t"]
    return np.ascontiguousarray(y.transpose(1, 0, 2).reshape(D, S).T)[None]
```

```python
from contextlib import ExitStack

import numpy as np

import concourse.bass as bass
from concourse import mybir

F32 = mybir.dt.float32
F32R = mybir.dt.float32r
BF16 = mybir.dt.bfloat16
I32 = mybir.dt.int32
ALU = mybir.AluOpType
ACT = mybir.ActivationFunctionType
AX = mybir.AxisListType

P = 128
S = 512
D = 1024
KT = D // P
QT = S // P
EPS = 1e-6
NEG = -1e30
ROT = 16
THETA = 500000.0
N_CMP = 31
CMP_STRIDE = 16
WINDOWS = (2, 4, 8, 16)
D_FF = 2816
FF_TILES = D_FF // P
ROUNDS = (8, 8, 6)
TOPK = 128
CH = 64
LAYERS = 2
CHUNK = 2048
OFF = (0, 128, 384, 768)
TRI = 1280
KOFF = (0, 512, 896, 1152)

V_MIX, V_FFN, V_N2 = 0, 8, 16
V_CONVB, V_CONVW = 32, 54
V_PSCALE = 120
V_QG, V_KG = 124, 125
V_PE = 128
V_GLA, V_DQ, V_DK, V_CQ, V_CK = 192, 194, 196, 198, 200
V_LAM = 202
NVEC = 210
C_ID, C_ONE, C_PERM, C_SUF = 0, 128, 256, 384
C_IND = 512
C_CNT = 514
C_INVF, C_SGN, C_VALID, C_EPS, C_ONES1 = 578, 579, 580, 581, 582
C_LINIT, C_1ML = 584, 586
C_E64, C_E128 = 588, 618
C_S128 = 633
NCST = 641
M_ID, M_TRI, M_CH, M_CMP = 0, 128, 256, 384
NMSK = 512

TWO_PI = 2 * np.pi
PI_HI = float(np.float32(201 / 32))
PI_MID = float(np.float32(np.floor((TWO_PI - 201 / 32) * 2**20) / 2**20))
PI_LO = float(np.float32(TWO_PI - 201 / 32 - np.floor((TWO_PI - 201 / 32) * 2**20) / 2**20))
ROUND = float(1.5 * 2**23)
TAKEN = -3e38


BLOCK1 = [("u", 2, 2), ("q", 2, 2), ("cmp", 1, 2), ("ksw", 1, 2), ("vsw", 1, 4), ("nsag", 1, 4),
          ("mg", 8, 2), ("merge1", 4, 4), ("wout", 4, 2),
          ("up0", 8, 2), ("down0", 4, 2), ("up1", 8, 2), ("down1", 4, 2), ("up2", 6, 2), ("down2", 4, 2)]
BLOCK2 = [("bq", 2, 2), ("bk", 2, 2), ("iq", 2, 2), ("ik", 1, 1), ("bv", 2, 4),
          ("bgate", 4, 2), ("bz", 2, 2), ("bbr", 2, 4),
          ("cq", 2, 2), ("ck", 2, 2), ("cv", 2, 4),
          ("cz", 2, 2), ("cgate", 4, 2), ("cbr", 2, 4),
          ("ga", 1, 1), ("gk", 1, 4), ("gv", 2, 4), ("gq", 1, 2), ("gz", 2, 2), ("agate", 4, 2), ("abr", 2, 4),
          ("wout2", 4, 2)]


def positions(sections):
    at, c, t = {}, 0, 0
    for name, n, per in sections:
        at[name] = (c, n, t, per)
        c += n
        t += n * per
    return at, c, t


POS1, CHUNKS1, TILES1 = positions(BLOCK1)
POS2, CHUNKS2, TILES2 = positions(BLOCK2)
CHUNKS = CHUNKS1 + LAYERS * CHUNKS2
assert CHUNKS1 % 2 == 0 and CHUNKS2 % 2 == 0 and TILES1 % 2 == 0 and TILES2 % 2 == 0


def section(name, l=None):
    if l is None:
        return POS1[name]
    c, n, t, per = POS2[name]
    return CHUNKS1 + CHUNKS2 * l + c, n, TILES1 + TILES2 * l + t, per


def two_block_kernel(nc, x_in, pos_in, w_in, vec_in, cst_in, msk_in, cmpw_in, small_in, spread_in, out):
    with ExitStack() as ctx:
        def sb(name, shape, dt):
            return ctx.enter_context(nc.sbuf_tensor(name, shape, dt))

        def sem(name):
            return ctx.enter_context(nc.semaphore(name))

        xT = sb("xT", [P, KT, S], F32)
        hhi, hlo = sb("hhi", [P, KT, S], F32R), sb("hlo", [P, KT, S], F32R)
        wraw = sb("wraw", [P, 2, CHUNK], F32)
        whi, wlo = sb("whi", [P, 2, CHUNK], F32R), sb("wlo", [P, 2, CHUNK], F32R)
        vec, cst, msk = sb("vec", [P, NVEC], F32), sb("cst", [P, NCST], F32), sb("msk", [P, NMSK], BF16)
        stat = sb("stat", [P, 64], F32)
        work = sb("work", [P, 15360], F32)
        split = sb("split", [P, 11328], F32R)

        pp = [ctx.enter_context(nc.psum_tensor(f"pp{i}", [P, S], F32)) for i in range(2)]
        ps = [ctx.enter_context(nc.psum_tensor(f"ps{i}", [P, S], F32)) for i in range(2)]
        pt = [ctx.enter_context(nc.psum_tensor(f"pt{i}", [P, S], F32)) for i in range(2)]
        po = [ctx.enter_context(nc.psum_tensor(f"po{i}", [P, S], F32)) for i in range(2)]

        def wv(at, *dims):
            n = int(np.prod(dims))
            v = work[:, at:at + n]
            if len(dims) == 2:
                v = v.rearrange("p (a b) -> p a b", a=dims[0])
            elif len(dims) == 3:
                v = v.rearrange("p (a b c) -> p a b c", a=dims[0], b=dims[1])
            return v

        def rv(at, *dims):
            n = int(np.prod(dims))
            v = split[:, at:at + n]
            if len(dims) == 2:
                v = v.rearrange("p (a b) -> p a b", a=dims[0])
            elif len(dims) == 3:
                v = v.rearrange("p (a b c) -> p a b c", a=dims[0], b=dims[1])
            return v

        def col(c, n=1):
            return vec[:, c:c + n]

        def con(c, n=1):
            return cst[:, c:c + n]

        ident, ones, perm, suf = (con(c, P) for c in (C_ID, C_ONE, C_PERM, C_SUF))
        idb = msk[:, M_ID:M_ID + P]

        raw_in = [sem(f"raw_in{i}") for i in range(2)]
        w_hi, w_lo = sem("w_hi"), sem("w_lo")
        mm_done = sem("mm_done")
        evac = sem("evac")
        const_in = sem("const_in")
        stage = {e: sem(f"stage_{e}") for e in ("pe", "act", "dve", "pool")}
        sq_ready, ss_done, root_ready = sem("sq_ready"), sem("ss_done"), sem("root_ready")
        nrm_ready, nrm_hi = sem("nrm_ready"), sem("nrm_hi")
        inv_ready, inv_spread = sem("inv_ready"), sem("inv_spread")
        h_even, h_odd = sem("h_even"), sem("h_odd")
        hn_sq, hn_ss, hn_root, hn_out = sem("hn_sq"), sem("hn_ss"), sem("hn_root"), sem("hn_out")
        hn_fin = sem("hn_fin")
        hn_inv, hn_bc, spread_in_sb = sem("hn_inv"), sem("hn_bc"), sem("spread_in_sb")
        hn_perm, hn_rope = sem("hn_perm"), sem("hn_rope")
        post = sem("post")
        rope_red, rope_sin = sem("rope_red"), sem("rope_sin")
        cmp_in, blk_ready, hid_done, hid_out = sem("cmp_in"), sem("blk_ready"), sem("hid_done"), sem("hid_out")
        kvc_done = sem("kvc_done")
        sc_ready, mx_ready, ex_done = sem("sc_ready"), sem("mx_ready"), sem("ex_done")
        diag_ready = sem("diag_ready")
        tr_done, pt_hi, pt_lo, pv_done = sem("tr_done"), sem("pt_hi"), sem("pt_lo"), sem("pv_done")
        o_out, ring_in, v_in = sem("o_out"), sem("ring_in"), sem("v_in")
        cs_ready, cs_sub, cs_exp, cs_p = sem("cs_ready"), sem("cs_sub"), sem("cs_exp"), sem("cs_p")
        ct_done, ct_out = sem("ct_done"), sem("ct_out")
        pool_in, pool_mm, poolw_in = sem("pool_in"), sem("pool_mm"), sem("poolw_in")
        part_hi = sem("part_hi")
        ff_conv, ff_sig, ff_prod, ff_hi = sem("ff_conv"), sem("ff_sig"), sem("ff_prod"), sem("ff_hi")
        ff_lo = sem("ff_lo")
        iw_turned = sem("iw_turned")
        ix_parts, ix_done, ix_relu = sem("ix_parts"), sem("ix_done"), sem("ix_relu")
        z_ready, x_ready = sem("z_ready"), sem("x_ready")
        y_ready, y_lo, m_lo = sem("y_ready"), sem("y_lo"), sem("m_lo")
        lam_in, lam_sum, lam_exp = sem("lam_in"), sem("lam_sum"), sem("lam_exp")
        o_done, pool_out = sem("o_done"), sem("pool_out")
        alr_out = sem("alr_out")
        wa2_in, z_done, g_exp, g_la = sem("wa2_in"), sem("z_done"), sem("g_exp"), sem("g_la")
        suf_done, decayed, kdec_ready = sem("suf_done"), sem("decayed"), sem("kdec_ready")
        u_done, state_ready, gla_o = sem("u_done"), sem("state_ready"), sem("gla_o")
        out_done = sem("out_done")

        stage_no = {e: 0 for e in stage}
        block = ctx.enter_context(nc.Block())

        def stage_end(eng, me):
            eng.drain().then_inc(stage[me], 1)
            stage_no[me] += 1
            for other in stage:
                if other != me:
                    eng.wait_ge(stage[other], stage_no[me])

        def pairs(eng, n, body, peel=False):
            if peel:
                for j in range(n):
                    body(j)
            elif n >= 2:
                with eng.Fori(0, n) as j:
                    body(j)
            else:
                body(0)

        def act_conv(act, c, slot):
            act.wait_ge(raw_in[slot], (c - slot) * 8 + 16)
            nc.scalar.activation(whi[:, slot, :], wraw[:, slot, :], ACT.Copy).then_inc(w_hi, 1)

        def dve_conv(dve, c, slot):
            dve.wait_ge(w_hi, c + 1)
            nc.vector.tensor_tensor(wlo[:, slot, :], wraw[:, slot, :], whi[:, slot, :].bitcast(F32),
                                    ALU.subtract).then_inc(w_lo, 1)

        def three(out_ap, a, b, start, stop):
            (ah, al), (bh, bl) = a, b
            nc.tensor.matmul(out_ap, ah, bh, start=start, stop=False)
            nc.tensor.matmul(out_ap, ah, bl, start=False, stop=False)
            return nc.tensor.matmul(out_ap, al, bh, start=False, stop=stop)

        def weights(slot, kt, cols):
            return [w[:, slot, 0:kt * cols].rearrange("p (k n) -> p k n", k=kt) for w in (whi, wlo)]

        def pe_tile(pe, t, par, product):
            if not (isinstance(t, int) and t < 2):
                pe.wait_ge(evac, t - 1)
            product(pp[par]).then_inc(mm_done, 1)

        def pe_fm(pe, name, l, h, kt, cols, ready=None, last_late=False, only=None):
            c0, n, t0, per = section(name, l)
            par0, slot0 = par_of(name, l)

            def body(j):
                for k in range(min(2, n)):
                    slot = (slot0 + k) % 2
                    c = c0 + 2 * j + k
                    pe.wait_ge(w_lo, c + 1)
                    wh, wl = weights(slot, kt, cols)
                    if last_late:
                        t = t0 + (2 * j + k) * per
                        for x0, x1 in ((0, kt - 1), (kt - 1, kt)):
                            for m in range(per):
                                if x0 == 0:
                                    pe.wait_ge(evac, t + m - 1)
                                for x in range(x0, x1):
                                    if k == 0 and m == 0:
                                        ready(x)
                                    cc = slice(m * P, m * P + P)
                                    last = three(pp[(par0 + k * per + m) % 2][:, :], (wh[:, x, cc], wl[:, x, cc]),
                                                 (h[0][:, x, :], h[1][:, x, :]), x == 0, x == kt - 1)
                                if x1 == kt:
                                    last.then_inc(mm_done, 1)
                        continue
                    for m in range(per):
                        t = t0 + (2 * j + k) * per + m

                        def product(bank):
                            for x in range(kt):
                                if ready is not None and k == 0 and m == 0:
                                    ready(x)
                                cc = slice(m * P, m * P + P)
                                last = three(bank[:, :], (wh[:, x, cc], wl[:, x, cc]),
                                             (h[0][:, x, :], h[1][:, x, :]), x == 0, x == kt - 1)
                            return last
                        pe_tile(pe, t, (par0 + k * per + m) % 2, product)
            if only is not None:
                body(only)
            else:
                pairs(pe, max(1, n // 2), body)

        def pe_tm(pe, name, l, cols):
            c0, n, t0, per = section(name, l)
            par0, slot0 = par_of(name, l)
            for k in range(n):
                slot = (slot0 + k) % 2
                pe.wait_ge(w_lo, c0 + k + 1)
                wh, wl = weights(slot, KT, 256)
                for i in range(QT):
                    def product(bank):
                        for x in range(KT):
                            tt = slice(i * P, i * P + P)
                            last = three(bank[:, 0:cols], (hhi[:, x, tt], hlo[:, x, tt]),
                                         (wh[:, x, 0:cols], wl[:, x, 0:cols]), x == 0, x == KT - 1)
                        return last
                    pe_tile(pe, t0 + k * per + i, (par0 + k * per + i) % 2, product)

        def pe_tile_part(pe, name, l, n, part, parts):
            c0, _, t0, per = section(name, l)
            par0, slot0 = par_of(name, l)
            k, m = n // per, n % per
            if part == 0:
                pe.wait_ge(w_lo, c0 + k + 1)
                pe.wait_ge(evac, t0 + n - 1)
            wh, wl = weights((slot0 + k) % 2, KT, 256)
            size = KT // parts
            cc = slice(m * P, m * P + P)
            for x in range(part * size, part * size + size):
                last = three(pp[(par0 + n) % 2][:, :], (wh[:, x, cc], wl[:, x, cc]), (hhi[:, x, :], hlo[:, x, :]),
                             x == 0, x == KT - 1)
            if part == parts - 1:
                last.then_inc(mm_done, 1)

        def par_of(name, l):
            c, _, t, _ = (POS1 if l is None else POS2)[name]
            return t % 2, c % 2

        def act_tiles(act, name, l, evacuate, only=None):
            c0, n, t0, per = section(name, l)
            par0, slot0 = par_of(name, l)

            def body(j):
                for k in range(min(2, n)):
                    for m in range(per):
                        t = t0 + (2 * j + k) * per + m
                        act.wait_ge(mm_done, t + 1)
                        evacuate(pp[(par0 + k * per + m) % 2], (2 * j + k) * per + m, m).then_inc(evac, 1)
                    act_next(act, name, l, c0 + 2 * j + k, (slot0 + k) % 2)
            if only is not None:
                body(only)
            else:
                pairs(act, max(1, n // 2), body, peel=is_last(name, l))

        def is_last(name, l):
            return name == "wout2" and l == LAYERS - 1

        def act_next(act, name, l, c, slot):
            if not is_last(name, l) or c + 2 < CHUNKS:
                act_conv(act, c + 2, slot)

        def dve_next(dve, name, l, after=None):
            c0, n, t0, per = section(name, l)
            _, slot0 = par_of(name, l)

            def body(j):
                for k in range(min(2, n)):
                    if not is_last(name, l) or c0 + 2 * j + k + 2 < CHUNKS:
                        dve_conv(dve, c0 + 2 * j + k + 2, (slot0 + k) % 2)
                    if after is not None:
                        for m in range(per):
                            after((2 * j + k) * per + m, t0 + (2 * j + k) * per + m)
            pairs(dve, max(1, n // 2), body, peel=is_last(name, l))

        T_SQ, T_RR, T_T = 0, 1024, 2048

        def act_norm(act, n):
            for k in range(KT):
                if n >= 1:
                    act.wait_ge(x_ready, KT * ((0, 0, 3, 4)[n]) + k + 1)
                if k >= 2:
                    act.wait_ge(ss_done, KT * n + k - 1)
                nc.scalar.activation(wv(T_SQ + 512 * (k % 2), 512), xT[:, k, :], ACT.Square).then_inc(sq_ready, 1)
            act.wait_ge(ss_done, KT * n + KT)
            nc.scalar.activation(stat[:, 40:44], ps[0][:, 0:QT], ACT.Sqrt, scale=1.0 / D,
                                 bias=con(C_EPS)).then_inc(root_ready, 1)
            for k in range(KT):
                act.wait_ge(nrm_ready, KT * n + k + 1)
                nc.scalar.activation(hhi[:, k, :], wv(T_T + 512 * k, 512), ACT.Copy).then_inc(nrm_hi, 1)

        def pe_norm(pe, n):
            for k in range(KT):
                pe.wait_ge(sq_ready, KT * n + k + 1)
                for i in range(QT):
                    last = nc.tensor.matmul(ps[0][:, i:i + 1], wv(T_SQ + 512 * (k % 2) + P * i, P), ones[:, 0:1],
                                            start=(k == 0 and i == 0), stop=(k == KT - 1 and i == QT - 1))
                last.then_inc(ss_done, 1)
            pe.wait_ge(inv_ready, n + 1)
            for i in range(QT):
                last = nc.tensor.matmul(ps[1][:, i * P:i * P + P], ones, wv(T_RR + P * i, P), start=True, stop=True)
            last.then_inc(inv_spread, 1)

        def inverse_root(dve, inv, root, squares, dim):
            nc.vector.reciprocal(inv, root)
            dve.drain()
            nc.vector.scalar_tensor_tensor(out=root, in0=inv, scalar=-0.5 / dim, in1=inv, op0=ALU.mult, op1=ALU.mult)
            dve.drain()
            nc.vector.scalar_tensor_tensor(out=root, in0=squares, scalar=EPS * dim, in1=root, op0=ALU.add, op1=ALU.mult)
            dve.drain()
            nc.vector.scalar_tensor_tensor(out=inv, in0=root, scalar=1.5, in1=inv, op0=ALU.add, op1=ALU.mult)
            dve.drain()

        def dve_norm(dve, n, gain):
            dve.drain()
            dve.wait_ge(root_ready, n + 1)
            inverse_root(dve, stat[:, 44:48], stat[:, 40:44], ps[0][:, 0:QT], D)
            make_diag(wv(T_RR, QT, P), stat[:, 44:48]).then_inc(inv_ready, 1)
            dve.wait_ge(inv_spread, n + 1)
            for k in range(KT + 2):
                if k < KT:
                    nc.vector.scalar_tensor_tensor(out=wv(T_T + 512 * k, 512), in0=xT[:, k, :], scalar=gain(k),
                                                   in1=ps[1][:, :], op0=ALU.mult, op1=ALU.mult).then_inc(nrm_ready, 1)
                if k >= 2 and k % 2:
                    j = k - 2
                    dve.wait_ge(nrm_hi, KT * n + j + 1)
                    nc.vector.tensor_tensor(hlo[:, j, :], wv(T_T + 512 * j, 512), hhi[:, j, :].bitcast(F32),
                                            ALU.subtract).then_inc(h_odd, 1)

        def pool_norm(pool, n):
            for k in range(0, KT, 2):
                pool.wait_ge(nrm_hi, KT * n + k + 1)
                nc.gpsimd.tensor_tensor(hlo[:, k, :], wv(T_T + 512 * k, 512), hhi[:, k, :].bitcast(F32),
                                        ALU.subtract).then_inc(h_even, 1)

        def h_ready(pe, n):
            return lambda x: pe.wait_ge(h_odd if x % 2 else h_even, KT // 2 * n + x // 2 + 1)

        def scale_order(items):
            return (0, 4, 1, 5, 2, 6, 3, 7) if len(items) == 8 else range(len(items))

        def act_squares(act, base, items, sq, bufs, first=0):
            act.drain()
            for s in range(first, len(items)):
                src, width = items[s][0:2]
                if s >= bufs:
                    act.wait_ge(hn_ss, base + s - bufs + 1)
                nc.scalar.activation(wv(sq + 512 * (s % bufs), 512)[:, 0:width], src, ACT.Square).then_inc(hn_sq, 1)

        def act_roots(act, base, items, root):
            dim = items[0][3]
            rows = 8 * P // dim
            act.wait_ge(hn_ss, base + len(items))
            nc.scalar.activation(wv(root, 512)[0:rows, :], po[1][0:rows, :], ACT.Sqrt, scale=1.0 / dim,
                                 bias=con(C_EPS)[0:rows, :]).then_inc(hn_root, 1)

        def act_spread(act, call, at):
            act.dma_start(wv(at, 8 * P)[0:16, :], spread_in[min(call, 1)]).then_inc(spread_in_sb, 16)

        def act_hn(act, base, call, items, sq, root):
            if items[0][3] == 64:
                act_spread(act, call, root + 1536)
            act_squares(act, base, items, sq, 2)
            act_roots(act, base, items, root)

        def pe_sums(pe, base, items, sq, bufs):
            for s, (_, width, _, dim, _, _) in enumerate(items):
                pe.wait_ge(hn_sq, base + s + 1)
                pick = con(C_E64 + 14 - 2 * s, 16) if dim == 64 else con(C_E128 + 7 - s, 8)
                nc.tensor.matmul(po[1][0:pick.shape[1], 0:width], pick, wv(sq + 512 * (s % bufs), 512)[:, 0:width],
                                 start=(s == 0), stop=(s == len(items) - 1)).then_inc(hn_ss, 1)

        def pe_spread(pe, base, call, rbase, items, inv, spread_at):
            pe.wait_ge(hn_inv, call + 1)
            if items[0][3] == 64:
                pe.wait_ge(spread_in_sb, 16 * (1 + (call + 2) // 4))
            r = 0
            for s in range(len(items) + 1):
                if s < len(items):
                    item = scale_order(items)[s]
                    _, width, _, dim, _, spread = items[item]
                    if s >= 2:
                        pe.wait_ge(hn_out, base + s - 1)
                    if dim == 64:
                        rows, lhs = 16, wv(spread_at + item * P, P)[0:16, :]
                    else:
                        rows, lhs = 8, con(spread + item)[0:8, :].broadcast_to([8, P])
                    nc.tensor.matmul(ps[s % 2][:, 0:width], lhs, wv(inv, 512)[0:rows, 0:width], start=True,
                                     stop=True).then_inc(hn_bc, 1)
                if s >= 1:
                    src, width, _, _, tables, _ = items[s - 1]
                    if tables is not None:
                        pe.wait_ge(hn_out, base + s)
                        if r >= 2:
                            pe.wait_ge(hn_rope, rbase + r - 1)
                        nc.tensor.matmul(pt[r % 2][:, 0:width], perm, src, start=True, stop=True).then_inc(hn_perm, 1)
                        r += 1

        def pe_hn(pe, base, call, rbase, items, sq, inv):
            pe_sums(pe, base, items, sq, 2)
            pe_spread(pe, base, call, rbase, items, inv, inv + 1024)

        def dve_inverse(dve, call, items, root, inv):
            dim = items[0][3]
            rows = 8 * P // dim
            dve.wait_ge(hn_root, call + 1)
            inverse_root(dve, wv(inv, 512)[0:rows, :], wv(root, 512)[0:rows, :], po[1][0:rows, :], dim)
            dve.drain().then_inc(hn_inv, 1)

        def dve_scale(dve, base, rbase, items, tmp):
            def rotate(s):
                src, width, _, _, (cos, sin), _ = items[s]
                t2 = wv(tmp, 512)[:, 0:width]
                dve.wait_ge(hn_perm, rbase + s + 1)
                nc.vector.tensor_tensor(t2, pt[s % 2][:, 0:width], sin, ALU.mult).then_inc(hn_rope, 1)
                nc.vector.tensor_tensor(src, src, cos, ALU.mult)
                dve.drain()
                nc.vector.tensor_tensor(src, src, t2, ALU.add)
                dve.drain().then_inc(hn_fin, 1)
            for s, item in enumerate(scale_order(items)):
                src, width, gain, _, tables, _ = items[item]
                dve.wait_ge(hn_bc, base + s + 1)
                nc.vector.scalar_tensor_tensor(out=src, in0=src, scalar=gain, in1=ps[s % 2][:, 0:width], op0=ALU.mult,
                                               op1=ALU.mult).then_inc(hn_out, 1)
                if tables is not None and s >= 1:
                    rotate(s - 1)
            if items[-1][4] is not None:
                rotate(len(items) - 1)

        def dve_hn(dve, base, call, rbase, items, root, inv, tmp):
            dve_inverse(dve, call, items, root, inv)
            dve_scale(dve, base, rbase, items, tmp)

        u_f, q_f, kcv_f, ksw_f = wv(0, 4, S), wv(2048, 4, S), wv(4096, 2, S), wv(5120, 2, S)
        v_f, g_f = wv(6144, 4, 256), wv(7168, 4, 24)
        kc_f, vc_f = wv(7264, 32), wv(7296, P)
        cos_t, sin_t = wv(7424, S), wv(7936, S)
        T = 8448
        w1_f = wv(T, 32, P)
        blk_f = [wv(T + 4096 + 992 * kv, 16, 2 * N_CMP) for kv in range(2)]
        hid_f = [wv(T + 6080 + 64 * kv, 64) for kv in range(2)]
        cw2 = wv(T + 6208, 2, P)
        cp_f, ct_f = wv(T, 4, 32), wv(T + 128, S)
        poolw = wv(T + 2048, 4, P)
        mg_f, br_f = wv(4096, 16, S), wv(12288, 2, S)
        prod_f = wv(4096, KT, S)
        gp_f, vl_f, dn_f = wv(0, KT, S), wv(4096, KT, S), wv(8192, KT, S)
        cv_f, sg_f = wv(12288, 2, S), wv(13312, 2, S)
        pt_r = [[rv(2560 * b + TRI * y, TRI) for y in range(2)] for b in range(2)]
        qr = [[rv(5120 + 1024 * b + 512 * y, 512) for y in range(2)] for b in range(2)]
        kr = [[rv(7168 + 1024 * b + 512 * y, 512) for y in range(2)] for b in range(2)]
        vr = [[rv(9216 + 1024 * b + 512 * y, 4, P) for y in range(2)] for b in range(2)]
        kcr = [rv(11264 + 32 * y, 32) for y in range(2)]
        yr = [rv(0, 4, S), rv(2048, 4, S)]
        yr2 = [rv(4096, 4, S), rv(6144, 4, S)]
        mr = [rv(0, KT, S), rv(4096, KT, S)]
        merged = wv(0, KT, S)
        a_f, b_f = wv(4096, 4, S), wv(6144, 4, S)
        c_f = wv(8192, 4, S)
        iq_f, ik_f, iw_f = wv(10240, 4, S), wv(12288, S), wv(14464, 4, 8)
        iwt_f = wv(14496, S)
        sc_f = [None, wv(12288, 256), wv(12544, 384), wv(12928, S)]
        selm = wv(13824, 640).bitcast(BF16)
        relu_f = [wv(10240 + 512 * b, S) for b in range(2)]
        iqr = [rv(2048 * y, 4, S) for y in range(2)]
        ikr = [rv(4096 + 512 * y, 512) for y in range(2)]
        z_f, gate_f, br2_f = wv(6144, 4, S), wv(8192, KT, S), wv(12288, 2, S)
        gq_f, gk_f, gv_f = wv(6144, 2, S), wv(7168, 4, 256), wv(8192, 4, S)
        alr_f, za_f, la_f, kd_f = wv(10240, S), wv(10752, 4, 256), wv(11776, 4, 256), wv(12800, 4, 256)
        st_f = [wv(13824 + 512 * b, 2, 256) for b in range(2)]
        dec_f, wa2_f = wv(14848, 2, 8), wv(14880, 256)
        nmx = [stat[:, 4 * b:4 * b + 4] for b in range(2)]
        rsum = [stat[:, 8 + 4 * b:12 + 4 * b] for b in range(2)]
        rcp = [stat[:, 16 + 4 * b:20 + 4 * b] for b in range(2)]
        cstat, lam = stat[:, 24:32], stat[:, 32:40]

        def p_of(base, b):
            return wv(base + TRI * b, TRI)

        P1, P_DSA, P_DIFF = 12800, 10240, 10240
        diag1, diag_dsa = ([wv(at + 512 * b, QT, P) for b in range(2)] for at in (10240, 12800))
        diag_diff = [b_f[:, c, :].rearrange("p (i n) -> p i n", i=QT) for c in range(2)]

        h = (hhi, hlo)

        def pe_scores(pe, u, i, q, k, rows, mask):
            w = P * (i + 1)
            if 4 * u + i >= 2:
                pe.wait_ge(ex_done, 4 * u + i - 1)
            bank = ps[i % 2]
            three(bank[:, 0:w], [x[rows, i * P:i * P + P] for x in q], [x[rows, 0:w] for x in k], True, False)
            at, mk = mask(i)
            nc.tensor.matmul(bank[:, at:w], idb, mk, start=False, stop=True).then_inc(sc_ready, 1)

        def dve_max(dve, u, i):
            dve.wait_ge(sc_ready, 4 * u + i + 1)
            nc.vector.tensor_reduce(nmx[u % 2][:, i:i + 1], ps[i % 2][:, 0:P * (i + 1)], AX.X, ALU.max,
                                    negate=True).then_inc(mx_ready, 1)

        def act_exp(act, u, i, dst):
            w = P * (i + 1)
            act.wait_ge(mx_ready, 4 * u + i + 1)
            nc.scalar.activation(dst[:, OFF[i]:OFF[i] + w], ps[i % 2][:, 0:w], ACT.Exp, bias=nmx[u % 2][:, i:i + 1],
                                 accum_out=rsum[u % 2][:, i:i + 1]).then_inc(ex_done, 1)

        def pe_transpose(pe, v, kb, exps, diags):
            if kb == 0:
                pe.wait_ge(diag_ready, v + 1)
            if 4 * v + kb >= 2:
                pe.wait_ge(pt_lo, 4 * v + kb - 1)
            for i in range(kb, QT):
                for n, (src, diag) in enumerate(zip(exps, diags)):
                    last = nc.tensor.matmul(pt[kb % 2][:, (i - kb) * P:(i - kb + 1) * P],
                                            src[:, OFF[i] + kb * P:OFF[i] + kb * P + P], diag[:, i, :],
                                            start=(n == 0), stop=(n == len(exps) - 1))
            last.then_inc(tr_done, 1)

        def make_diag(diag, factor):
            return nc.vector.tensor_tensor(diag, ident.unsqueeze(1).broadcast_to([P, QT, P]),
                                           factor.unsqueeze(2).broadcast_to([P, QT, P]), ALU.mult)

        def act_pt(act, v, kb):
            w = S - P * kb
            act.wait_ge(tr_done, 4 * v + kb + 1)
            nc.scalar.activation(pt_r[v % 2][0][:, KOFF[kb]:KOFF[kb] + w], pt[kb % 2][:, 0:w],
                                 ACT.Copy).then_inc(pt_hi, 1)

        def dve_pt(dve, v, kb):
            w = S - P * kb
            dve.wait_ge(pt_hi, 4 * v + kb + 1)
            nc.vector.tensor_tensor(pt_r[v % 2][1][:, KOFF[kb]:KOFF[kb] + w], pt[kb % 2][:, 0:w],
                                    pt_r[v % 2][0][:, KOFF[kb]:KOFF[kb] + w].bitcast(F32),
                                    ALU.subtract).then_inc(pt_lo, 1)

        def pe_pv(pe, v, kb, vals, bank, start, stop):
            pe.wait_ge(pt_lo, 4 * v + kb + 1)
            w = S - P * kb
            last = three(bank[:, kb * P:S], [x[:, kb, :] for x in vals],
                         [x[:, KOFF[kb]:KOFF[kb] + w] for x in pt_r[v % 2]], start, stop)
            if kb == QT - 1:
                last.then_inc(pv_done, 1)

        def split_pool(pool, parts, src):
            nc.gpsimd.tensor_copy(parts[0], src)
            pool.drain()
            return nc.gpsimd.tensor_tensor(parts[1], src, parts[0].bitcast(F32), ALU.subtract)

        def copy_to(dst, func=ACT.Copy, **kw):
            return lambda bank, n, m: nc.scalar.activation(tile(dst, n), bank[:, :], func, **kw)

        def tile(v, n):
            return v[:, n, :] if isinstance(n, int) else v[:, bass.ds(n, 1), :].rearrange("p a s -> p (a s)")

        def gated_add(dve, t0, first, gate, branch, n, par, merged_tile):
            dve.wait_ge(evac, t0 + n + 1)
            if first:
                nc.vector.tensor_tensor(merged_tile, gate, branch[:, par, :], ALU.mult).then_inc(post, 1)
            else:
                nc.vector.tensor_tensor(branch[:, par, :], gate, branch[:, par, :], ALU.mult)
                dve.drain()
                nc.vector.tensor_tensor(merged_tile, merged_tile, branch[:, par, :], ALU.add).then_inc(post, 1)

        def act_branch(act, name, l, post0, branch):
            c0, n, t0, per = section(name, l)
            par0, slot0 = par_of(name, l)
            for k in range(n):
                for m in range(4):
                    tt = 4 * k + m
                    act.wait_ge(mm_done, t0 + tt + 1)
                    if tt >= 2:
                        act.wait_ge(post, post0 + tt - 1)
                    nc.scalar.activation(branch[:, m % 2, :], pp[(par0 + m) % 2][:, :], ACT.Copy).then_inc(evac, 1)
                act_next(act, name, l, c0 + k, (slot0 + k) % 2)

        def pe_branch(pe, name, l, operand, ready):
            c0, n, t0, per = section(name, l)
            par0, slot0 = par_of(name, l)
            for k in range(n):
                pe.wait_ge(w_lo, c0 + k + 1)
                wh, wl = weights((slot0 + k) % 2, 4, 512)
                y = operand(k)
                for m in range(4):
                    def product(bank):
                        for x in range(4):
                            if m == 0:
                                ready(k, x)
                            cc = slice(m * P, m * P + P)
                            last = three(bank[:, :], (wh[:, x, cc], wl[:, x, cc]), (y[0][:, x, :], y[1][:, x, :]),
                                         x == 0, x == 3)
                        return last
                    pe_tile(pe, t0 + 4 * k + m, (par0 + m) % 2, product)

        def dve_add_x(dve, src, n, t):
            dve.wait_ge(evac, t + 1)
            nc.vector.tensor_tensor(tile(xT, n), tile(xT, n), tile(src, n), ALU.add).then_inc(x_ready, 1)

        def y_rows(g):
            return slice(64 * g, 64 * g + 64)

        k_items = [(ksw_f[:, 0, :], S, col(V_KG + 1), 64, (cos_t, sin_t), None),
                   (ksw_f[:, 1, :], S, col(V_KG + 2), 64, (cos_t, sin_t), None)]
        k_items += [(q_f[:, t, :], S, col(V_QG), 64, (cos_t, sin_t), C_ID) for t in range(4)]
        cmp_at = slice(2 * CMP_STRIDE - 1, None, CMP_STRIDE)
        k_items += [(kc_f[:, 0:N_CMP], N_CMP, col(V_KG), 64, (cos_t[:, cmp_at], sin_t[:, cmp_at]), None)]
        HN1 = len(k_items)
        HN_LAYER = 8 + 8 + 4 + 4
        U1 = 16
        FF = [0, 8, 16]

        def causal(i):
            return P * i, msk[:, M_TRI:M_TRI + P]

        def chunked(i):
            return P * i, msk[:, M_CH:M_CH + P]

        def selected(i):
            return (0, selm[:, OFF[i]:OFF[i] + P * (i + 1)]) if i else (0, msk[:, M_CH:M_CH + P])

        def layer_items(l):
            dsa = [(a_f[:, t, :], S, col(V_DQ + l), P, None, C_ID) for t in range(4)]
            dsa += [(b_f[:, t, :], S, col(V_DK + l), P, None, C_S128) for t in range(4)]
            diff = [(a_f[:, t, :], S, col(V_CQ + l), 64, None, C_ID) for t in range(4)]
            diff += [(b_f[:, t, :], S, col(V_CK + l), 64, None, None) for t in range(4)]
            diff_o = [(a_f[:, t, :], S, con(C_1ML + l), P, None, C_ID) for t in range(4)]
            gla_o_ = [(a_f[:, t, :], S, col(V_GLA + l), P, None, C_ID) for t in range(4)]
            return dsa, diff, diff_o, gla_o_

        def y_parts(pe, n):
            return lambda k, x: pe.wait_ge(y_lo, 8 + 4 * n + x + 1)

        def pe_layer(pe, l):
            dsa, diff, diff_out, gla_out = layer_items(l)
            hb = HN1 + HN_LAYER * l
            pe_norm(pe, 2 + l)
            for name in ("bq", "bk", "iq"):
                pe_fm(pe, name, l, h, KT, 256, h_ready(pe, 2 + l) if name == "bq" else None)
            pe_sums(pe, hb, dsa, 0, 8)
            c0, n, t0, per = section("ik", l)
            par0, slot0 = par_of("ik", l)
            pe.wait_ge(w_lo, c0 + 1)
            wh, wl = weights(slot0, KT, 256)

            def ik_product(bank):
                for x in range(KT):
                    last = three(bank[0:72, :], (wh[:, x, 0:72], wl[:, x, 0:72]), (hhi[:, x, :], hlo[:, x, :]),
                                 x == 0, x == KT - 1)
                return last
            pe_tile(pe, t0, par0, ik_product)
            pe.wait_ge(evac, t0 + 1)
            for i in range(QT):
                last = nc.tensor.matmul(pt[0][:, 8 * i:8 * i + 8], iwt_f[64:72, i * P:i * P + P], ident[64:72, 64:72],
                                        start=True, stop=True)
            last.then_inc(iw_turned, 1)
            pe_spread(pe, hb, 1 + 4 * l, 0, dsa, 13312, None)
            pe.wait_ge(hn_out, hb + 8)
            pe.wait_ge(ix_parts, 5 * (l + 1))
            for i in range(1, QT):
                for hd in range(8):
                    e = 24 * l + 8 * (i - 1) + hd
                    if e >= 2:
                        pe.wait_ge(ix_relu, e - 1)
                    rows = y_rows(hd % 2)
                    three(ps[e % 2][:, 0:P * (i + 1)], [x[rows, hd // 2, i * P:i * P + P] for x in iqr],
                          [x[rows, 0:P * (i + 1)] for x in ikr], True, True).then_inc(ix_done, 1)
                if i == 1:
                    pe_tm(pe, "bv", l, 256)
                else:
                    pe_fm(pe, "bgate", l, h, KT, 256, only=i - 2)
            stage_end(pe, "pe")
            for s in range(4 + 2):
                if s < 4:
                    pe.wait_ge(ring_in, 4 + 8 * l + s + 1)
                for i in range(QT + 1):
                    if s < 4 and i < QT:
                        pe_scores(pe, U1 + 12 * l + s, i, qr[s % 2], kr[s % 2], slice(0, P), selected)
                    if 1 <= s <= 4 and i >= 1:
                        pe_transpose(pe, U1 + 8 * l + s - 1, i - 1, [p_of(P_DSA, (s - 1) % 2)], [diag_dsa[(s - 1) % 2]])
                    if s >= 2 and i < QT:
                        if i == 0 and s >= 4:
                            pe.wait_ge(o_out, 8 + 8 * l + s - 3)
                        if i == 0:
                            pe.wait_ge(v_in, 8 * l + s - 1)
                        pe_pv(pe, U1 + 8 * l + s - 2, i, vr[s % 2], po[s % 2], i == 0, i == 3)
                        pe_tile_part(pe, "bz", l, s - 2, i, QT)
            pe_branch(pe, "bbr", l, lambda k: yr, y_parts(pe, 3 * l))
            pe_fm(pe, "cq", l, h, KT, 256)
            pe_fm(pe, "ck", l, h, KT, 256)
            pe_sums(pe, hb + 8, diff, 10240, 8)
            pe_tm(pe, "cv", l, 256)
            pe.wait_ge(lam_in, l + 1)
            nc.tensor.matmul(po[0][:, 0:2], ones, lam[:, 0:2], start=True, stop=True).then_inc(lam_sum, 1)
            pe_spread(pe, hb + 8, 2 + 4 * l, 0, diff, 14848, 10240)
            stage_end(pe, "pe")
            for s in range(4 + 2):
                if s < 4:
                    pe.wait_ge(ring_in, 4 + 8 * l + 4 + s + 1)
                for comp in range(2):
                    for i in range(QT):
                        if s < 4:
                            pe_scores(pe, U1 + 12 * l + 4 + 2 * s + comp, i, qr[s % 2], kr[s % 2], y_rows(comp),
                                      chunked)
                        if s >= 2 and comp == 0:
                            if i == 0 and s >= 4:
                                pe.wait_ge(o_out, 8 + 8 * l + 4 + s - 3)
                            if i == 0:
                                pe.wait_ge(v_in, 8 * l + 4 + s - 1)
                            pe_pv(pe, U1 + 8 * l + 4 + s - 2, i, vr[s % 2], po[s % 2], i == 0, i == 3)
                        if 1 <= s <= 4 and comp == 1:
                            pe_transpose(pe, U1 + 8 * l + 4 + s - 1, i,
                                         [wv(P_DIFF + TRI * (2 * ((s - 1) % 2) + c), TRI) for c in range(2)], diag_diff)
            stage_end(pe, "pe")
            pe_hn(pe, hb + 16, 3 + 4 * l, 0, diff_out, P_DIFF, P_DIFF + 1536)
            stage_end(pe, "pe")
            pe_fm(pe, "cz", l, h, KT, 256)
            pe_fm(pe, "cgate", l, h, KT, 256)
            pe_branch(pe, "cbr", l, lambda k: yr, y_parts(pe, 3 * l + 1))
            stage_end(pe, "pe")
            pe_fm(pe, "ga", l, h, KT, 256)
            pe.wait_ge(wa2_in, 16 * (l + 1))
            pe.wait_ge(alr_out, l + 1)
            for i in range(QT):
                last = nc.tensor.matmul(ps[i // 2][:, 256 * (i % 2):256 * (i % 2) + 256], alr_f[0:17, i * P:i * P + P],
                                        wa2_f[0:17, :], start=True, stop=True)
            last.then_inc(z_done, 1)
            pe_tm(pe, "gk", l, 256)
            pe.wait_ge(g_la, l + 1)
            for i in range(QT):
                nc.tensor.matmul(pt[i // 2][:, 256 * (i % 2):256 * (i % 2) + 256], suf, la_f[:, i, :], start=True,
                                 stop=True)
            for hp in range(2):
                for i in range(QT):
                    last = nc.tensor.matmul(po[0][:, 8 * hp + 2 * i:8 * hp + 2 * i + 2], la_f[:, i, hp * P:hp * P + P],
                                            con(C_IND, 2), start=True, stop=True)
            last.then_inc(suf_done, 1)
            pe_tm(pe, "gv", l, 256)
            pe_fm(pe, "gq", l, h, KT, 256)
            pe.wait_ge(evac, section("gz", l)[2])
            pe.wait_ge(kdec_ready, l + 1)
            for c in range(8 + 1):
                if c < 8:
                    i, rows = c // 2, y_rows(c % 2)
                    if c >= 2:
                        pe.wait_ge(state_ready, 8 * l + c - 1)
                    for hp in range(2):
                        last = nc.tensor.matmul(pt[c % 2][:, 256 * hp:256 * hp + 256], kd_f[rows, i, hp * P:hp * P + P],
                                                gv_f[rows, i, 256 * hp:256 * hp + 256], start=True, stop=True)
                    last.then_inc(u_done, 1)
                if c >= 1:
                    pe.wait_ge(state_ready, 8 * l + c)
                    for hd in range(4):
                        rows = y_rows(hd % 2)
                        bank = (po[0], po[1], ps[0], ps[1])[hd]
                        last = nc.tensor.matmul(bank[:, CH * (c - 1):CH * c],
                                                st_f[(c - 1) % 2][rows, hd // 2, P * (hd % 2):P * (hd % 2) + P],
                                                gq_f[rows, hd // 2, CH * (c - 1):CH * c], start=True, stop=True)
                    last.then_inc(gla_o, 1)
            stage_end(pe, "pe")
            pe_hn(pe, hb + 20, 4 + 4 * l, 0, gla_out, 6144, 6144 + 1536)
            stage_end(pe, "pe")
            pe_fm(pe, "gz", l, h, KT, 256)
            pe_fm(pe, "agate", l, h, KT, 256)
            pe_branch(pe, "abr", l, lambda k: yr, y_parts(pe, 3 * l + 2))
            pe_fm(pe, "wout2", l, mr, KT, 256, lambda x: pe.wait_ge(m_lo, KT * (1 + l) + x + 1))
            if l == LAYERS - 1:
                stage_end(pe, "pe")

        def act_layer(act, l):
            dsa, diff, diff_out, gla_out = layer_items(l)
            hb = HN1 + HN_LAYER * l
            act_norm(act, 2 + l)
            act_tiles(act, "bq", l, copy_to(a_f))
            act_squares(act, hb, dsa[0:4], 0, 8)
            act_tiles(act, "bk", l, copy_to(b_f))
            act_squares(act, hb, dsa, 0, 8, first=4)
            act_tiles(act, "iq", l, copy_to(iq_f))
            act_roots(act, hb, dsa, 12800)
            c0, _, t0, _ = section("ik", l)
            par0, slot0 = par_of("ik", l)
            act.wait_ge(mm_done, t0 + 1)
            for half in range(2):
                nc.scalar.activation(ik_f[y_rows(half), :], pp[par0][0:64, :], ACT.Copy)
            nc.scalar.activation(iwt_f[64:72, :], pp[par0][64:72, :], ACT.Copy)
            act.drain().then_inc(evac, 1)
            act_next(act, "ik", l, c0, slot0)
            act.drain()
            for x in range(5):
                dst, src = (iqr[0][:, x, :], iq_f[:, x, :]) if x < 4 else (ikr[0], ik_f)
                nc.scalar.activation(dst, src, ACT.Copy).then_inc(part_hi, 1)
            for i in range(1, QT):
                for hd in range(8):
                    e = 24 * l + 8 * (i - 1) + hd
                    act.wait_ge(ix_done, e + 1)
                    if e - 24 * l >= 2:
                        act.wait_ge(post, POST_IX(l) + e - 24 * l - 1)
                    nc.scalar.activation(relu_f[e % 2][:, 0:P * (i + 1)], ps[e % 2][:, 0:P * (i + 1)], ACT.Relu,
                                         scale=0.125).then_inc(ix_relu, 1)
                if i == 1:
                    act_tiles(act, "bv", l, lambda bank, n, m: nc.scalar.activation(
                        c_f[:, m, 256 * (n // 4):256 * (n // 4) + 256], bank[:, 0:256], ACT.Copy))
                else:
                    act_tiles(act, "bgate", l, copy_to(merged, ACT.Sigmoid), only=i - 2)
            stage_end(act, "act")
            bz0 = section("bz", l)
            for s in range(4 + 2):
                for i in range(QT + 1):
                    if s < 4 and i < QT:
                        u = U1 + 12 * l + s
                        if i == 0 and s >= 2:
                            act.wait_ge(tr_done, 4 * (U1 + 8 * l + s - 2) + 4)
                        act_exp(act, u, i, p_of(P_DSA, s % 2))
                    if 1 <= s <= 4 and i >= 1:
                        v = U1 + 8 * l + s - 1
                        if i == 1 and s >= 3:
                            act.wait_ge(pv_done, v - 1)
                        act_pt(act, v, i - 1)
                if s >= 2:
                    n = s - 2
                    act.wait_ge(pv_done, U1 + 8 * l + n + 1)
                    nc.scalar.activation(a_f[:, n, :], po[s % 2][:, :], ACT.Copy).then_inc(o_out, 1)
                    act.wait_ge(mm_done, bz0[2] + n + 1)
                    bank = pp[(par_of("bz", l)[0] + n) % 2]
                    if n < 2:
                        nc.scalar.activation(z_f[:, n, :], bank[:, :], ACT.Copy).then_inc(evac, 1)
                    else:
                        nc.scalar.activation(z_f[:, n, :], bank[:, :], ACT.Silu).then_inc(evac, 1)
                    if n % 2 == 1:
                        act_next(act, "bz", l, bz0[0] + n // 2, (par_of("bz", l)[1] + n // 2) % 2)
                    if n == 2:
                        for x in range(2):
                            nc.scalar.activation(z_f[:, x, :], z_f[:, x, :], ACT.Silu)
                    if n >= 2:
                        act.drain().then_inc(z_ready, 1)
            act_y(act, 3 * l)
            act_branch(act, "bbr", l, POST_BR(l, 0), br2_f)
            act.wait_ge(post, POST_BR(l, 1))
            act_tiles(act, "cq", l, copy_to(a_f))
            act_squares(act, hb + 8, diff[0:4], 10240, 8)
            act_tiles(act, "ck", l, copy_to(b_f))
            act_squares(act, hb + 8, diff, 10240, 8, first=4)
            act_roots(act, hb + 8, diff, 14336)
            act_spread(act, 2 + 4 * l, 10240)
            act_tiles(act, "cv", l, lambda bank, n, m: nc.scalar.activation(
                c_f[:, m, 256 * (n // 4):256 * (n // 4) + 256], bank[:, 0:256], ACT.Copy))
            act.wait_ge(lam_sum, l + 1)
            nc.scalar.activation(lam[:, 2:4], po[0][:, 0:2], ACT.Exp).then_inc(lam_exp, 1)
            stage_end(act, "act")
            for s in range(4 + 2):
                for comp in range(2):
                    for i in range(QT):
                        if s < 4:
                            u = U1 + 12 * l + 4 + 2 * s + comp
                            if comp == 0 and i == 0 and s >= 2:
                                act.wait_ge(tr_done, 4 * (U1 + 8 * l + 4 + s - 2) + 4)
                            act_exp(act, u, i, wv(P_DIFF + TRI * (2 * (s % 2) + comp), TRI))
                        if 1 <= s <= 4 and comp == 1:
                            v = U1 + 8 * l + 4 + s - 1
                            if i == 0 and s >= 3:
                                act.wait_ge(pv_done, v - 1)
                            act_pt(act, v, i)
                if 2 <= s < 6:
                    act.wait_ge(pv_done, U1 + 8 * l + 4 + s - 2 + 1)
                    nc.scalar.activation(a_f[:, s - 2, :], po[s % 2][:, :], ACT.Copy).then_inc(o_out, 1)
            stage_end(act, "act")
            act_hn(act, hb + 16, 3 + 4 * l, diff_out, P_DIFF, P_DIFF + 1024)
            stage_end(act, "act")
            act_tiles(act, "cz", l, copy_to(z_f, ACT.Silu))
            act_y(act, 3 * l + 1)
            act_tiles(act, "cgate", l, copy_to(gate_f, ACT.Sigmoid))
            act_branch(act, "cbr", l, POST_BR(l, 1), br2_f)
            stage_end(act, "act")
            act.dma_start(wa2_f, small_in[:, 6 * P + 256 * l:6 * P + 256 * l + 256]).then_inc(wa2_in, 16)
            act_tiles(act, "ga", l, lambda bank, n, m: nc.scalar.activation(alr_f[0:16, :], bank[0:16, :], ACT.Copy))
            act.drain().then_inc(alr_out, 1)
            act.wait_ge(z_done, l + 1)
            for x in range(2):
                nc.scalar.activation(za_f[:, 2 * x:2 * x + 2, :].rearrange("p a b -> p (a b)"), ps[x][:, :], ACT.Abs)
            act.drain()
            za = za_f.rearrange("p a b -> p (a b)")
            nc.scalar.activation(za, za, ACT.Exp, scale=-1.0)
            act.drain()
            nc.scalar.activation(za, za, ACT.Ln, bias=con(C_ONES1)).then_inc(g_exp, 1)
            act_tiles(act, "gk", l, lambda bank, n, m: nc.scalar.activation(gk_f[:, m, :], bank[:, 0:256], ACT.Copy))
            act.wait_ge(suf_done, l + 1)
            for x in range(2):
                nc.scalar.activation(za_f[:, 2 * x:2 * x + 2, :].rearrange("p a b -> p (a b)"), pt[x][:, :], ACT.Exp)
            nc.scalar.activation(dec_f, po[0][:, 0:16].rearrange("p (a b) -> p a b", a=2), ACT.Exp)
            act.drain().then_inc(decayed, 1)
            act_tiles(act, "gv", l, lambda bank, n, m: nc.scalar.activation(
                gv_f[:, m, 256 * (n // 4):256 * (n // 4) + 256], bank[:, 0:256], ACT.Copy))
            act_tiles(act, "gq", l, copy_to(gq_f, scale=0.125))
            act.wait_ge(gla_o, 8 * l + 8)
            for hd in range(4):
                nc.scalar.activation(a_f[:, hd, :], (po[0], po[1], ps[0], ps[1])[hd][:, :], ACT.Copy)
            stage_end(act, "act")
            act_hn(act, hb + 20, 4 + 4 * l, gla_out, 6144, 6144 + 1024)
            stage_end(act, "act")
            act_tiles(act, "gz", l, copy_to(z_f, ACT.Silu))
            act_y(act, 3 * l + 2)
            act_tiles(act, "agate", l, copy_to(gate_f, ACT.Sigmoid))
            act_branch(act, "abr", l, POST_BR(l, 2), br2_f)
            for x in range(KT):
                act.wait_ge(post, POST_BR(l, 2) + x + 1)
                nc.scalar.activation(mr[0][:, x, :], merged[:, x, :], ACT.Copy).then_inc(part_hi, 1)
            act_tiles(act, "wout2", l, copy_to(prod_f))
            if l == LAYERS - 1:
                stage_end(act, "act")

        def act_y(act, n):
            for x in range(4):
                act.wait_ge(y_ready, 4 * n + x + 1)
                nc.scalar.activation(yr[0][:, x, :], a_f[:, x, :], ACT.Copy).then_inc(part_hi, 1)

        def pool_y(pool, n, hi0):
            for x in range(4):
                pool.wait_ge(part_hi, hi0 + x + 1)
                nc.gpsimd.tensor_tensor(yr[1][:, x, :], a_f[:, x, :], yr[0][:, x, :].bitcast(F32),
                                        ALU.subtract).then_inc(y_lo, 1)

        POST_LAYER = 24 + 24
        def POST_IX(l):
            return 16 + POST_LAYER * l

        def POST_BR(l, b):
            return 16 + POST_LAYER * l + 24 + 8 * b

        PART1 = 4 + KT
        PART_LAYER = 5 + 12 + KT

        def dve_branch(dve, name, l, b):
            c0, n, t0, per = section(name, l)
            _, slot0 = par_of(name, l)
            for k in range(n):
                for m in range(4):
                    j = 4 * k + m
                    gated_add(dve, t0, b == 0, (gate_f if b else merged)[:, j, :], br2_f, j, m % 2, merged[:, j, :])
                dve_conv(dve, c0 + k + 2, (slot0 + k) % 2)

        def dve_y(dve, z_name, gate_name, l):
            c0, n, t0, per = section(z_name, l)

            def after(nn, t):
                dve.wait_ge(evac, t + 1)
                nc.vector.tensor_tensor(tile(a_f, nn), tile(a_f, nn), tile(z_f, nn), ALU.mult).then_inc(y_ready, 1)
            dve_next(dve, z_name, l, after)
            dve_next(dve, gate_name, l)

        def dve_layer(dve, l):
            dsa, diff, diff_out, gla_out = layer_items(l)
            hb = HN1 + HN_LAYER * l
            dve_norm(dve, 2 + l, lambda k: col(V_N2 + 8 * l + k))
            for name in ("bq", "bk", "iq"):
                dve_next(dve, name, l)
            dve_inverse(dve, 1 + 4 * l, dsa, 12800, 13312)
            dve_next(dve, "ik", l)
            dve.wait_ge(iw_turned, l + 1)
            nc.vector.tensor_scalar(iw_f, pt[0][:, 0:32].rearrange("p (i n) -> p i n", i=QT), float(8 ** -0.5), None,
                                    ALU.mult)
            dve_scale(dve, hb, 0, dsa, None)
            m8 = stat[:, 48:56]
            for i in range(1, QT):
                w, sc = P * (i + 1), sc_f[i]
                for hd in range(8):
                    e = 24 * l + 8 * (i - 1) + hd
                    dve.wait_ge(ix_relu, e + 1)
                    r = relu_f[e % 2][:, 0:w]
                    if hd == 0:
                        nc.vector.tensor_scalar(sc, r, iw_f[:, i, hd:hd + 1], None, ALU.mult).then_inc(post, 1)
                    else:
                        dve.drain()
                        nc.vector.scalar_tensor_tensor(out=sc, in0=r, scalar=iw_f[:, i, hd:hd + 1], in1=sc,
                                                       op0=ALU.mult, op1=ALU.add).then_inc(post, 1)
                dve.drain()
                nc.vector.memset(sc[0:64, w - CH:w], NEG)
                for _ in range(TOPK // 8):
                    dve.drain()
                    nc.vector.max(m8, sc)
                    dve.drain()
                    nc.vector.match_replace(sc, m8, sc, TAKEN)
                dve.drain()
                nc.vector.tensor_scalar(selm[:, OFF[i]:OFF[i] + w], sc, TAKEN, NEG, ALU.is_gt, ALU.mult)
            stage_end(dve, "dve")
            bz0, slot0 = section("bz", l)[0], par_of("bz", l)[1]
            for s in range(4 + 1):
                for i in range(QT + 1):
                    if s < 4 and i < QT:
                        u = U1 + 12 * l + s
                        if i == 0 and s >= 2:
                            dve.wait_ge(ex_done, 4 * (u - 1))
                        dve_max(dve, u, i)
                    if s < 4 and i == QT:
                        dve.wait_ge(ex_done, 4 * (U1 + 12 * l + s) + 4)
                        nc.vector.reciprocal(rcp[0], rsum[s % 2])
                        dve.drain()
                        if s >= 2:
                            dve.wait_ge(tr_done, 4 * (U1 + 8 * l + s - 1))
                        make_diag(diag_dsa[s % 2], rcp[0]).then_inc(diag_ready, 1)
                    if 1 <= s <= 4 and i >= 1:
                        dve_pt(dve, U1 + 8 * l + s - 1, i - 1)
                if s == 1:
                    dve.wait_ge(w_lo, bz0 + 1)
                    dve_conv(dve, bz0 + 1, (slot0 + 1) % 2)
                if s == 3:
                    dve_conv(dve, bz0 + 2, slot0 % 2)
            for n in range(4):
                dve.wait_ge(o_out, 8 + 8 * l + n + 1)
                dve.wait_ge(z_ready, 2 * l + (1 if n < 3 else 2))
                nc.vector.tensor_tensor(a_f[:, n, :], a_f[:, n, :], z_f[:, n, :], ALU.mult).then_inc(y_ready, 1)
            dve_conv(dve, bz0 + 3, (slot0 + 1) % 2)
            dve_branch(dve, "bbr", l, 0)
            dve_next(dve, "cq", l)
            dve_next(dve, "ck", l)
            dve_inverse(dve, 2 + 4 * l, diff, 14336, 14848)
            dve_next(dve, "cv", l)
            v0 = V_LAM + 4 * l
            for x in range(2):
                nc.vector.tensor_tensor(lam[:, x:x + 1], col(v0 + 2 * x), col(v0 + 2 * x + 1), ALU.mult)
            dve.drain().then_inc(lam_in, 1)
            dve.wait_ge(lam_exp, l + 1)
            nc.vector.tensor_tensor(lam[:, 4:5], lam[:, 3:4], lam[:, 2:3], ALU.subtract)
            dve.drain()
            nc.vector.tensor_tensor(lam[:, 4:5], lam[:, 4:5], con(C_LINIT + l), ALU.subtract)
            dve_scale(dve, hb + 8, 0, diff, None)
            stage_end(dve, "dve")
            for s in range(4 + 1):
                for comp in range(2):
                    for i in range(QT):
                        if s < 4:
                            u = U1 + 12 * l + 4 + 2 * s + comp
                            if i == 0 and 2 * s + comp >= 2:
                                dve.wait_ge(ex_done, 4 * (u - 1))
                            dve_max(dve, u, i)
                        if 1 <= s <= 4 and comp == 1:
                            dve_pt(dve, U1 + 8 * l + 4 + s - 1, i)
                    if s < 4:
                        dve.wait_ge(ex_done, 4 * u + 4)
                        nc.vector.reciprocal(rcp[comp], rsum[u % 2])
                        dve.drain()
                if s < 4:
                    nc.vector.tensor_scalar(rcp[1], rcp[1], lam[:, 4:5], None, ALU.mult)
                    dve.drain()
                    if s == 0:
                        dve.wait_ge(ring_in, 4 + 8 * l + 4 + 2)
                    else:
                        dve.wait_ge(tr_done, 4 * (U1 + 8 * l + 4 + s))
                    make_diag(diag_diff[0], rcp[0])
                    make_diag(diag_diff[1], rcp[1])
                    dve.drain().then_inc(diag_ready, 1)
            stage_end(dve, "dve")
            dve_hn(dve, hb + 16, 3 + 4 * l, 0, diff_out, P_DIFF + 1024, P_DIFF + 1536, P_DIFF + 2048)
            stage_end(dve, "dve")
            dve_y(dve, "cz", "cgate", l)
            dve_branch(dve, "cbr", l, 1)
            nc.vector.memset(alr_f[0:32, :], 1.0)
            stage_end(dve, "dve")
            dve_next(dve, "ga", l)
            dve.wait_ge(g_exp, l + 1)
            for x in range(2):
                a = la_f[:, 2 * x:2 * x + 2, :].rearrange("p a b -> p (a b)")
                nc.vector.tensor_scalar(a, ps[x][:, :], 0.0, None, ALU.min)
            dve.drain()
            nc.vector.tensor_tensor(la_f, la_f, za_f, ALU.subtract)
            dve.drain()
            nc.vector.tensor_scalar(la_f, la_f, 1.0 / 16, None, ALU.mult).then_inc(g_la, 1)
            dve_next(dve, "gk", l)
            dve.wait_ge(decayed, l + 1)
            nc.vector.tensor_tensor(kd_f, gk_f, za_f, ALU.mult).then_inc(kdec_ready, 1)
            dve_next(dve, "gv", l)
            dve_next(dve, "gq", l)
            for c in range(8):
                dve.wait_ge(u_done, 8 * l + c + 1)
                if c >= 2:
                    dve.wait_ge(gla_o, 8 * l + c - 1)
                for hp in range(2):
                    new = st_f[c % 2][:, hp, :]
                    if c == 0:
                        nc.vector.tensor_copy(new, pt[0][:, 256 * hp:256 * hp + 256])
                    else:
                        nc.vector.scalar_tensor_tensor(out=new, in0=st_f[(c - 1) % 2][:, hp, :], scalar=dec_f[:, hp, c:c + 1],
                                                       in1=pt[c % 2][:, 256 * hp:256 * hp + 256], op0=ALU.mult, op1=ALU.add)
                dve.drain().then_inc(state_ready, 1)
            stage_end(dve, "dve")
            dve_hn(dve, hb + 20, 4 + 4 * l, 0, gla_out, 6144 + 1024, 6144 + 1536, 6144 + 2048)
            stage_end(dve, "dve")
            dve_y(dve, "gz", "agate", l)
            dve_branch(dve, "abr", l, 2)
            dve_next(dve, "wout2", l, lambda n, t: dve_add_x(dve, prod_f, n, t))
            if l == LAYERS - 1:
                stage_end(dve, "dve")

        def pool_layer(pool, l):
            p0 = PART1 + PART_LAYER * l
            pool_norm(pool, 2 + l)
            for x in range(5):
                hi, lo, src = (iqr[0][:, x, :], iqr[1][:, x, :], iq_f[:, x, :]) if x < 4 else (ikr[0], ikr[1], ik_f)
                pool.wait_ge(part_hi, p0 + x + 1)
                nc.gpsimd.tensor_tensor(lo, src, hi.bitcast(F32), ALU.subtract).then_inc(ix_parts, 1)

            def ring(s):
                split_pool(pool, qr[s % 2], a_f[:, s, :])
                split_pool(pool, kr[s % 2], b_f[:, s, :])
                pool.drain().then_inc(ring_in, 1)

            def v_ring(s, v):
                if s >= 2:
                    pool.wait_ge(pv_done, v - 1)
                split_pool(pool, vr[s % 2], c_f[:, :, s * P:s * P + P]).then_inc(v_in, 1)
            pool.wait_ge(hn_out, HN1 + HN_LAYER * l + 8)
            c0, slot0 = section("bv", l)[0], par_of("bv", l)[1]
            for k in range(5):
                c, slot = c0 + k + 2, (slot0 + k) % 2
                if k == 0:
                    ring(0)
                    pool.wait_ge(w_lo, c)
                pool.wait_ge(w_hi, c + 1)
                nc.gpsimd.tensor_tensor(wlo[:, slot, :], wraw[:, slot, :], whi[:, slot, :].bitcast(F32),
                                        ALU.subtract).then_inc(w_lo, 1)
                if k == 1:
                    ring(1)
                if k == 3:
                    pool.wait_ge(evac, section("bgate", l)[2])
                    v_ring(0, 0)
                if k == 4:
                    v_ring(1, 0)
            stage_end(pool, "pool")
            for s in range(4):
                if s < 2:
                    pool.wait_ge(ex_done, 4 * (U1 + 12 * l + s + 1))
                    ring(s + 2)
                else:
                    v_ring(s, U1 + 8 * l + 0 + s)
            pool_y(pool, 3 * l, p0 + 5)
            pool.drain().then_inc(stage["pool"], 1)
            pool.wait_ge(evac, section("cz", l)[2])
            v_ring(0, 0)
            for s in range(2):
                pool.wait_ge(hn_out, HN1 + HN_LAYER * l + 8 + 2 * s + 2)
                ring(s)
            v_ring(1, 0)
            stage_no["pool"] += 1
            for other in ("pe", "act", "dve"):
                pool.wait_ge(stage[other], stage_no["pool"])
            for s in range(4):
                if s < 2:
                    pool.wait_ge(ex_done, 4 * (U1 + 12 * l + 4 + 2 * s + 2))
                    ring(s + 2)
                else:
                    v_ring(s, U1 + 8 * l + 4 + s)
            stage_end(pool, "pool")
            stage_end(pool, "pool")
            pool_y(pool, 3 * l + 1, p0 + 9)
            for _ in range(3):
                stage_end(pool, "pool")
            pool_y(pool, 3 * l + 2, p0 + 13)
            for x in range(KT):
                pool.wait_ge(part_hi, p0 + 17 + x + 1)
                nc.gpsimd.tensor_tensor(mr[1][:, x, :], merged[:, x, :], mr[0][:, x, :].bitcast(F32),
                                        ALU.subtract).then_inc(m_lo, 1)
            if l == LAYERS - 1:
                stage_end(pool, "pool")

        def act_ff(act, r, k):
            n = sum(ROUNDS[:r]) + k
            act.wait_ge(ff_conv, n + 1)
            nc.scalar.activation(sg_f[:, k % 2, :], cv_f[:, k % 2, :], ACT.Sigmoid).then_inc(ff_sig, 1)
            act.wait_ge(ff_prod, n + 1)
            nc.scalar.activation(mr[0][:, k, :], gp_f[:, k, :], ACT.Copy).then_inc(ff_hi, 1)

        @block.tensor
        def _(pe):
            pe.wait_ge(const_in, 80)
            pe_norm(pe, 0)
            pe_fm(pe, "u", None, h, KT, 256, h_ready(pe, 0))
            pe_fm(pe, "q", None, h, KT, 256)
            pe_fm(pe, "cmp", None, h, KT, 256)
            pe_fm(pe, "ksw", None, h, KT, 256)
            pe_tm(pe, "vsw", None, 256)
            pe.wait_ge(cmp_in, 32)
            for kv in range(2):
                pe.wait_ge(blk_ready, kv + 1)
                for x in range(16):
                    last = nc.tensor.matmul(ps[kv][:, 0:2 * N_CMP], w1_f[:, 16 * kv + x, :], blk_f[kv][:, x, :],
                                            start=(x == 0), stop=(x == 15))
                last.then_inc(hid_done, 1)
            pe.wait_ge(hid_out, 1)
            nc.tensor.matmul(pt[0][:, 0:2 * N_CMP], cw2[:, 0, :], hid_f[0][:, 0:2 * N_CMP], start=True,
                             stop=True).then_inc(kvc_done, 1)
            pe.wait_ge(hid_out, 2)
            for g in range(2):
                last = nc.tensor.matmul(pt[1][0:N_CMP, 64 * g:64 * g + 64], hid_f[1][:, N_CMP * g:N_CMP * g + N_CMP],
                                        cw2[:, 1, 0:64], start=True, stop=True)
            last.then_inc(kvc_done, 1)
            pe_tm(pe, "nsag", None, 24)
            stage_end(pe, "pe")
            pe_hn(pe, 0, 0, 0, k_items, T, T + 1536)
            stage_end(pe, "pe")
            for s in range(U1 + 2):
                if s < U1:
                    hd, b = s // 2, s % 2
                    t, g = hd // 2, hd % 2
                    if b == 0:
                        if g == 0:
                            pe.wait_ge(ring_in, t + 1)
                        if hd >= 1:
                            pe.wait_ge(cs_sub, hd)
                        rows = y_rows(g)
                        for i in range(QT):
                            three(pp[0][:, 32 * i:32 * i + 32], [x[rows, i * P:i * P + P] for x in qr[t % 2]],
                                  [x[rows, :] for x in kcr], True, False)
                            last = nc.tensor.matmul(pp[0][:, 32 * i:32 * i + 32], idb,
                                                    msk[:, M_CMP + 32 * i:M_CMP + 32 * i + 32],
                                                    start=False, stop=True)
                        last.then_inc(cs_ready, 1)
                for i in range(QT + 1):
                    if s < U1 and i < QT:
                        pe_scores(pe, s, i, qr[t % 2], kr[b], y_rows(g), causal)
                    if 1 <= s <= U1 and i >= 1:
                        pe_transpose(pe, s - 1, i - 1, [p_of(P1, (s - 1) % 2)], [diag1[(s - 1) % 2]])
                    if s >= 2 and i < QT:
                        v = s - 2
                        hv = v // 2
                        if v % 2 == 0 and i == 0 and hv >= 2:
                            pe.wait_ge(o_out, hv - 1)
                        pe_pv(pe, v, i, vr[v % 2], po[hv % 2], v % 2 == 0 and i == 0, False)
                        if v % 2 == 1 and i == 3:
                            pe.wait_ge(ct_out, hv + 1)
                            last = nc.tensor.matmul(po[hv % 2][:, :], vc_f[0:32, :], ct_f[0:32, :],
                                                    start=False, stop=True)
                            last.then_inc(o_done, 1)
                if s < U1 and s % 2 == 1:
                    hd = s // 2
                    pe.wait_ge(cs_p, hd + 1)
                    if hd >= 1:
                        pe.wait_ge(ct_out, hd)
                    for i in range(QT):
                        last = nc.tensor.transpose(pp[1][0:32, i * P:i * P + P], cp_f[:, i, :], ident)
                    last.then_inc(ct_done, 1)
            stage_end(pe, "pe")
            for g in range(4):
                pe.wait_ge(pool_in, g + 1)
                if g == 0:
                    pe.wait_ge(poolw_in, 16)
                if g >= 2:
                    pe.wait_ge(pool_out, g - 1)
                nc.tensor.matmul(ps[g % 2][:, :], poolw[:, g, :], u_f[:, g, :], start=True,
                                 stop=True).then_inc(pool_mm, 1)
            stage_end(pe, "pe")
            pe_fm(pe, "mg", None, h, KT, 256)
            pe_branch(pe, "merge1", None, lambda k: yr if k % 2 == 0 else yr2,
                      lambda k, x: pe.wait_ge(y_lo, 2 * x + 1 + k % 2))
            pe_fm(pe, "wout", None, mr, KT, 256, lambda x: pe.wait_ge(m_lo, x + 1))
            pe_norm(pe, 1)
            for r in range(3):
                pe_fm(pe, f"up{r}", None, h, KT, 256, h_ready(pe, 1) if r == 0 else None)
                pe_fm(pe, f"down{r}", None, mr, ROUNDS[r], 256,
                      lambda x: pe.wait_ge(ff_lo, FF[r] + x + 1), last_late=True)
            for l in range(LAYERS):
                pe_layer(pe, l)

        @block.scalar
        def _(act):
            act.wait_ge(const_in, 80)
            act_conv(act, 0, 0)
            act_conv(act, 1, 1)
            act_norm(act, 0)
            act.wait_ge(rope_red, 1)
            nc.scalar.activation(sin_t, wv(T + 1024, S), ACT.Sin).then_inc(rope_sin, 1)
            nc.scalar.activation(cos_t, wv(T + 1536, S), ACT.Sin)
            act.drain()
            act.dma_start(w1_f, cmpw_in).then_inc(cmp_in, 16)
            act.dma_start(cw2, small_in[:, 4 * P:6 * P].rearrange("p (v n) -> p v n", v=2)).then_inc(cmp_in, 16)
            act_tiles(act, "u", None, copy_to(u_f))
            act_tiles(act, "q", None, copy_to(q_f))
            act_tiles(act, "cmp", None, copy_to(kcv_f))
            act_tiles(act, "ksw", None, copy_to(ksw_f))
            act_tiles(act, "vsw", None, lambda bank, n, m: nc.scalar.activation(v_f[:, m, :], bank[:, 0:256], ACT.Copy))
            for kv in range(2):
                act.wait_ge(hid_done, kv + 1)
                nc.scalar.activation(hid_f[kv][:, 0:2 * N_CMP], ps[kv][:, 0:2 * N_CMP], ACT.Silu).then_inc(hid_out, 1)
            act.wait_ge(kvc_done, 1)
            for g in range(2):
                nc.scalar.activation(kc_f[y_rows(g), 0:N_CMP], pt[0][y_rows(g), N_CMP * g:N_CMP * g + N_CMP], ACT.Copy)
            act.wait_ge(kvc_done, 2)
            nc.scalar.activation(vc_f[0:N_CMP, :], pt[1][0:N_CMP, 0:P], ACT.Copy)
            act_tiles(act, "nsag", None,
                      lambda bank, n, m: nc.scalar.activation(g_f[:, m, :], bank[:, 0:24], ACT.Sigmoid))
            stage_end(act, "act")
            act_hn(act, 0, 0, k_items, T, T + 1024)
            stage_end(act, "act")
            for s in range(U1 + 2):
                for i in range(QT + 1):
                    if s < U1 and i < QT:
                        if i == 0 and s >= 2:
                            act.wait_ge(tr_done, 4 * (s - 2) + 4)
                        act_exp(act, s, i, p_of(P1, s % 2))
                    if 1 <= s <= U1 and i >= 1:
                        v = s - 1
                        if i == 1 and v >= 2:
                            act.wait_ge(pv_done, v - 1)
                        act_pt(act, v, i - 1)
                if s < U1 and s % 2 == 0:
                    hd = s // 2
                    act.wait_ge(cs_sub, hd + 1)
                    nc.scalar.activation(cp_f, cp_f, ACT.Exp).then_inc(cs_exp, 1)
                if s < U1 and s % 2 == 1:
                    hd = s // 2
                    act.wait_ge(ct_done, hd + 1)
                    if hd >= 1:
                        act.wait_ge(o_done, hd)
                    nc.scalar.activation(ct_f[0:32, :], pp[1][0:32, :], ACT.Copy).then_inc(ct_out, 1)
                if s >= 3 and s % 2 == 1:
                    hv = (s - 3) // 2
                    t, g = hv // 2, hv % 2
                    act.wait_ge(o_done, hv + 1)
                    nc.scalar.activation(q_f[y_rows(g), t, :], po[hv % 2][y_rows(g), :], ACT.Copy).then_inc(o_out, 1)
            stage_end(act, "act")
            act.dma_start(poolw, small_in[:, 0:4 * P].rearrange("p (g n) -> p g n", g=4)).then_inc(poolw_in, 16)
            for g in range(4):
                act.wait_ge(pool_mm, g + 1)
                nc.scalar.activation(u_f[:, g, :], ps[g % 2][:, :], ACT.Copy, scale=col(V_PSCALE + g)
                                     ).then_inc(pool_out, 1)
            stage_end(act, "act")
            for x in range(4):
                nc.scalar.activation(yr[0][:, x, :], u_f[:, x, :], ACT.Copy)
                nc.scalar.activation(yr2[0][:, x, :], q_f[:, x, :], ACT.Copy).then_inc(part_hi, 1)
            act_tiles(act, "mg", None, copy_to(mg_f, ACT.Sigmoid))
            act_branch(act, "merge1", None, 0, br_f)
            for x in range(KT):
                act.wait_ge(post, 4 + 8 * (x // 4) + x % 4 + 1)
                nc.scalar.activation(mr[0][:, x, :], mg_f[:, x, :], ACT.Copy).then_inc(part_hi, 1)
            act_tiles(act, "wout", None, copy_to(prod_f))
            act_norm(act, 1)
            for r in range(3):
                c0, n, t0, per = section(f"up{r}")
                for k in range(ROUNDS[r]):
                    act.wait_ge(mm_done, t0 + 2 * k + 1)
                    nc.scalar.activation(gp_f[:, k, :], pp[0][:, :], ACT.Copy).then_inc(evac, 1)
                    act.wait_ge(mm_done, t0 + 2 * k + 2)
                    nc.scalar.activation(vl_f[:, k, :], pp[1][:, :], ACT.Copy).then_inc(evac, 1)
                    act_conv(act, c0 + k + 2, (c0 + k) % 2)
                    if k >= 1:
                        act_ff(act, r, k - 1)
                act_ff(act, r, ROUNDS[r] - 1)
                act_tiles(act, f"down{r}", None, copy_to(dn_f))
            for l in range(LAYERS):
                act_layer(act, l)

        @block.vector
        def _(dve):
            dve.wait_ge(const_in, 80)
            dve_conv(dve, 0, 0)
            dve_conv(dve, 1, 1)
            ang, kk, red, redc = wv(T, S), wv(T + 512, S), wv(T + 1024, S), wv(T + 1536, S)
            nc.vector.tensor_copy(kk, cos_t.bitcast(I32))
            nc.vector.tensor_copy(msk[:, :], wv(T + 2048, NMSK))
            dve.drain()
            nc.vector.tensor_scalar(ang, kk, con(C_INVF), None, ALU.mult)
            dve.drain()
            nc.vector.tensor_scalar(kk, ang, 1.0 / TWO_PI, None, ALU.mult)
            dve.drain()
            nc.vector.tensor_scalar(kk, kk, ROUND, None, ALU.add)
            dve.drain()
            nc.vector.tensor_scalar(kk, kk, -ROUND, None, ALU.add)
            dve.drain()
            for part in (PI_HI, PI_MID, PI_LO):
                nc.vector.scalar_tensor_tensor(out=ang, in0=kk, scalar=-part, in1=ang, op0=ALU.mult, op1=ALU.add)
                dve.drain()
            nc.vector.tensor_scalar(red, ang, 3.1415925, -3.1415925, ALU.min, ALU.max)
            nc.vector.tensor_scalar(redc, ang, float(np.pi / 2), None, ALU.add)
            dve.drain()
            nc.vector.tensor_scalar(kk, redc, float(np.pi), -TWO_PI, ALU.is_gt, ALU.mult)
            dve.drain()
            nc.vector.tensor_tensor(redc, redc, kk, ALU.add)
            dve.drain()
            nc.vector.tensor_scalar(redc, redc, 3.1415925, -3.1415925, ALU.min, ALU.max).then_inc(rope_red, 1)
            nc.vector.memset(kc_f, 0.0)
            nc.vector.memset(vc_f, 0.0)
            dve_norm(dve, 0, lambda k: col(V_MIX + k))
            dve.wait_ge(rope_sin, 1)
            nc.vector.tensor_scalar(sin_t, sin_t, con(C_SGN), None, ALU.mult)
            for name in ("u", "q", "cmp", "ksw"):
                dve_next(dve, name, None)
            dve.wait_ge(evac, section("ksw")[2])
            for kv in range(2):
                for odd in range(2):
                    for g in range(2):
                        src = kcv_f[y_rows(g), kv, :]
                        taps = bass.AP(src.tensor, src.offset + odd, [src.ap[0], [2, 16], [CMP_STRIDE, N_CMP]])
                        pos = vec[y_rows(g), V_PE + 32 * kv:V_PE + 32 * kv + 32]
                        pos = bass.AP(pos.tensor, pos.offset + odd, [pos.ap[0], [2, 16], [0, N_CMP]])
                        nc.vector.tensor_tensor(blk_f[kv][y_rows(odd), :, N_CMP * g:N_CMP * g + N_CMP], taps, pos, ALU.add)
                dve.drain().then_inc(blk_ready, 1)
            for name in ("vsw", "nsag"):
                dve_next(dve, name, None)
            stage_end(dve, "dve")
            dve_hn(dve, 0, 0, 0, k_items, T + 1024, T + 1536, T + 2048)
            stage_end(dve, "dve")
            for s in range(U1 + 2):
                if s < U1 and s % 2 == 0:
                    hd = s // 2
                    dve.wait_ge(cs_ready, hd + 1)
                    if hd >= 1:
                        dve.wait_ge(ct_done, hd)
                    c3 = pp[0][:, 0:P].rearrange("p (i n) -> p i n", i=4)
                    nc.vector.tensor_reduce(cstat[:, 0:4], c3, AX.X, ALU.max)
                    dve.drain()
                    nc.vector.tensor_tensor(cp_f, c3, cstat[:, 0:4].unsqueeze(2).broadcast_to([P, 4, 32]),
                                            ALU.subtract).then_inc(cs_sub, 1)
                for i in range(QT + 1):
                    if s < U1 and i < QT:
                        if i == 0 and s >= 2:
                            dve.wait_ge(ex_done, 4 * (s - 1))
                        dve_max(dve, s, i)
                    if s < U1 and i == QT:
                        hd, b = s // 2, s % 2
                        head = hd // 2 + 4 * (hd % 2)
                        dve.wait_ge(ex_done, 4 * s + 4)
                        nc.vector.reciprocal(rcp[0], rsum[s % 2])
                        dve.drain()
                        nc.vector.tensor_tensor(rcp[0], rcp[0], g_f[:, :, 3 * head + 1 + b], ALU.mult)
                        dve.drain()
                        if s >= 2:
                            dve.wait_ge(tr_done, 4 * (s - 1))
                        make_diag(diag1[s % 2], rcp[0]).then_inc(diag_ready, 1)
                    if 1 <= s <= U1 and i >= 1:
                        dve_pt(dve, s - 1, i - 1)
                if s < U1 and s % 2 == 0:
                    hd = s // 2
                    head = hd // 2 + 4 * (hd % 2)
                    dve.wait_ge(cs_exp, hd + 1)
                    nc.vector.tensor_reduce(cstat[:, 4:8], cp_f, AX.X, ALU.add)
                    dve.drain()
                    nc.vector.reciprocal(cstat[:, 4:8], cstat[:, 4:8])
                    dve.drain()
                    nc.vector.tensor_tensor(cstat[:, 4:8], cstat[:, 4:8], g_f[:, :, 3 * head], ALU.mult)
                    dve.drain()
                    nc.vector.tensor_tensor(cstat[:, 4:5], cstat[:, 4:5], con(C_VALID), ALU.mult)
                    dve.drain()
                    nc.vector.tensor_tensor(cp_f, cp_f, cstat[:, 4:8].unsqueeze(2).broadcast_to([P, 4, 32]),
                                            ALU.mult).then_inc(cs_p, 1)
            stage_end(dve, "dve")
            pa, pb = wv(T, S), wv(T + 512, S)
            for g, w in enumerate(WINDOWS):
                src = u_f[:, g, :]
                cur, span, bufs = src, 1, [pa, pb]
                while span < w:
                    dst = bufs[0] if cur is not bufs[0] else bufs[1]
                    nc.vector.tensor_copy(dst[:, 0:span], cur[:, 0:span])
                    nc.vector.tensor_tensor(dst[:, span:S], cur[:, span:S], cur[:, 0:S - span], ALU.add)
                    dve.drain()
                    cur, span = dst, 2 * span
                nc.vector.tensor_tensor(cur[:, 0:16], cur[:, 0:16], con(C_CNT + 16 * g, 16), ALU.mult)
                dve.drain()
                nc.vector.scalar_tensor_tensor(out=src[:, 16:S], in0=cur[:, 16:S], scalar=1.0 / w, in1=src[:, 16:S],
                                               op0=ALU.mult, op1=ALU.subtract)
                nc.vector.tensor_tensor(src[:, 0:16], cur[:, 0:16], src[:, 0:16], ALU.subtract)
                dve.drain().then_inc(pool_in, 1)
            stage_end(dve, "dve")
            dve_next(dve, "mg", None)
            c0, n, t0, per = section("merge1")
            for k in range(4):
                for m in range(4):
                    j = 4 * (k // 2) + m
                    if k % 2 == 0:
                        gated_add(dve, t0, True, mg_f[:, j, :], br_f, 4 * k + m, m % 2, mg_f[:, j, :])
                    else:
                        gated_add(dve, t0, False, mg_f[:, 8 + j, :], br_f, 4 * k + m, m % 2, mg_f[:, j, :])
                dve_conv(dve, c0 + k + 2, (c0 + k) % 2)
            dve_next(dve, "wout", None, lambda n, t: dve_add_x(dve, prod_f, n, t))
            dve_norm(dve, 1, lambda k: col(V_FFN + k))
            for r in range(3):
                c0, n, t0, per = section(f"up{r}")
                for k in range(ROUNDS[r]):
                    dve_conv(dve, c0 + k + 2, (c0 + k) % 2)
                    ft = sum(ROUNDS[:r]) + k
                    y, gp = cv_f[:, k % 2, :], gp_f[:, k, :]
                    dve.wait_ge(evac, t0 + 2 * k + 1)
                    nc.vector.tensor_scalar(y, gp, col(V_CONVW + 2 * FF_TILES + ft), None, ALU.mult)
                    dve.drain()
                    nc.vector.scalar_tensor_tensor(out=y[:, 1:S], in0=gp[:, 0:S - 1], scalar=col(V_CONVW + FF_TILES + ft),
                                                   in1=y[:, 1:S], op0=ALU.mult, op1=ALU.add)
                    dve.drain()
                    nc.vector.scalar_tensor_tensor(out=y[:, 2:S], in0=gp[:, 0:S - 2], scalar=col(V_CONVW + ft),
                                                   in1=y[:, 2:S], op0=ALU.mult, op1=ALU.add)
                    dve.drain()
                    nc.vector.tensor_scalar(y, y, col(V_CONVB + ft), None, ALU.add).then_inc(ff_conv, 1)
                    dve.wait_ge(evac, t0 + 2 * k + 2)
                    dve.drain()
                    nc.vector.tensor_tensor(gp, y, vl_f[:, k, :], ALU.mult)
                    dve.drain()
                    dve.wait_ge(ff_sig, ft + 1)
                    nc.vector.tensor_tensor(gp, gp, sg_f[:, k % 2, :], ALU.mult).then_inc(ff_prod, 1)
                dve_next(dve, f"down{r}", None, lambda n, t: dve_add_x(dve, dn_f, n, t))
            for l in range(LAYERS):
                dve_layer(dve, l)

        @block.gpsimd
        def _(pool):
            pool.wait_ge(const_in, 80)
            pool_norm(pool, 0)
            stage_end(pool, "pool")
            for b in range(2):
                split_pool(pool, vr[b], v_f[:, :, b * P:b * P + P])
            for b in range(2):
                pool.wait_ge(hn_fin, b + 1)
                split_pool(pool, kr[b], ksw_f[:, b, :])
            pool.wait_ge(hn_fin, 3)
            split_pool(pool, qr[0], q_f[:, 0, :]).then_inc(ring_in, 1)
            pool.wait_ge(hn_fin, 7)
            split_pool(pool, kcr, kc_f)
            stage_end(pool, "pool")

            def q_parts(t):
                if t >= 2:
                    pool.wait_ge(ex_done, 16 * (t - 1))
                split_pool(pool, qr[t % 2], q_f[:, t, :]).then_inc(ring_in, 1)
            for t in range(1, 4):
                q_parts(t)
            stage_end(pool, "pool")
            stage_end(pool, "pool")
            for x in range(4):
                pool.wait_ge(part_hi, x + 1)
                nc.gpsimd.tensor_tensor(yr[1][:, x, :], u_f[:, x, :], yr[0][:, x, :].bitcast(F32),
                                        ALU.subtract).then_inc(y_lo, 1)
                nc.gpsimd.tensor_tensor(yr2[1][:, x, :], q_f[:, x, :], yr2[0][:, x, :].bitcast(F32),
                                        ALU.subtract).then_inc(y_lo, 1)
            for x in range(KT):
                pool.wait_ge(part_hi, 4 + x + 1)
                nc.gpsimd.tensor_tensor(mr[1][:, x, :], mg_f[:, x, :], mr[0][:, x, :].bitcast(F32),
                                        ALU.subtract).then_inc(m_lo, 1)
            pool_norm(pool, 1)
            for r in range(3):
                for k in range(ROUNDS[r]):
                    n = sum(ROUNDS[:r]) + k
                    pool.wait_ge(ff_hi, n + 1)
                    nc.gpsimd.tensor_tensor(mr[1][:, k, :], gp_f[:, k, :], mr[0][:, k, :].bitcast(F32),
                                            ALU.subtract).then_inc(ff_lo, 1)
            for l in range(LAYERS):
                pool_layer(pool, l)

        assert len(set(stage_no.values())) == 1, stage_no

        @block.sync
        def _(sp):
            sp.dma_start(xT[:, :, :], x_in).then_inc(const_in, 16)
            sp.dma_start(cst[:, :], cst_in).then_inc(const_in, 16)
            sp.dma_start(vec[:, :], vec_in).then_inc(const_in, 16)
            sp.dma_start(wv(T + 2048, NMSK), msk_in).then_inc(const_in, 16)
            sp.dma_start(cos_t.bitcast(I32), pos_in).then_inc(const_in, 16)
            for k in range(2):
                sp.dma_start(wraw[:, k, :], w_in[k]).then_inc(raw_in[k], 16)
            with sp.Fori(1, CHUNKS // 2) as j:
                for k in range(2):
                    sp.wait_ge(w_lo, 2 * j + k - 1)
                    sp.dma_start(wraw[:, k, :], w_in[bass.ds(2 * j + k, 1)].rearrange("a p n -> p (a n)")
                                 ).then_inc(raw_in[k], 16)
            sp.wait_ge(stage["dve"], stage_no["dve"])
            sp.dma_start(out, xT[:, :, :]).then_inc(out_done, 16)
            sp.wait_ge(out_done, 16)


_OUTS = [((P, KT, S), "float32")]


def _tiles(m):
    return m.reshape(-1, P, m.shape[1]).transpose(1, 0, 2)


def _stream(a):
    chunks = []

    def put(m):
        t = _tiles(m)
        c = np.zeros((P, CHUNK), np.float32)
        c[:, :t.shape[1] * t.shape[2]] = t.reshape(P, -1)
        chunks.append(c)

    def columns(m, width=256):
        for c in range(0, m.shape[1], width):
            put(m[:, c:c + width])

    w = a["w_in"][0]
    columns(w[:, 0:512])
    q = w[:, 512:1024].reshape(D, 2, 4, 64).transpose(0, 2, 1, 3).reshape(D, 512)
    columns(q)
    kv = w[:, 1024:1792].reshape(D, 6, P)
    put(kv[:, 0:2].reshape(D, 256))
    put(kv[:, [2, 4]].reshape(D, 256))
    put(kv[:, [3, 5]].reshape(D, 256))
    put(np.pad(w[:, 1792:1816], ((0, 0), (0, 232))))
    columns(w[:, 1816:3864])
    nsa_out = a["w_nsa_out"][0].reshape(2, 4, 64, D).transpose(1, 0, 2, 3).reshape(512, D)
    for half in range(2):
        for m in (a["w_pool_out"][0], nsa_out):
            put(m[:, 512 * half:512 * half + 512])
    columns(a["w_out"][0])
    up, down = a["w_up"][0], a["w_down"][0]
    first = 0
    for n in ROUNDS:
        for f in range(first, first + n):
            put(np.concatenate([up[:, f * P:f * P + P], up[:, D_FF + f * P:D_FF + f * P + P]], axis=1))
        columns(down[first * P:(first + n) * P])
        first += n
    for l in range(LAYERS):
        w, br = a["w_in_2"][l], a["w_br_2"][l]
        gate = w[:, 6232:]
        columns(w[:, 1552:2064])
        columns(w[:, 2064:2576])
        columns(w[:, 3088:3600])
        put(np.pad(w[:, 3600:3672], ((0, 0), (0, 184))))
        columns(w[:, 2576:3088])
        columns(gate[:, 1024:2048])
        columns(w[:, 3672:4184])
        columns(br[1], 512)
        columns(w[:, 4184:4696])
        columns(w[:, 4696:5208])
        columns(w[:, 5208:5720])
        columns(w[:, 5720:6232])
        columns(gate[:, 2048:3072])
        columns(br[2], 512)
        put(np.pad(w[:, 1024:1040], ((0, 0), (0, 240))))
        columns(w[:, 256:512])
        columns(w[:, 512:1024])
        columns(w[:, 0:256])
        columns(w[:, 1040:1552])
        columns(gate[:, 0:1024])
        columns(br[0], 512)
        columns(a["w_out_2"][l])
    assert len(chunks) == CHUNKS
    return np.stack(chunks)


def _vectors(a):
    v = np.zeros((P, NVEC), np.float32)

    def cols(at, x):
        x = x.reshape(-1, P)
        v[:, at:at + len(x)] = x.T

    def twice(at, x):
        v[:, at] = np.concatenate([x, x])

    cols(V_MIX, a["mix_norm_g"]), cols(V_FFN, a["ffn_norm_g"]), cols(V_N2, a["norm_g_2"])
    cols(V_CONVB, a["conv_b"]), cols(V_CONVW, a["conv_w"]), cols(V_PSCALE, a["pool_scale"])
    twice(V_QG, a["q_norm_g"][0])
    for i in range(3):
        twice(V_KG + i, a["k_norm_g"][0, i])
    for kv in range(2):
        for t in range(32):
            twice(V_PE + 32 * kv + t, a["cmp_pe"][0, kv, t])
    cols(V_GLA, a["gla_norm_g_2"]), cols(V_DQ, a["dsa_qn_g_2"]), cols(V_DK, a["dsa_kn_g_2"])
    for l in range(LAYERS):
        twice(V_CQ + l, a["diff_qn_g_2"][l])
        twice(V_CK + l, a["diff_kn_g_2"][l])
        for i, name in enumerate(("diff_lq1_2", "diff_lk1_2", "diff_lq2_2", "diff_lk2_2")):
            v[0:64, V_LAM + 4 * l + i] = a[name][l]
    return v


def _constants():
    c = np.zeros((P, NCST), np.float32)
    p = np.arange(P)
    c[:, C_ID:C_ID + P] = np.eye(P)
    c[:, C_ONE:C_ONE + P] = 1
    d = p % 64
    partner = np.where(d < ROT // 2, p + ROT // 2, np.where(d < ROT, p - ROT // 2, -1))
    c[:, C_PERM:C_PERM + P] = p[:, None] == partner[None, :]
    c[:, C_SUF:C_SUF + P] = (p[:, None] > p[None, :]) & (p[:, None] // CH == p[None, :] // CH)
    c[:, C_IND:C_IND + 2] = p[:, None] // CH == np.arange(2)
    for g, w in enumerate(WINDOWS):
        c[:, C_CNT + 16 * g:C_CNT + 16 * g + 16] = np.float32(1) / np.minimum(np.arange(16) + 1, w).astype(np.float32)
    inv = THETA ** (-np.arange(ROT // 2) * 2.0 / ROT)
    c[:, C_INVF] = np.where(d < ROT, inv[d % (ROT // 2)], 0)
    c[:, C_SGN] = np.where(d < ROT // 2, -1, np.where(d < ROT, 1, 0))
    c[:, C_VALID] = p >= 2 * CMP_STRIDE - 1
    c[:, C_EPS] = EPS
    c[:, C_ONES1] = 1
    c[0:64, C_E64 + 14] = c[64:128, C_E64 + 15] = c[:, C_E128 + 7] = 1
    c[0:8, C_S128:C_S128 + 8] = np.eye(8) * P ** -0.5
    for l in range(LAYERS):
        init = 0.8 - 0.6 * np.exp(-0.3 * l)
        c[:, C_LINIT + l], c[:, C_1ML + l] = init, 1.0 - init
    m = np.zeros((P, NMSK), np.float32)
    m[:, M_ID:M_ID + P] = np.eye(P)
    m[:, M_TRI:M_TRI + P] = np.where(p[None, :] <= p[:, None], 0, NEG)
    m[:, M_CH:M_CH + P] = np.where(p[None, :] // CH <= p[:, None] // CH, 0, NEG)
    for i in range(QT):
        end = np.arange(32) * CMP_STRIDE + 2 * CMP_STRIDE - 1
        seen = (end[None, :] <= p[:, None] + P * i) & (np.arange(32) < N_CMP)[None, :]
        m[:, M_CMP + 32 * i:M_CMP + 32 * i + 32] = np.where(seen, 0, NEG)
    heads = np.repeat(np.eye(16), 64, axis=1).astype(np.float32)
    is_key = np.zeros((2, 8, P), np.float32)
    is_key[0, [0, 1, 6]] = is_key[1, 4:8] = 1
    spread = heads * np.where(is_key == 1, 0.125, 1).reshape(2, 1, 8 * P)
    return c, m, spread.astype(np.float32)


def kernel(**inputs):
    import concourse.bacc as bacc
    from concourse.bass_utils import run_bass_kernel_spmd

    a = {k: np.asarray(v) for k, v in inputs.items()}
    cst, msk, spread = _constants()
    w1 = a["cmp_w1"][0].reshape(2, 16, 2, 64, P).transpose(2, 3, 0, 1, 4)
    w2 = a["cmp_w2"][0].transpose(1, 0, 2)
    wa2 = np.zeros((P, LAYERS, 256), np.float32)
    wa2[0:16] = a["gla_wa2_2"].transpose(1, 0, 2)
    wa2[16] = a["gla_ba_2"]
    arrays = {
        "x_t": np.ascontiguousarray(a["x"][0].T.reshape(KT, P, S).transpose(1, 0, 2)),
        "positions": np.ascontiguousarray(np.broadcast_to(a["positions"][0].astype(np.int32), (P, S))),
        "weights": _stream(a),
        "vectors": _vectors(a),
        "constants": cst,
        "masks": msk,
        "cmp_w1": np.ascontiguousarray(w1.reshape(P, 32, P)),
        "small": np.ascontiguousarray(np.concatenate([
            a["pool_w"][0].transpose(1, 0, 2).reshape(P, 4 * P), np.concatenate([w2, w2], axis=2).reshape(P, 2 * P),
            wa2.reshape(P, LAYERS * 256)], axis=1)),
        "spread": spread,
    }
    nc = bacc.Bacc("TRN2", target_bir_lowering=False, num_devices=1)
    args = [nc.dram_tensor(name, v.shape, mybir.dt.from_np(v.dtype), kind="ExternalInput").ap()
            for name, v in arrays.items()]
    args.append(nc.dram_tensor("out_t", (P, KT, S), F32, kind="ExternalOutput").ap())
    two_block_kernel(nc, *args)
    r = run_bass_kernel_spmd(nc, [arrays], core_ids=[0])
    y = r.results[0]["out_t"]
    return np.ascontiguousarray(y.transpose(1, 0, 2).reshape(D, S).T)[None]
```
